# Optimizing a Trainium2 kernel written in Bass

```python
import math
import jax, jax.numpy as jnp
from jax import lax
import numpy as np

D_MODEL = 1024
BATCH = 1
SEQ = 128
DEPTH = 2
DEC_BATCH = 1
DEC_SEQ = 128
PAST_LEN = 128

GRID_W = 64
CONV_W = 512
CONV_K = 31
CONV_PAD = (CONV_K - 1) // 2
SSM_W = 512
SSM_GC = 16
SSM_G = SSM_W // SSM_GC
SSM_P = 64
N_DIR = 2
N_HEADS = 8
N_KV_HEADS = 2
HEAD_DIM = 64
GQ = N_HEADS // N_KV_HEADS
ATTN_W = N_HEADS * HEAD_DIM
KV_W = N_KV_HEADS * HEAD_DIM
ROPE_PAIRS = HEAD_DIM // 4
ROPE_BASE = 10000.0
Q_BLOCK = 128
N_BRANCH = 3
EPS = 1e-6
IN_SIZES = (2 * CONV_W, CONV_W, SSM_W, SSM_W, ATTN_W, KV_W, KV_W, ATTN_W, N_BRANCH * D_MODEL)
IN_COLS = sum(IN_SIZES)

kernel_name = 'hybrid_conv_s5_gqa_prefix_dit_step'

F32 = jnp.float32

def _rmsnorm(x, g):
    xf = x.astype(F32)
    y = xf * lax.rsqrt(jnp.mean(xf * xf, axis=-1, keepdims=True) + EPS)
    return (y * g.astype(F32)).astype(x.dtype)

def _layernorm(x, g, b):
    xf = x.astype(F32)
    mu = jnp.mean(xf, axis=-1, keepdims=True)
    xc = xf - mu
    y = xc * lax.rsqrt(jnp.mean(xc * xc, axis=-1, keepdims=True) + EPS)
    return (y * g.astype(F32) + b.astype(F32)).astype(x.dtype)

def _adaln(cond, w, b):
    m = jax.nn.silu(cond) @ w + b
    return jnp.split(m[:, None, :], 3, axis=-1)

def _grid_angles(n_tok):
    rows = n_tok // GRID_W
    row = jnp.repeat(jnp.arange(rows, dtype=F32), GRID_W)
    col = jnp.tile(jnp.arange(GRID_W, dtype=F32), rows)
    inv = ROPE_BASE ** (-jnp.arange(ROPE_PAIRS, dtype=F32) / ROPE_PAIRS)
    return row[:, None] * inv[None, :], col[:, None] * inv[None, :]

def _rotate(xp, ang):
    x1, x2 = xp[..., :ROPE_PAIRS], xp[..., ROPE_PAIRS:]
    cos = jnp.cos(ang)[None, :, None, :]
    sin = jnp.sin(ang)[None, :, None, :]
    return jnp.concatenate([x1 * cos - x2 * sin, x1 * sin + x2 * cos], axis=-1)

def _axial_rope(x, angles):
    ang_row, ang_col = angles
    xf = x.astype(F32)
    half = HEAD_DIM // 2
    out = jnp.concatenate([_rotate(xf[..., :half], ang_row), _rotate(xf[..., half:], ang_col)], axis=-1)
    return out.astype(x.dtype)

def _blocked_attention(q, k, v):
    bsz, lq = q.shape[:2]
    nb = lq // Q_BLOCK
    qb = q.reshape(bsz, nb, Q_BLOCK, N_KV_HEADS, GQ, HEAD_DIM).transpose(1, 0, 2, 3, 4, 5)
    scale = HEAD_DIM ** -0.5

    def one_block(qblk):
        s = jnp.einsum('bqkgd,bskd->bkgqs', qblk, k).astype(F32) * scale
        p = jax.nn.softmax(s, axis=-1).astype(v.dtype)
        return jnp.einsum('bkgqs,bskd->bqkgd', p, v)

    o = lax.map(one_block, qb)
    return o.transpose(1, 0, 2, 3, 4, 5).reshape(bsz, lq, ATTN_W)

def _conformer_conv(u, dw_w, dw_b, ln_g, ln_b):
    a, g = jnp.split(u, 2, axis=-1)
    y = a * jax.nn.sigmoid(g)
    y = lax.conv_general_dilated(
        y, dw_w[:, None, :].astype(y.dtype), window_strides=(1,), padding=[(CONV_PAD, CONV_PAD)],
        dimension_numbers=('NWC', 'WIO', 'NWC'), feature_group_count=CONV_W) + dw_b.astype(y.dtype)
    return jax.nn.silu(_layernorm(y, ln_g, ln_b))

def _ssm_combine(e1, e2):
    a1, b1 = e1
    a2, b2 = e2
    return a1 * a2, a2 * b1 + b2

def _s5_bidirectional(u, a_re, a_im, log_dt, b_re, b_im, c_re, c_im, d, init_re, init_im):
    bsz, n = u.shape[:2]
    uf = u.astype(F32).reshape(bsz, n, SSM_G, SSM_GC)
    uc = uf.astype(jnp.complex64)
    y = d.astype(F32).reshape(SSM_G, SSM_GC) * uf
    want_final = init_re is None
    fin_re, fin_im = [], []
    for dirn in range(N_DIR):
        rev = dirn == 1
        lam = lax.complex(a_re[dirn].astype(F32), a_im[dirn].astype(F32))
        dt = jnp.exp(log_dt[dirn].astype(F32))[:, None]
        lam_bar = jnp.exp(lam * dt)
        b_bar = ((lam_bar - 1.0) / lam)[..., None] * lax.complex(b_re[dirn].astype(F32), b_im[dirn].astype(F32))
        bu = jnp.einsum('blgc,gpc->blgp', uc, b_bar)
        if not want_final:
            h0 = lax.complex(init_re[:, dirn].astype(F32), init_im[:, dirn].astype(F32))
            edge = n - 1 if rev else 0
            bu = bu.at[:, edge].add(lam_bar * h0)
        a = jnp.broadcast_to(lam_bar, bu.shape)
        _, hs = lax.associative_scan(_ssm_combine, (a, bu), axis=1, reverse=rev)
        if want_final:
            fin = hs[:, 0] if rev else hs[:, -1]
            fin_re.append(fin.real)
            fin_im.append(fin.imag)
        c_mat = lax.complex(c_re[dirn].astype(F32), c_im[dirn].astype(F32))
        y = y + jnp.einsum('blgp,gcp->blgc', hs, c_mat).real
    y = y.reshape(bsz, n, SSM_W).astype(u.dtype)
    if want_final:
        return y, jnp.stack(fin_re, axis=1), jnp.stack(fin_im, axis=1)
    return y, None, None

def _layer(x, mods, lp, angles, ctx_k, ctx_v, init_re, init_im):
    shift, scale, gate = mods
    bsz, n = x.shape[:2]
    h = _rmsnorm(x, lp['norm_g']) * (1.0 + scale) + shift
    z = h @ lp['w_in']
    cuts = np.cumsum(IN_SIZES)[:-1].tolist()
    conv_in, conv_gate, ssm_in, ssm_gate, q, k, v, attn_gate, merge = jnp.split(z, cuts, axis=-1)
    ya = _conformer_conv(conv_in, lp['conv_dw_w'], lp['conv_dw_b'], lp['conv_ln_g'], lp['conv_ln_b'])
    br_a = (ya * jax.nn.silu(conv_gate)) @ lp['w_conv_out']
    yb, fin_re, fin_im = _s5_bidirectional(
        ssm_in, lp['ssm_a_re'], lp['ssm_a_im'], lp['ssm_log_dt'], lp['ssm_b_re'], lp['ssm_b_im'],
        lp['ssm_c_re'], lp['ssm_c_im'], lp['ssm_d'], init_re, init_im)
    yg_a, yg_b = jnp.split(jax.nn.gelu(yb) @ lp['w_ssm_glu'], 2, axis=-1)
    yb = yg_a * jax.nn.sigmoid(yg_b)
    br_b = (yb * jax.nn.silu(ssm_gate)) @ lp['w_ssm_out']
    q = _rmsnorm(q.reshape(bsz, n, N_HEADS, HEAD_DIM), lp['q_norm_g'])
    k = _rmsnorm(k.reshape(bsz, n, N_KV_HEADS, HEAD_DIM), lp['k_norm_g'])
    v = v.reshape(bsz, n, N_KV_HEADS, HEAD_DIM)
    if ctx_k is None:
        k_all, v_all = k, v
    else:
        q = _axial_rope(q, angles)
        k_all = jnp.concatenate([_axial_rope(k, angles), ctx_k.astype(k.dtype)], axis=1)
        v_all = jnp.concatenate([v, ctx_v.astype(v.dtype)], axis=1)
    o = _blocked_attention(q, k_all, v_all)
    br_c = (o * jax.nn.silu(attn_gate)) @ lp['w_attn_out']
    g_a, g_b, g_c = jnp.split(jax.nn.sigmoid(merge), N_BRANCH, axis=-1)
    mixed = g_a * br_a + g_b * br_b + g_c * br_c
    x = x + gate * (mixed @ lp['w_out'])
    side = (k, v, fin_re, fin_im) if ctx_k is None else None
    return x, side

def setup_inputs(seed: int = 0) -> dict:
    key = jax.random.key(seed)
    ks = iter(jax.random.split(key, 48))

    def nrm(shape, scale):
        return jax.random.normal(next(ks), shape, F32) * scale

    n_idx = jnp.arange(SSM_P, dtype=F32)
    return {
        'x_prompt': nrm((BATCH, SEQ, D_MODEL), 1.0),
        'x_sample': nrm((DEC_BATCH, DEC_SEQ, D_MODEL), 1.0),
        'cache_k': nrm((DEC_BATCH, DEPTH, PAST_LEN, N_KV_HEADS, HEAD_DIM), 1.0),
        'cache_v': nrm((DEC_BATCH, DEPTH, PAST_LEN, N_KV_HEADS, HEAD_DIM), 1.0),
        'state_ssm_re': nrm((DEC_BATCH, DEPTH, N_DIR, SSM_G, SSM_P), 0.5),
        'state_ssm_im': nrm((DEC_BATCH, DEPTH, N_DIR, SSM_G, SSM_P), 0.5),
        'c': nrm((DEC_BATCH, D_MODEL), 1.0),
        'c_ctx': nrm((D_MODEL,), 1.0),
        'norm_g': 1.0 + nrm((DEPTH, D_MODEL), 0.02),
        'w_ada': nrm((DEPTH, D_MODEL, 3 * D_MODEL), 0.5 * D_MODEL ** -0.5),
        'b_ada': nrm((DEPTH, 3 * D_MODEL), 0.01),
        'w_in': nrm((DEPTH, D_MODEL, IN_COLS), D_MODEL ** -0.5),
        'conv_dw_w': nrm((DEPTH, CONV_K, CONV_W), CONV_K ** -0.5),
        'conv_dw_b': nrm((DEPTH, CONV_W), 0.01),
        'conv_ln_g': 1.0 + nrm((DEPTH, CONV_W), 0.02),
        'conv_ln_b': nrm((DEPTH, CONV_W), 0.01),
        'w_conv_out': nrm((DEPTH, CONV_W, D_MODEL), CONV_W ** -0.5),
        'ssm_a_re': -0.5 + nrm((DEPTH, N_DIR, SSM_G, SSM_P), 0.01),
        'ssm_a_im': math.pi * n_idx + nrm((DEPTH, N_DIR, SSM_G, SSM_P), 0.01),
        'ssm_log_dt': jax.random.uniform(next(ks), (DEPTH, N_DIR, SSM_G), F32, math.log(1e-3), math.log(1e-1)),
        'ssm_b_re': nrm((DEPTH, N_DIR, SSM_G, SSM_P, SSM_GC), (2 * SSM_GC) ** -0.5),
        'ssm_b_im': nrm((DEPTH, N_DIR, SSM_G, SSM_P, SSM_GC), (2 * SSM_GC) ** -0.5),
        'ssm_c_re': nrm((DEPTH, N_DIR, SSM_G, SSM_GC, SSM_P), (2 * SSM_P) ** -0.5),
        'ssm_c_im': nrm((DEPTH, N_DIR, SSM_G, SSM_GC, SSM_P), (2 * SSM_P) ** -0.5),
        'ssm_d': nrm((DEPTH, SSM_W), 1.0),
        'w_ssm_glu': nrm((DEPTH, SSM_W, 2 * SSM_W), SSM_W ** -0.5),
        'w_ssm_out': nrm((DEPTH, SSM_W, D_MODEL), SSM_W ** -0.5),
        'q_norm_g': 1.0 + nrm((DEPTH, HEAD_DIM), 0.02),
        'k_norm_g': 1.0 + nrm((DEPTH, HEAD_DIM), 0.02),
        'w_attn_out': nrm((DEPTH, ATTN_W, D_MODEL), ATTN_W ** -0.5),
        'w_out': nrm((DEPTH, D_MODEL, D_MODEL), D_MODEL ** -0.5),
    }

def reference(x_prompt, x_sample, cache_k, cache_v, state_ssm_re, state_ssm_im, c, c_ctx,
              norm_g, w_ada, b_ada, w_in, conv_dw_w, conv_dw_b, conv_ln_g, conv_ln_b, w_conv_out,
              ssm_a_re, ssm_a_im, ssm_log_dt, ssm_b_re, ssm_b_im, ssm_c_re, ssm_c_im, ssm_d,
              w_ssm_glu, w_ssm_out, q_norm_g, k_norm_g, w_attn_out, w_out):
    angles = _grid_angles(x_sample.shape[1])
    yp = x_prompt
    ys = x_sample
    ks_out, vs_out, re_out, im_out = [], [], [], []
    for l in range(DEPTH):
        lp = dict(norm_g=norm_g[l], w_in=w_in[l], conv_dw_w=conv_dw_w[l], conv_dw_b=conv_dw_b[l],
                  conv_ln_g=conv_ln_g[l], conv_ln_b=conv_ln_b[l], w_conv_out=w_conv_out[l],
                  ssm_a_re=ssm_a_re[l], ssm_a_im=ssm_a_im[l], ssm_log_dt=ssm_log_dt[l],
                  ssm_b_re=ssm_b_re[l], ssm_b_im=ssm_b_im[l], ssm_c_re=ssm_c_re[l], ssm_c_im=ssm_c_im[l],
                  ssm_d=ssm_d[l], w_ssm_glu=w_ssm_glu[l], w_ssm_out=w_ssm_out[l],
                  q_norm_g=q_norm_g[l], k_norm_g=k_norm_g[l], w_attn_out=w_attn_out[l], w_out=w_out[l])
        ctx_mods = _adaln(c_ctx[None, :], w_ada[l], b_ada[l])
        yp, side = _layer(yp, ctx_mods, lp, None, None, None, None, None)
        k_l, v_l, re_l, im_l = side
        ks_out.append(k_l)
        vs_out.append(v_l)
        re_out.append(re_l)
        im_out.append(im_l)
        lat_mods = _adaln(c, w_ada[l], b_ada[l])
        ys, _ = _layer(ys, lat_mods, lp, angles, cache_k[:, l], cache_v[:, l],
                       state_ssm_re[:, l], state_ssm_im[:, l])
    new_cache_k = jnp.stack(ks_out, axis=1)
    new_cache_v = jnp.stack(vs_out, axis=1)
    new_state_ssm_re = jnp.stack(re_out, axis=1)
    new_state_ssm_im = jnp.stack(im_out, axis=1)
    return (yp, ys, new_cache_k, new_cache_v, new_state_ssm_re, new_state_ssm_im)


_drawn_inputs = setup_inputs


def setup_inputs(seed=0):
    import zlib

    import numpy as np

    out = dict(_drawn_inputs(seed))
    spreads = {}
    factors = {'cache_k': 6.593,
     'cache_v': 5.198,
     'state_ssm_re': 2.837,
     'state_ssm_im': 2.803,
     'norm_g': 2.917,
     'b_ada': 3.152,
     'conv_dw_b': 8.0,
     'conv_ln_g': 8.0,
     'conv_ln_b': 8.0,
     'ssm_a_re': 4.457,
     'ssm_c_re': 2.773,
     'ssm_c_im': 2.84,
     'q_norm_g': 8.0,
     'k_norm_g': 2.826}
    for name, (base, spread) in spreads.items():
        noise = np.random.default_rng([zlib.crc32(name.encode()), seed]).standard_normal(out[name].shape)
        drawn = base * np.exp(spread * noise) if base else spread * noise
        out[name] = __import__('jax').numpy.asarray(drawn.astype(out[name].dtype))
    for name, factor in factors.items():
        out[name] = (out[name] * factor).astype(out[name].dtype)
    return out
```

```python
from contextlib import ExitStack

import concourse.bass as bass
from concourse import mybir

F32 = mybir.dt.float32
ALU = mybir.AluOpType
ACT = mybir.ActivationFunctionType
AX_X = mybir.AxisListType.X

P = 128
NS = 2
D = 1024
DT = D // P
DEPTH = 2
W = 512
WT = W // P
HEADS, KV, HD = 8, 2, 64
QK = (HEADS + KV) * HD
TAPS = 31
PAD = TAPS // 2
GC, G, SP = 16, 32, 64
L = 4
NCHUNK = P // L
GP = G // 2
ROW = G * 2 * NS
EPS = 1e-6
NEXP = 11
TWO_PI = 6.283185307179586
PI_PARTS = (6.28125, 0.0019350051879882812, 3.0199159819e-07)
MAGIC = 12582912.0
GELU_C = 0.7978845608028654
GELU_A = 0.044715

KT_SLAB = 2
RAW = 4

IN_UNITS = {"ssm": (1536, 512), "ca": (0, 512), "cg": (512, 512), "q": (2560, 512), "kv": (3072, 256),
            "sg": (2048, 512), "gg": (1024, 512), "ag": (3328, 512)}
MERGE0 = 3840
BRANCHES = ("C", "B", "A")
MERGE_OF = {"A": 0, "B": 1, "C": 2}


def order(l):
    st = [("xn", 0), ("xn", 1), ("hT", 0), ("hT", 1), ("unit", "ssm"), ("unit", "ca"), ("unit", "cg"), ("UT",),
          ("unit", "q"), ("S",), ("unit", "kv"), ("convT", 0), ("convT", 1), ("qkn", 0), ("qkn", 1), ("cp",),
          ("scan",), ("unit", "sg"), ("qkT", 0), ("qkT", 1), ("conv", 0), ("unit", "gg"), ("unit", "ag"),
          ("att", 0), ("K",), ("conv", 1), ("att", 1), ("Y",), ("conv", 2), ("conv", 3)]
    if l + 1 < DEPTH:
        st += [("ada", l + 1), ("small", l + 1), ("tab", l + 1)]
    st += [("gelu", 0), ("gelu", 1), ("cback", 0), ("cback", 1)]
    if l + 1 < DEPTH:
        st += [("preP", l + 1, 0)]
    st += [("geT", 0), ("geT", 1), ("unit", "glub"), ("unit", "glua"), ("brT", "C", 0), ("brT", "C", 1),
           ("comb", "C", 0), ("comb", "C", 1)]
    if l + 1 < DEPTH:
        st += [("preE", l + 1, 0), ("preP", l + 1, 1)]
    st += [("brT", "B", 0), ("brT", "B", 1), ("comb", "B", 0), ("comb", "B", 1),
           ("brT", "A", 0), ("brT", "A", 1), ("comb", "A", 0), ("comb", "A", 1)]
    if l + 1 < DEPTH:
        st += [("preE", l + 1, 1)]
    st += [("mixT", 0), ("mixT", 1), ("wout", 0), ("wout", 1)]
    return st


def stages():
    out = [(0, s) for s in (("small", 0), ("ada", 0), ("tab", 0), ("preP", 0, 0), ("preE", 0, 0),
                            ("preP", 0, 1), ("preE", 0, 1))]
    for l in range(DEPTH):
        out += [(l, s) for s in order(l)]
    return out


def units_of(stage):
    if stage[0] == "unit":
        u = stage[1]
        if u in ("glua", "glub"):
            return [(u, WT, W)]
        return [(u, DT, IN_UNITS[u][1])]
    if stage[0] == "comb":
        return [("br" + stage[1] + str(stage[2]), WT, W), ("me" + stage[1] + str(stage[2]), DT, W)]
    if stage[0] == "wout":
        return [("wo" + str(stage[1]), DT, W)]
    return []


def side_uses(l, stage):
    k = stage[0]
    if k == "small":
        return [(("small", stage[1], i), 1) for i in ((0, 1, 2, 3, 4) if stage[1] == 0 else (0, 1, 3, 4))]
    if k == "preE":
        return [(("E", stage[1], 4 * stage[2] + i), 1) for i in range(4)]
    if k == "hT":
        return [(("hT", l, stage[1], h), 1) for h in range(2)]
    if k == "UT":
        return [(("UT", l, h), 2) for h in range(2)]
    if k == "convT":
        return [(("convT", l, stage[1]), 1)]
    if k == "S":
        return [(("S", l, i), 2) for i in range(8)]
    if k == "qkT":
        return [(("qT", l, stage[1]), 1), (("kT", l, stage[1]), 2)]
    if k == "K":
        return [(("K", l, i), 1) for i in range(8)]
    if k == "att":
        s = stage[1]
        out = []
        for p in range(4 + 1):
            if p < 4:
                out.append((("sc", l, s, p), 1))
            if p >= 1:
                out.append((("pT", l, s, p - 1), 1))
        return out
    if k == "Y":
        return [(("Y", l, q), 1) for q in range(4)] + [(("fin", l), 1)]
    if k == "cback":
        return [(("cback", l, stage[1]), 1)]
    if k == "geT":
        return [(("geT", l, stage[1]), 1)]
    if k == "brT":
        return [(("brT", l, stage[1], stage[2]), 1)]
    if k == "mixT":
        return [(("mixT", l, stage[1], h), 1) for h in range(2)]
    if k == "wout":
        return [(("gate", l, stage[1], s), 1) for s in range(NS)]
    return []


class Ring:

    def __init__(self, name, banks, uses, sem):
        self.banks, self.full, self.free = banks, sem(name + "_full"), [sem(f"{name}_free{b}") for b in range(len(banks))]
        self.at, total = {}, [0] * len(banks)
        for n, (key, drains) in enumerate(uses):
            b = n % len(banks)
            self.at[key] = (n, b, total[b], total[b] + drains)
            total[b] += drains

    def bank(self, key):
        return self.banks[self.at[key][1]]

    def claim(self, pe, key):
        n, b, before, _ = self.at[key]
        if before:
            pe.wait_ge(self.free[b], before)

    def filled(self, eng, key):
        eng.wait_ge(self.full, self.at[key][0] + 1)

    def freed(self, key):
        return self.free[self.at[key][1]]

    def drained(self, eng, key):
        eng.wait_ge(self.free[self.at[key][1]], self.at[key][3])


def build(nc, A, C, O):
    with ExitStack() as ctx:
        def sb(name, shape):
            return ctx.enter_context(nc.sbuf_tensor(name, shape, F32))

        sems = {}

        def sem(name):
            if name not in sems:
                sems[name] = ctx.enter_context(nc.semaphore(name))
            return sems[name]

        todo = stages()

        ident = sb("ident", [P, P])
        expo = sb("expo", [P, NEXP])
        rope = sb("rope", [P, 2, HD])
        x = sb("x", [P, NS, D])
        H = sb("H", [P, NCHUNK + 1, ROW])
        xn = H[:, :, :].rearrange("p a b -> p (a b)")[:, 0:NS * D].rearrange("p (s d) -> p s d", s=NS)
        mixed = sb("mixed", [P, NS, D])
        y2 = mixed[:, :, 0:W]
        ytok = mixed[:, :, W:D]
        hT = sb("hT", [P, NS, DT, P])
        raw = sb("raw", [P, RAW, KT_SLAB * W])
        EC = sb("EC", [P, 2 * (L + 1) * W])
        E = EC[:, 0:2 * GP * P].rearrange("p (r g q) -> p r g q", r=2, g=GP)
        CP = EC[:, :].rearrange("p (r i g c) -> p r i g c", r=2, i=L + 1, g=G)
        M = sb("M", [P, L, GP, GC])
        pre = sb("pre", [P, 2, 16, L, GC])
        craw = pre[:, 0, :, :, :].rearrange("p g j c -> p (g j c)").rearrange("p (r t q) -> p r t q", r=2, t=4)
        tA = sb("tA", [P, 1024])
        tB = sb("tB", [P, 1024])
        braw = tA[:, :].rearrange("p (r g c) -> p r g c", r=2, g=G)
        bz = sb("bz", [P, 2, 16, 3 * GC])
        bbar = sb("bbar", [P, 2, G, GC])
        cT = sb("cT", [P, 2, G, GC])
        lamr = sb("lamr", [P, NEXP, G])
        lami = sb("lami", [P, NEXP, G])
        tt = [pre[:, 1, :, :, :].rearrange("p g j c -> p (g j c)")[:, 352 * i:352 * i + 352] for i in range(2)]
        bzf = bz[:, :, :, :].rearrange("p r g c -> p (r g c)")
        tt += [bzf[:, 352 * i:352 * i + 352] for i in range(4)]
        lamR = sb("lamR", [P, ROW])
        lamI = sb("lamI", [P, ROW])
        a32 = sb("a32", [P, 5, P])
        st32 = a32[:, 0:2, :]
        t5 = sb("t5", [P, 5, G])
        ss = sb("ss", [P, 16, G])
        wide = sb("wide", [P, (L + 1) * W])
        KTs = wide[0:3 * GC, :].rearrange("p (i a b) -> p i a b", i=L + 1, a=2)
        U64 = wide[0:NS * NCHUNK, 0:L * W].rearrange("p (j c) -> p j c", j=L)
        Uz = sb("Uz", [P, G, NS * NCHUNK])
        HY = sb("HY", [P, 2, 8, 2, NS, NCHUNK])
        HYf = HY[:, :, :, :, :, :].rearrange("p a g r s k -> p a (g r s k)")
        Ug = HY[0:NS * NCHUNK].rearrange("p a g r s k -> p (a g r s k)")
        geT = HYf[:, 0, :].rearrange("p (s t q) -> p s t q", s=NS, t=WT)
        utok = sb("utok", [P, NS, W])
        cvpad = sb("cvpad", [P, WT, NS, P + 2 * PAD])
        cvacc = sb("cvacc", [P, WT, NS, P])
        taps = sb("taps", [P, WT, TAPS + 1])
        taprow = sb("taprow", [P, W])
        rows = sb("rows", [P, 3, W])
        modrow = rows[:, 0, 0:P]
        condrow = rows[:, 0, P:2 * P]
        cond = sb("cond", [P, NS, DT])
        condt = sb("condt", [P, NS, DT])
        condx = sb("condx", [P, NS, DT])
        h0 = sb("h0", [P, ROW])
        modc = sb("modc", [P, DEPTH, 4 * DT])
        ada = sb("ada", [P, DEPTH, 3 * DT, NS])
        gsc = sb("gsc", [P, DEPTH, DT, NS])
        gates = sb("gates", [P, 3, NS, W])
        GATE = {"sg": 0, "gg": 1, "ag": 2}
        th = sb("th", [P, 4, W])
        qk = sb("qk", [P, NS, QK])
        qkt = sb("qkt", [P, QK])
        v = sb("v", [P, NS, KV * HD])
        ck = sb("ck", [P, KV * HD])
        cv = sb("cv", [P, KV * HD])
        qT = sb("qT", [P, NS, 4, P])
        brT = {"C": qT, "B": HYf[:, 1, :].rearrange("p (s t q) -> p s t q", s=NS, t=WT),
               "A": cvacc[:, :, :, :].rearrange("p t s q -> p (t s q)").rearrange("p (s t q) -> p s t q", s=NS, t=WT)}
        kz = [sb("kz0", [P, KV, P]), sb("kz1", [P, KV, 2 * P])]
        prob, probT = (pre[:, r, :, :, :].rearrange("p g j c -> p (g j c)").rearrange("p (b k) -> p b k", b=2)
                       for r in range(2))
        qkg = sb("qkg", [P, 2, HD])
        st = sb("st", [P, 144])
        nmx = sb("nmx", [P, NS, HEADS, 2])
        scan_t = qkt[:, 0:2 * ROW].rearrange("p (a b) -> p a b", a=2)
        ldt = sb("ldt", [P, 2])

        proj_banks = [ctx.enter_context(nc.psum_tensor(f"proj{i}", [P, W], F32)) for i in range(4)]
        side_banks = [ctx.enter_context(nc.psum_tensor(f"side{i}", [P, W], F32)) for i in range(3)]
        long_banks = [ctx.enter_context(nc.psum_tensor("long0", [P, W], F32))]

        proj = Ring("proj", proj_banks, [((l, u, s), 1) for l, stg in todo for u, _, _ in units_of(stg)
                                         for s in range(NS)], sem)
        side = Ring("side", side_banks, [use for l, stg in todo for use in side_uses(l, stg)], sem)
        long_ = Ring("long", long_banks, [(("ada", stg[1]), 1) if stg[0] == "ada" else (("pv", l, stg[1]), 1)
                                          for l, stg in todo if stg[0] in ("ada", "att")], sem)

        slabs = []

        def w_src(l, u):
            if u in IN_UNITS:
                c0, n = IN_UNITS[u]
                return A["w_in"][l, :, c0:c0 + n]
            if u[:2] == "gl":
                c0 = 0 if u == "glua" else W
                return A["w_ssm_glu"][l, :, c0:c0 + W]
            if u[:2] == "wo":
                return A["w_out"][l, :, W * int(u[2]):W * int(u[2]) + W]
            h = int(u[3])
            if u[:2] == "me":
                c0 = MERGE0 + D * MERGE_OF[u[2]] + W * h
                return A["w_in"][l, :, c0:c0 + W]
            name = {"A": "w_conv_out", "B": "w_ssm_out", "C": "w_attn_out"}[u[2]]
            return A[name][l, :, W * h:W * h + W]

        for l, stg in todo:
            if stg[0] == "ada":
                src = A["w_ada"][stg[1]].rearrange("(k p) n -> p k n", p=P)
                for ct in range(3 * DT):
                    slabs.append((("ada", stg[1], ct), DT, P, src[:, :, P * ct:P * ct + P]))
            for u, nk, n in units_of(stg):
                src = w_src(l, u).rearrange("(k p) n -> p k n", p=P)
                for kp in range(nk // KT_SLAB):
                    slabs.append(((l, u, kp), KT_SLAB, n, src[:, KT_SLAB * kp:KT_SLAB * kp + KT_SLAB, :]))
        slab_at = {s[0]: n for n, s in enumerate(slabs)}
        slab_in = [sem(f"slab_in{r}") for r in range(RAW)]
        slab_used = sem("slab_used")
        slab_read, n_used = [], 0
        for key, _, _, _ in slabs:
            if key[0] == "ada" and key[2] == 3 * DT - 1:
                slab_read.append((long_.full, long_.at[("ada", key[1])][0] + 1))
            elif key[0] != "ada" and (key[0], key[1], key[2] + 1) not in {q[0] for q in slabs}:
                slab_read.append((proj.full, proj.at[(key[0], key[1], NS - 1)][0] + 1))
            else:
                n_used += 1
                slab_read.append((slab_used, n_used))

        def slab_view(key):
            n = slab_at[key]
            _, nk, cols, _ = slabs[n]
            return raw[:, n % RAW, 0:nk * cols].rearrange("p (k n) -> p k n", k=nk)

        def slab_landed(eng, key):
            n = slab_at[key]
            eng.wait_ge(slab_in[n % RAW], 16 * (n // RAW + 1))

        consts_in = sem("consts_in")
        x_in = sem("x_in")
        N_SMALL = 7
        small_in = sem("small_in")
        c_in = sem("c_in")
        b_in = sem("b_in")
        rows_in = sem("rows_in")
        cache_in = sem("cache_in")
        zeroed = sem("zeroed")
        ldt_spread = sem("ldt_spread")
        sq_done = sem("sq_done")
        rstd_done = sem("rstd_done")
        xn_done = sem("xn_done")
        ada_done = sem("ada_done")
        cond_th = sem("cond_th")
        cond_pre = sem("cond_pre")
        cond_done = sem("cond_done")
        gelu_pre = sem("gelu_pre")
        ln_pre = sem("ln_pre")
        N_ZERO = 4
        tab_dt = sem("tab_dt")
        tab_pre = sem("tab_pre")
        tab_act = sem("tab_act")
        tab_done = sem("tab_done")
        pre_done = sem("pre_done")
        bbar_done = sem("bbar_done")
        cp_done = sem("cp_done")
        bz_done = sem("bz_done")
        th_done = sem("th_done")
        u_in = sem("u_in")
        u_packed = sem("u_packed")
        y_in = sem("y_in")
        m_in = sem("m_in")
        conv_done = sem("conv_done")
        h0_done = sem("h0_done")
        scan_done = sem("scan_done")
        hy_fwd = sem("hy_fwd")
        hy_bwd = sem("hy_bwd")
        pv_read = sem("pv_read")
        gelu_done = sem("gelu_done")
        qk_sq = sem("qk_sq")
        qk_rs = sem("qk_rs")
        qk_done = sem("qk_done")
        nmax_done = sem("nmax_done")
        ln_var = sem("ln_var")
        ln_rs = sem("ln_rs")
        prodA = sem("prodA")
        prodB = sem("prodB")
        prodC = sem("prodC")
        prods = {"A": prodA, "B": prodB, "C": prodC}
        mixed_done = sem("mixed_done")
        x_done = sem("x_done")
        fin_sb = sem("fin_sb")
        out_done = sem("out_done")
        OUTS = DEPTH * 4 + NS
        dve_chain = sem("dve_chain")
        act_chain = sem("act_chain")
        pool_chain = sem("pool_chain")

        def u_gate(l, h, s):
            return ("gate", l, h, s)

        def ls(l, s):
            return NS * l + s + 1

        th_list, n_th = [], 0
        for l, stg in todo:
            if stg[0] == "unit" and stg[1] in ("sg", "gg", "ag"):
                for s in range(NS):
                    n_th += 1
                    th_list.append(((l, stg[1], s), (th_done, n_th), ("proj", (l, stg[1], s))))
            elif stg == ("unit", "cg"):
                th_list += [((l, "cg", s), ("proj", (l, "cg", s)), ("proj", (l, "ca", s))) for s in range(NS)]
            elif stg == ("unit", "glub"):
                th_list += [((l, "glub", s), ("proj", (l, "glub", s)), ("proj", (l, "glua", s))) for s in range(NS)]
            elif stg[0] == "gelu":
                n_th += 1
                th_list.append(((l, "gelu", stg[1]), (th_done, n_th), (gelu_done, ls(l, stg[1]))))
            elif stg[0] == "cback":
                n_th += 1
                th_list.append(((l, "ln", stg[1]), (th_done, n_th), (prodA, ls(l, stg[1]))))
            elif stg[0] == "comb":
                u = stg[1] + str(stg[2])
                th_list += [((l, "me" + u, s), ("proj", (l, "me" + u, s)), ("proj", (l, "br" + u, s)))
                            for s in range(NS)]
            elif stg[0] == "wout":
                th_list += [((l, "gate" + str(stg[1]), s), ("side", (u_gate(l, stg[1], s))),
                             ("proj", (l, "wo" + str(stg[1]), s))) for s in range(NS)]
        th_at = {k: n for n, (k, _, _) in enumerate(th_list)}

        def th_wait(eng, what):
            if what[0] == "proj":
                proj.drained(eng, what[1])
            elif what[0] == "side":
                side.drained(eng, what[1])
            else:
                eng.wait_ge(*what)

        def th_view(key):
            return th[:, th_at[key] % 4, :]

        def th_claim(act, key):
            if th_at[key] >= 4:
                th_wait(act, th_list[th_at[key] - 4][2])

        def th_ready(dve, key):
            th_wait(dve, th_list[th_at[key]][1])

        block = ctx.enter_context(nc.Block())

        @block.sync
        def _(sp):
            def small_loads(l):
                if l:
                    sp.wait_ge(out_done, 64 * l)
                    side.filled(sp, ("small", l - 1, 4))
                sp.dma_start(a32[0:G, 0, :].rearrange("g (d p) -> g d p", d=2),
                             A["ssm_a_re"][l].rearrange("d g p -> g d p")).then_inc(small_in, 16)
                sp.dma_start(a32[0:G, 1, :].rearrange("g (d p) -> g d p", d=2),
                             A["ssm_a_im"][l].rearrange("d g p -> g d p")).then_inc(small_in, 16)
                sp.dma_start(a32[0:G, 3, :].rearrange("g (d p) -> g d p", d=2),
                             A["state_ssm_re"][0, l].rearrange("d g p -> g d p")).then_inc(small_in, 16)
                sp.dma_start(a32[0:G, 4, :].rearrange("g (d p) -> g d p", d=2),
                             A["state_ssm_im"][0, l].rearrange("d g p -> g d p")).then_inc(small_in, 16)
                sp.dma_start(ldt[0:G, :], A["ssm_log_dt"][l].rearrange("d g -> g d"), allow_slow_non_contiguous=True).then_inc(small_in, 16)
                sp.dma_start(taprow[0:TAPS, :], A["conv_dw_w"][l]).then_inc(small_in, 16)
                sp.dma_start(taprow[TAPS:TAPS + 1, :], A["conv_dw_b"][l:l + 1, :]).then_inc(small_in, 16)
                for r, nm in enumerate(("ssm_c_re", "ssm_c_im")):
                    for d in range(2):
                        if l and r == 0 and d == 0:
                            side.filled(sp, ("pT", l - 1, 1, 3))
                        sp.dma_start(craw[:, r, :, SP * d:SP * d + SP],
                                     A[nm][l, d].rearrange("(t g) c p -> (g c) t p", t=4)).then_inc(c_in, 16)
                if l:
                    sp.wait_ge(bz_done, 2 * l)
                for r, nm in enumerate(("ssm_b_re", "ssm_b_im")):
                    for d in range(2):
                        sp.dma_start(braw[SP * d:SP * d + SP, r, :, :],
                                     A[nm][l, d].rearrange("g p c -> p g c")).then_inc(b_in, 16)

            def mid_loads(l):
                if l == 0:
                    side.filled(sp, ("small", 0, 2))
                if l:
                    sp.wait_ge(prodA, NS * l)
                    sp.wait_ge(gelu_done, NS * l)
                    sp.wait_ge(qk_done, NS * l)
                    sp.wait_ge(long_.full, long_.at[("pv", l - 1, 1)][0] + 1)
                for i, nm in enumerate(("ssm_d", "conv_ln_g", "conv_ln_b")):
                    sp.dma_start(rows[:, i, :], A[nm][l:l + 1, :].to_broadcast([P, W])).then_inc(rows_in, 16)
                sp.dma_start(qkg[:, 0, :], A["q_norm_g"][l:l + 1, :].to_broadcast([P, HD])).then_inc(rows_in, 16)
                sp.dma_start(qkg[:, 1, :], A["k_norm_g"][l:l + 1, :].to_broadcast([P, HD])).then_inc(rows_in, 16)
                sp.dma_start(ck[:, :], A["cache_k"][0, l].rearrange("t h d -> t (h d)")).then_inc(cache_in, 16)
                sp.dma_start(cv[:, :], A["cache_v"][0, l].rearrange("t h d -> t (h d)")).then_inc(cache_in, 16)

            def results(l):
                sp.wait_ge(qk_done, ls(l, 0))
                sp.dma_start(O["new_cache_k"][0, l].rearrange("t h d -> t (h d)"),
                             qk[:, 0, HEADS * HD:QK]).then_inc(out_done, 16)
                proj.drained(sp, (l, "kv", 0))
                sp.dma_start(O["new_cache_v"][0, l].rearrange("t h d -> t (h d)"), v[:, 0, :]).then_inc(out_done, 16)
                side.drained(sp, ("fin", l))
                for r, nm in enumerate(("new_state_ssm_re", "new_state_ssm_im")):
                    sp.dma_start(O[nm][0, l].rearrange("d g p -> g d p"),
                                 st32[0:G, r, :].rearrange("g (d p) -> g d p", d=2)).then_inc(out_done, 16)

            def slab(n):
                key, nk, cols, src = slabs[n]
                if n >= RAW:
                    sp.wait_ge(*slab_read[n - RAW])
                sp.dma_start(slab_view(key), src).then_inc(slab_in[n % RAW], 16)

            sp.dma_start(ident[:, :], C["ident"]).then_inc(consts_in, 16)
            sp.dma_start(condrow[0:DT, :], A["c_ctx"].rearrange("(t p) -> t p", p=P)).then_inc(consts_in, 16)
            sp.dma_start(condrow[DT:2 * DT, :], A["c"][0].rearrange("(t p) -> t p", p=P)).then_inc(consts_in, 16)
            for l in range(DEPTH):
                sp.dma_start(modrow[32 * l:32 * l + 24, :],
                             A["b_ada"][l].rearrange("(t p) -> t p", p=P)).then_inc(consts_in, 16)
                sp.dma_start(modrow[32 * l + 24:32 * l + 32, :],
                             A["norm_g"][l].rearrange("(t p) -> t p", p=P)).then_inc(consts_in, 16)
            sp.dma_start(expo[:, :], C["expo"]).then_inc(consts_in, 16)
            small_loads(0)
            sp.dma_start(x[:, 0, :], A["x_prompt"][0]).then_inc(x_in, 16)
            sp.dma_start(x[:, 1, :], A["x_sample"][0]).then_inc(x_in, 16)
            sp.dma_start(rope[:, :, :], C["rope"]).then_inc(consts_in, 16)
            n = 0
            for l, stg in todo:
                keys = [("ada", stg[1], ct) for ct in range(3 * DT)] if stg[0] == "ada" else []
                keys += [(l, u, kp) for u, nk, _ in units_of(stg) for kp in range(nk // KT_SLAB)]
                if stg == ("unit", "q"):
                    mid_loads(l)
                if stg[0] == "small" and stg[1]:
                    results(l)
                    small_loads(stg[1])
                for _ in keys:
                    slab(n)
                    n += 1
            results(DEPTH - 1)
            sp.wait_ge(x_done, 2 * NS * DEPTH)
            sp.dma_start(O["y_prompt"][0], x[:, 0, :]).then_inc(out_done, 16)
            sp.dma_start(O["y_sample"][0], x[:, 1, :]).then_inc(out_done, 16)
            sp.wait_ge(out_done, 16 * OUTS)


        @block.tensor
        def _(pe):
            T = nc.tensor

            def transpose(out, in_):
                k = in_.shape[0]
                return T.transpose(out, in_, ident[0:k, 0:k])

            for l, stg in todo:
                k = stg[0]
                if k == "small":
                    ll = stg[1]
                    key = lambda i: ("small", ll, i)
                    if ll == 0:
                        pe.wait_ge(consts_in, 16 * 9)
                    pe.wait_ge(small_in, 16 * N_SMALL * (ll + 1))
                    pe.wait_ge(ldt_spread, ll + 1)
                    side.claim(pe, key(0))
                    for i in range(5):
                        m = transpose(side.bank(key(0))[:, G * i:G * i + G], a32[0:G, i, :])
                    m.then_inc(side.full, 1)
                    side.claim(pe, key(1))
                    for t in range(WT):
                        m = transpose(side.bank(key(1))[:, 32 * t:32 * t + 32], taprow[0:32, P * t:P * t + P])
                    m.then_inc(side.full, 1)
                    if ll == 0:
                        side.claim(pe, key(2))
                        transpose(side.bank(key(2))[:, 0:64], modrow[0:64, :])
                        transpose(side.bank(key(2))[:, 64:80], condrow[0:2 * DT, :]).then_inc(side.full, 1)
                    pe.wait_ge(c_in, 64 * (ll + 1))
                    for r in range(2):
                        side.claim(pe, key(3 + r))
                        for t in range(4):
                            m = transpose(side.bank(key(3 + r))[:, P * t:P * t + P], craw[:, r, t, :])
                        m.then_inc(side.full, 1)
                elif k == "ada":
                    ll = stg[1]
                    pe.wait_ge(cond_done, 1)
                    long_.claim(pe, ("ada", ll))
                    for ct in range(3 * DT):
                        slab_landed(pe, ("ada", ll, ct))
                        w = slab_view(("ada", ll, ct))
                        for kt in range(DT):
                            m = T.matmul(long_.bank(("ada", ll))[:, NS * ct:NS * ct + NS], w[:, kt, :],
                                         cond[:, :, kt], start=(kt == 0), stop=(kt == DT - 1))
                        m.then_inc(slab_used if ct < 3 * DT - 1 else long_.full, 1)
                elif k == "preE":
                    ll, half = stg[1], stg[2]
                    pe.wait_ge(pre_done, 2 * ll + half + 1)
                    for r in range(2):
                        for q in range(2):
                            key = ("E", ll, 4 * half + 2 * r + q)
                            side.claim(pe, key)
                            for i in range(4):
                                g = 2 * (4 * q + i)
                                m = transpose(side.bank(key)[:, P * i:P * i + P],
                                              pre[:, r, g:g + 2, :, :].rearrange("p g j c -> p (g j c)"))
                            m.then_inc(side.full, 1)
                elif k == "hT":
                    s = stg[1]
                    pe.wait_ge(xn_done, ls(l, s))
                    for h in range(2):
                        key = ("hT", l, s, h)
                        side.claim(pe, key)
                        for i in range(4):
                            d = 4 * h + i
                            m = transpose(side.bank(key)[:, P * i:P * i + P], xn[:, s, P * d:P * d + P])
                        m.then_inc(side.full, 1)
                elif k == "UT":
                    pe.wait_ge(u_packed, l + 1)
                    for h in range(2):
                        key = ("UT", l, h)
                        side.claim(pe, key)
                        for i in range(8):
                            gp = 8 * h + i
                            m = transpose(side.bank(key)[:, 64 * i:64 * i + 64], Ug[:, P * gp:P * gp + P])
                        m.then_inc(side.full, 1)
                elif k == "convT":
                    s = stg[1]
                    proj.drained(pe, (l, "ca", s))
                    key = ("convT", l, s)
                    side.claim(pe, key)
                    for t in range(WT):
                        m = transpose(side.bank(key)[:, P * t:P * t + P], y2[:, s, P * t:P * t + P])
                    m.then_inc(side.full, 1)
                elif k == "S":
                    side.drained(pe, ("UT", l, 0))
                    side.drained(pe, ("UT", l, 1))
                    side.drained(pe, ("E", l, 5))
                    side.drained(pe, ("E", l, 6))
                    side.drained(pe, ("E", l, 7))
                    for i in range(8):
                        key = ("S", l, i)
                        side.claim(pe, key)
                        out = side.bank(key)[:, :].rearrange("p (g a r q) -> p g r a q", g=2, a=2, r=2)
                        for gg in range(2):
                            gp = 2 * i + gg
                            for r in range(2):
                                m = T.matmul(out[:, gg, r, :, :], E[:, r, gp, :], Uz[:, 2 * gp:2 * gp + 2, :],
                                             start=True, stop=True)
                        m.then_inc(side.full, 1)
                elif k == "K":
                    pe.wait_ge(cp_done, l + 1)
                    for i in range(8):
                        key = ("K", l, i)
                        if i % 4 == 0:
                            pe.wait_ge(bz_done, 2 * l + i // 4 + 1)
                        side.claim(pe, key)
                        for b in range(4):
                            g = 4 * i + b
                            for r in range(2):
                                m = T.matmul(side.bank(key)[0:48, 80 * b:80 * b + 80], bz[:, r, g % 16, :],
                                             CP[:, r, :, g, :], start=(r == 0), stop=(r == 1))
                        m.then_inc(side.full, 1)
                elif k == "qkT":
                    s = stg[1]
                    pe.wait_ge(qk_done, ls(l, s))
                    key = ("qT", l, s)
                    side.claim(pe, key)
                    for p in range(4):
                        m = transpose(side.bank(key)[:, P * p:P * p + P], qk[:, s, P * p:P * p + P])
                    m.then_inc(side.full, 1)
                    key = ("kT", l, s)
                    side.claim(pe, key)
                    m = transpose(side.bank(key)[:, 0:P], qk[:, s, HEADS * HD:QK])
                    if s == 1:
                        pe.wait_ge(cache_in, 32 * (l + 1))
                        m = transpose(side.bank(key)[:, P:2 * P], ck[:, :])
                    m.then_inc(side.full, 1)
                elif k == "att":
                    s = stg[1]
                    nk = s + 1
                    side.drained(pe, ("qT", l, s))
                    side.drained(pe, ("kT", l, s))
                    proj.drained(pe, (l, "kv", s))
                    long_.claim(pe, ("pv", l, s))

                    def scores(p):
                        key = ("sc", l, s, p)
                        side.claim(pe, key)
                        T.matmul(side.bank(key)[:, 0:2 * nk * P], qT[:, s, p, :],
                                 kz[s][:, :, :].rearrange("p a k -> p (a k)"), start=True, stop=True).then_inc(side.full, 1)

                    def probs_t(p):
                        key = ("pT", l, s, p)
                        side.claim(pe, key)
                        side.drained(pe, ("sc", l, s, p))
                        for i in range(2 * nk):
                            m = transpose(side.bank(key)[:, P * i:P * i + P], prob[:, p % 2, P * i:P * i + P])
                        m.then_inc(side.full, 1)

                    def values(p):
                        side.drained(pe, ("pT", l, s, p))
                        for a in range(2):
                            h = p + 4 * a
                            for kt in range(nk):
                                vv = (v[:, s, :] if kt == 0 else cv[:, :])[:, HD * a:HD * a + HD]
                                m = T.matmul(long_.bank(("pv", l, s))[:, HD * h:HD * h + HD],
                                             probT[:, p % 2, P * (nk * a + kt):P * (nk * a + kt) + P], vv,
                                             start=(kt == 0), stop=(kt == nk - 1))
                        return m

                    for p in range(6):
                        if p < 4:
                            scores(p)
                        if 1 <= p < 5:
                            probs_t(p - 1)
                        if p >= 2:
                            m = values(p - 2)
                            m.then_inc(long_.full, 1) if p == 5 else m.then_inc(pv_read, 1)
                elif k == "Y":
                    pe.wait_ge(m_in, 16 * 20 * (l + 1))
                    for q in range(4):
                        key = ("Y", l, q)
                        side.claim(pe, key)
                        pe.wait_ge(hy_fwd, 4 * l + q + 1)
                        pe.wait_ge(hy_bwd, 4 * l + q + 1)
                        for gi in range(8):
                            g = 8 * q + gi
                            o = side.bank(key)[0:64, 64 * gi:64 * gi + 64]
                            T.matmul(o, Uz[:, g, :], M[:, :, g // 2, :], start=True, stop=False)
                            for r in range(2):
                                m = T.matmul(o, HY[:, q % 2, gi, r, :, :].rearrange("p s k -> p (s k)"),
                                             CP[:, r, 1:L + 1, g, :], start=False, stop=(r == 1))
                        m.then_inc(side.full, 1)
                    key = ("fin", l)
                    side.claim(pe, key)
                    for r in range(2):
                        src = H[:, NCHUNK, :].rearrange("p (g r s) -> p r s g", g=G, r=2)[:, r, 0, :]
                        m = transpose(side.bank(key)[0:G, P * r:P * r + P], src)
                    m.then_inc(side.full, 1)
                elif k == "cback":
                    s = stg[1]
                    if s == 0:
                        pe.wait_ge(conv_done, WT * (l + 1))
                    key = ("cback", l, s)
                    side.claim(pe, key)
                    for t in range(WT):
                        m = transpose(side.bank(key)[:, P * t:P * t + P], cvacc[:, t, s, :])
                    m.then_inc(side.full, 1)
                elif k == "geT":
                    s = stg[1]
                    pe.wait_ge(gelu_done, ls(l, s))
                    key = ("geT", l, s)
                    side.claim(pe, key)
                    for t in range(WT):
                        m = transpose(side.bank(key)[:, P * t:P * t + P], ytok[:, s, P * t:P * t + P])
                    m.then_inc(side.full, 1)
                elif k == "brT":
                    b, s = stg[1], stg[2]
                    pe.wait_ge(prods[b], ls(l, s))
                    src = gates[:, {"A": 1, "B": 0, "C": 2}[b], s, :]
                    key = ("brT", l, b, s)
                    side.claim(pe, key)
                    for t in range(WT):
                        m = transpose(side.bank(key)[:, P * t:P * t + P], src[:, P * t:P * t + P])
                    m.then_inc(side.full, 1)
                elif k == "mixT":
                    s = stg[1]
                    pe.wait_ge(mixed_done, NS * 2 * l + 2 * NS)
                    for h in range(2):
                        key = ("mixT", l, s, h)
                        side.claim(pe, key)
                        for i in range(4):
                            d = 4 * h + i
                            m = transpose(side.bank(key)[:, P * i:P * i + P], mixed[:, s, P * d:P * d + P])
                        m.then_inc(side.full, 1)
                if k in ("unit", "comb", "wout"):
                    for u, nk, n in units_of(stg):
                        if u == "ssm":
                            for s in range(NS):
                                for h in range(2):
                                    side.drained(pe, ("hT", l, s, h))
                            lhs = hT
                        elif u in ("glua", "glub"):
                            for s in range(NS):
                                side.drained(pe, ("geT", l, s))
                            lhs = geT
                        elif u[:2] == "br":
                            for s in range(NS):
                                side.drained(pe, ("brT", l, u[2], s))
                            lhs = brT[u[2]]
                        elif u[:2] == "wo":
                            for s in range(NS):
                                for h in range(2):
                                    side.drained(pe, ("mixT", l, s, h))
                            lhs = hT
                        else:
                            lhs = hT
                        for s in range(NS):
                            proj.claim(pe, (l, u, s))
                        for kp in range(nk // KT_SLAB):
                            slab_landed(pe, (l, u, kp))
                            w = slab_view((l, u, kp))
                            for s in range(NS):
                                for i in range(KT_SLAB):
                                    kt = KT_SLAB * kp + i
                                    last = kt == nk - 1
                                    m = T.matmul(proj.bank((l, u, s))[:, 0:n], lhs[:, s, kt, :], w[:, i, :],
                                                 start=(kt == 0), stop=last)
                                if last:
                                    m.then_inc(proj.full, 1)
                            if not last:
                                m.then_inc(slab_used, 1)
                    if k == "wout":
                        h = stg[1]
                        for s in range(NS):
                            key = ("gate", l, h, s)
                            side.claim(pe, key)
                            for i in range(4):
                                col = ada[:, l, 2 * DT + 4 * h + i, s:s + 1]
                                m = T.matmul(side.bank(key)[:, P * i:P * i + P], col.to_broadcast([P, P]), ident[:, :],
                                             start=True, stop=True)
                            m.then_inc(side.full, 1)

        @block.scalar
        def _(act):
            S = nc.scalar
            n_chain = [0]

            def link(ins):
                n_chain[0] += 1
                ins.then_inc(act_chain, 1)
                act.wait_ge(act_chain, n_chain[0])

            for l, stg in todo:
                k = stg[0]
                if k == "small":
                    ll = stg[1]
                    if ll == 0:
                        act.wait_ge(cond_pre, 1)
                        S.activation(condt[:, :, :], cond[:, :, :], ACT.Tanh, scale=0.5).then_inc(cond_th, 1)
                    else:
                        act.wait_ge(cp_done, ll)
                    for r in range(2):
                        key = ("small", ll, 3 + r)
                        side.filled(act, key)
                        S.activation(cT[:, r, :, :].rearrange("p g c -> p (g c)"), side.bank(key)[:, :], ACT.Copy,
                                     scale=1.0 - 2.0 * r).then_inc(side.freed(key), 1)
                elif k == "tab":
                    ll = stg[1]
                    side.drained(act, ("small", ll, 0))
                    S.activation(ss[:, 0, :], t5[:, 2, :], ACT.Exp).then_inc(tab_dt, 1)
                    act.wait_ge(tab_pre, ll + 1)
                    S.activation(tt[0], tt[0], ACT.Exp)
                    S.activation(ss[:, 3, :], ss[:, 1, :], ACT.Tanh, scale=0.5)
                    S.activation(ss[:, 4, :], tt[3][:, 10 * G:11 * G], ACT.Sin, scale=0.5)
                    link(S.activation(tt[5], tt[5], ACT.Sin))
                    S.activation(tt[3], tt[3], ACT.Sin).then_inc(tab_act, 1)
                elif k == "preE":
                    ll, half = stg[1], stg[2]
                    for r in range(2):
                        for q in range(2):
                            key = ("E", ll, 4 * half + 2 * r + q)
                            side.filled(act, key)
                            g0 = 8 * half + 4 * q
                            S.activation(E[:, r, g0:g0 + 4, :].rearrange("p g q -> p (g q)"), side.bank(key)[:, :],
                                         ACT.Copy).then_inc(side.freed(key), 1)
                elif k == "xn":
                    s = stg[1]
                    if l == 0:
                        act.wait_ge(x_in, 32)
                    else:
                        act.wait_ge(x_done, 4 * l)
                        side.filled(act, ("fin", l - 1))
                        act.wait_ge(hy_fwd, 4 * l)
                        act.wait_ge(hy_bwd, 4 * l)
                    S.activation(xn[:, s, :], x[:, s, :], ACT.Square,
                                 accum_out=st[:, s:s + 1]).then_inc(sq_done, 1)
                elif k == "hT":
                    s = stg[1]
                    key = ("hT", l, s, 0)
                    side.filled(act, key)
                    act.wait_ge(ada_done, l + 1)
                    for i in range(4):
                        m = S.activation(hT[:, s, i, :], side.bank(key)[:, P * i:P * i + P], ACT.Identity,
                                         bias=ada[:, l, i, s:s + 1], scale=gsc[:, l, i, s:s + 1])
                    m.then_inc(side.freed(key), 1)
                elif k == "unit" and stg[1] in ("ssm", "q"):
                    if stg[1] == "ssm" and l:
                        act.wait_ge(gelu_done, NS * l)
                    for s in range(NS):
                        key = (l, stg[1], s)
                        proj.filled(act, key)
                        dst, src = utok[:, s, :], proj.bank(key)[:, :]
                        if stg[1] == "q":
                            dst = qk[:, s, 0:W].rearrange("p (h a d) -> p a h d", h=4, a=2)
                            src = src.rearrange("p (a h d) -> p a h d", a=2, h=4)
                        S.activation(dst, src, ACT.Copy).then_inc(proj.freed(key), 1)
                    if stg[1] == "ssm":
                        if l:
                            act.wait_ge(y_in, 16 * 8 * l)
                        for s in range(NS):
                            proj.drained(act, (l, "ssm", s))
                            for j in range(L):
                                act.dma_start(U64[NCHUNK * s:NCHUNK * s + NCHUNK, j, :],
                                              utok[j::L, s, :]).then_inc(u_in, 16)
                elif k == "unit" and stg[1] in ("cg", "glub", "sg", "gg", "ag"):
                    for s in range(NS):
                        key = (l, stg[1], s)
                        proj.filled(act, key)
                        th_claim(act, key)
                        m = S.activation(th_view(key), proj.bank(key)[:, :], ACT.Tanh, scale=0.5)
                        m.then_inc(proj.freed(key) if stg[1] in ("cg", "glub") else th_done, 1)
                elif k == "comb":
                    for s in range(NS):
                        key = (l, "me" + stg[1] + str(stg[2]), s)
                        proj.filled(act, key)
                        th_claim(act, key)
                        S.activation(th_view(key), proj.bank(key)[:, :], ACT.Tanh, scale=0.5).then_inc(proj.freed(key), 1)
                elif k == "UT":
                    act.wait_ge(u_in, 16 * 8 * (l + 1))
                    S.activation(Ug[:, :].rearrange("p (g j c) -> p g j c", g=G, j=L),
                                 U64.rearrange("p j (g c) -> p g j c", g=G), ACT.Copy).then_inc(u_packed, 1)
                    act.wait_ge(zeroed, N_ZERO)
                    for h in range(2):
                        key = ("UT", l, h)
                        side.filled(act, key)
                        dst = Uz[0:64, 16 * h:16 * h + 16, :].rearrange("p (g a) q -> p a g q", a=2)[:, 0, :, :]
                        S.activation(dst, side.bank(key)[0:64, :].rearrange("p (g q) -> p g q", g=8),
                                     ACT.Copy).then_inc(side.freed(key), 1)
                elif k == "convT":
                    s = stg[1]
                    key = ("convT", l, s)
                    side.filled(act, key)
                    act.wait_ge(zeroed, N_ZERO)
                    S.activation(cvpad[:, :, s, PAD:PAD + P], side.bank(key)[:, :].rearrange("p (t q) -> p t q", t=WT),
                                 ACT.Copy, scale=0.5).then_inc(side.freed(key), 1)
                elif k == "S":
                    for i in range(8):
                        key = ("S", l, i)
                        side.filled(act, key)
                        dst = H[0:64, 1:NCHUNK + 1, 16 * i:16 * i + 16].rearrange("p k x -> p x k")
                        S.activation(dst, side.bank(key)[0:64, :].rearrange("p (x k) -> p x k", k=NCHUNK),
                                     ACT.Copy).then_inc(side.freed(key), 1)
                elif k == "qkT":
                    s = stg[1]
                    key = ("qT", l, s)
                    side.filled(act, key)
                    S.activation(qT[:, s, :, :].rearrange("p a q -> p (a q)"), side.bank(key)[:, :],
                                 ACT.Copy).then_inc(side.freed(key), 1)
                    key = ("kT", l, s)
                    side.filled(act, key)
                    act.wait_ge(zeroed, N_ZERO)
                    S.activation(kz[s][0:64, 0, :], side.bank(key)[0:64, 0:P * (s + 1)],
                                 ACT.Copy).then_inc(side.freed(key), 1)
                elif k == "K":
                    for i in range(8):
                        key = ("K", l, i)
                        side.filled(act, key)
                        src = side.bank(key)[0:48, 0:320].rearrange("p (g a i c) -> p a i g c", g=2, a=2, i=L + 1)
                        for a in range(2):
                            dst = KTs[:, :, a, 32 * i:32 * i + 32].rearrange("p i (g c) -> p i g c", g=2)
                            m = S.activation(dst, src[:, a, :, :, :], ACT.Copy)
                        m.then_inc(side.freed(key), 1)
                    for i in range(5, 8):
                        side.drained(act, ("K", l, i))
                    Mf = M[:, :, :, :].rearrange("p t g c -> p t (g c)")
                    for a in range(2):
                        for s0 in range(L):
                            rows_ = slice(64 * a + GC * s0, 64 * a + GC * s0 + GC)
                            if s0 < L - 1:
                                act.dma_start(Mf[rows_, s0 + 1:L, :], KTs[0:GC, 1:L - s0, a, :]).then_inc(m_in, 16)
                            if s0:
                                act.dma_start(Mf[rows_, 0:s0, :], KTs[GC:2 * GC, L + 1 - s0:L + 1, a, :]).then_inc(m_in, 16)
                            act.dma_start(Mf[rows_, s0, :], KTs[2 * GC:3 * GC, 0, a, :]).then_inc(m_in, 16)
                elif k == "att":
                    s = stg[1]
                    nk = s + 1
                    for p in range(4):
                        key = ("sc", l, s, p)
                        side.filled(act, key)
                        act.wait_ge(nmax_done, 4 * (2 * l + s) + p + 1)
                        if p >= 2:
                            side.filled(act, ("pT", l, s, p - 2))
                        for a in range(2):
                            h = p + 4 * a
                            m = S.activation(prob[:, p % 2, nk * P * a:nk * P * a + nk * P],
                                             side.bank(key)[:, nk * P * a:nk * P * a + nk * P], ACT.Exp,
                                             bias=nmx[:, s, h, 0:1], scale=HD ** -0.5, accum_out=nmx[:, s, h, 1:2])
                        m.then_inc(side.freed(key), 1)
                elif k == "Y":
                    act.wait_ge(scan_done, l + 1)
                    for q in range(4 + 1):
                        if q < 4:
                            if q >= 2:
                                side.filled(act, ("Y", l, q - 2))
                            S.activation(HY[0:64, q % 2].rearrange("p g r s k -> p (g r s) k"),
                                         H[0:64, 0:NCHUNK, 32 * q:32 * q + 32].rearrange("p k x -> p x k"),
                                         ACT.Copy).then_inc(hy_fwd, 1)
                        if q >= 1:
                            key = ("Y", l, q - 1)
                            side.filled(act, key)
                            dst = U64.rearrange("p j (g c) -> p g j c", g=G)[:, 8 * (q - 1):8 * q, :, :]
                            S.activation(dst, side.bank(key)[0:64, :].rearrange("p (g j c) -> p g j c", g=8, j=L),
                                         ACT.Copy).then_inc(side.freed(key), 1)
                    for q in range(1, 4):
                        side.drained(act, ("Y", l, q))
                    for s in range(NS):
                        for j in range(L):
                            act.dma_start(ytok[j::L, s, :], U64[NCHUNK * s:NCHUNK * s + NCHUNK, j, :]).then_inc(y_in, 16)
                    key = ("fin", l)
                    side.filled(act, key)
                    S.activation(st32[0:G, :, :].rearrange("p r q -> p (r q)"), side.bank(key)[0:G, 0:2 * P],
                                 ACT.Copy).then_inc(side.freed(key), 1)
                elif k == "gelu":
                    key = (l, "gelu", stg[1])
                    act.wait_ge(gelu_pre, ls(l, stg[1]))
                    th_claim(act, key)
                    S.activation(th_view(key), qkt[:, 0:W], ACT.Tanh, scale=GELU_C).then_inc(th_done, 1)
                elif k == "cback":
                    key = (l, "ln", stg[1])
                    act.wait_ge(ln_pre, ls(l, stg[1]))
                    th_claim(act, key)
                    S.activation(th_view(key), qkt[:, 0:W], ACT.Tanh, scale=0.5).then_inc(th_done, 1)
                elif k == "geT":
                    s = stg[1]
                    key = ("geT", l, s)
                    side.filled(act, key)
                    S.activation(geT[:, s, :, :].rearrange("p t q -> p (t q)"), side.bank(key)[:, :], ACT.Copy,
                                 scale=0.5).then_inc(side.freed(key), 1)
                elif k == "brT":
                    b, s = stg[1], stg[2]
                    key = ("brT", l, b, s)
                    side.filled(act, key)
                    S.activation(brT[b][:, s, :, :].rearrange("p t q -> p (t q)"), side.bank(key)[:, :], ACT.Copy,
                                 scale=0.5 if b == "C" else 0.25).then_inc(side.freed(key), 1)
                elif k == "mixT":
                    s = stg[1]
                    key = ("mixT", l, s, 0)
                    side.filled(act, key)
                    S.activation(hT[:, s, 0:4, :].rearrange("p t q -> p (t q)"), side.bank(key)[:, :], ACT.Copy,
                                 scale=0.5).then_inc(side.freed(key), 1)
                elif k == "wout":
                    h = stg[1]
                    for s in range(NS):
                        key, gk = (l, "gate" + str(h), s), ("gate", l, h, s)
                        side.filled(act, gk)
                        th_claim(act, key)
                        S.activation(th_view(key), side.bank(gk)[:, :], ACT.Copy).then_inc(side.freed(gk), 1)

        @block.vector
        def _(dve):
            V = nc.vector
            n_chain = [0]

            def link(ins):
                n_chain[0] += 1
                ins.then_inc(dve_chain, 1)
                dve.wait_ge(dve_chain, n_chain[0])

            def tt_(out, a, b, op=ALU.mult):
                return V.tensor_tensor(out, a, b, op)

            for l, stg in todo:
                k = stg[0]
                if k == "small":
                    ll = stg[1]
                    key = ("small", ll, 0)
                    side.filled(dve, key)
                    V.tensor_copy(t5[:, :, :].rearrange("p i g -> p (i g)"),
                                  side.bank(key)[:, 0:5 * G]).then_inc(side.freed(key), 1)
                    key = ("small", ll, 1)
                    side.filled(dve, key)
                    V.tensor_copy(taps[:, :, :].rearrange("p t j -> p (t j)"),
                                  side.bank(key)[:, 0:WT * 32]).then_inc(side.freed(key), 1)
                    if ll == 0:
                        key = ("small", ll, 2)
                        side.filled(dve, key)
                        link(V.tensor_copy(modc[:, :, :].rearrange("p l t -> p (l t)"), side.bank(key)[:, 0:64]))
                        V.tensor_copy(cond[:, :, :].rearrange("p s t -> p (s t)"),
                                      side.bank(key)[:, 64:80]).then_inc(side.freed(key), 1)
                        side.drained(dve, key)
                        V.tensor_copy(condx[:, :, :], cond[:, :, :]).then_inc(cond_pre, 1)
                        dve.wait_ge(cond_th, 1)
                        dve.wait_ge(cond_pre, 1)
                        link(V.scalar_tensor_tensor(cond[:, :, :], condt[:, :, :], 1.0, condx[:, :, :], ALU.add, ALU.mult))
                        V.tensor_scalar(cond[:, :, :], cond[:, :, :], 0.5, None, ALU.mult).then_inc(cond_done, 1)
                elif k == "ada":
                    ll = stg[1]
                    key = ("ada", ll)
                    long_.filled(dve, key)
                    tt_(ada[:, ll, :, :], long_.bank(key)[:, 0:NS * 3 * DT].rearrange("p (t s) -> p t s", s=NS),
                        modc[:, ll, 0:24].unsqueeze(2).to_broadcast([P, 24, NS]), ALU.add).then_inc(long_.freed(key), 1)
                    long_.drained(dve, key)
                    V.scalar_tensor_tensor(gsc[:, ll, :, :], ada[:, ll, DT:2 * DT, :], 1.0,
                                           modc[:, ll, 24:32].unsqueeze(2).to_broadcast([P, DT, NS]),
                                           ALU.add, ALU.mult).then_inc(ada_done, 1)
                elif k == "tab":
                    ll = stg[1]
                    if ll:
                        dve.wait_ge(cp_done, ll)
                        side.filled(dve, ("K", ll - 1, 7))
                        side.filled(dve, ("E", ll - 1, 7))
                    side.filled(dve, ("small", ll, 4))
                    side.drained(dve, ("small", ll, 0))
                    dve.wait_ge(tab_dt, ll + 1)
                    tt_(ss[:, 1, :], t5[:, 0, :], ss[:, 0, :])
                    link(tt_(ss[:, 2, :], t5[:, 1, :], ss[:, 0, :]))
                    ex = expo[:, :].unsqueeze(2).to_broadcast([P, NEXP, G])
                    v3 = [t.rearrange("p (e g) -> p e g", e=NEXP) for t in tt]
                    tt_(v3[0], ss[:, 1:2, :].to_broadcast([P, NEXP, G]), ex)
                    link(tt_(v3[1], ss[:, 2:3, :].to_broadcast([P, NEXP, G]), ex))
                    link(V.tensor_scalar(tt[2], tt[1], 1.0 / TWO_PI, None, ALU.mult))
                    link(V.tensor_scalar(tt[4], tt[2], 0.25, None, ALU.add))
                    link(V.tensor_scalar(tt[2], tt[2], MAGIC, None, ALU.add))
                    link(V.tensor_scalar(tt[2], tt[2], MAGIC, None, ALU.subtract))
                    link(V.tensor_scalar(tt[4], tt[4], MAGIC, None, ALU.add))
                    link(V.tensor_scalar(tt[4], tt[4], MAGIC, None, ALU.subtract))
                    for turns, out in ((tt[2], tt[3]), (tt[4], tt[5])):
                        src = tt[1]
                        for part in PI_PARTS:
                            link(V.scalar_tensor_tensor(out, turns, -part, src, ALU.mult, ALU.add))
                            src = out
                    link(V.tensor_scalar(tt[5], tt[5], TWO_PI / 4, None, ALU.add))
                    link(V.tensor_scalar(tt[5], tt[5], 3.1415925, -3.1415925, ALU.min, ALU.max))
                    V.tensor_scalar(tt[3], tt[3], 3.1415925, -3.1415925, ALU.min, ALU.max).then_inc(tab_pre, 1)
                    dve.wait_ge(tab_act, ll + 1)
                    link(tt_(lamr[:, :, :].rearrange("p e g -> p (e g)"), tt[0], tt[5]))
                    link(tt_(lami[:, :, :].rearrange("p e g -> p (e g)"), tt[0], tt[3]))
                    sv = lambda i: ss[:, i, :]
                    cosy, siny = v3[5][:, 10, :], v3[3][:, 10, :]
                    link(V.tensor_scalar(sv(5), sv(3), -1.0, 1.0, ALU.mult, ALU.add))
                    link(V.reciprocal(sv(5), sv(5)))
                    link(V.scalar_tensor_tensor(sv(5), sv(5), 2.0, sv(3), ALU.mult, ALU.mult))
                    link(V.scalar_tensor_tensor(sv(6), sv(4), -2.0, sv(4), ALU.mult, ALU.mult))
                    link(tt_(sv(7), sv(5), cosy))
                    link(tt_(sv(6), sv(6), sv(7), ALU.add))
                    link(V.scalar_tensor_tensor(sv(7), sv(5), 1.0, siny, ALU.add, ALU.mult))
                    link(tt_(sv(8), t5[:, 0, :], t5[:, 0, :]))
                    link(tt_(sv(9), t5[:, 1, :], t5[:, 1, :]))
                    link(tt_(sv(8), sv(8), sv(9), ALU.add))
                    link(V.reciprocal(sv(8), sv(8)))
                    for o_, (a1, b1, a2, b2, op) in ((10, (6, 0, 7, 1, ALU.add)), (11, (7, 0, 6, 1, ALU.subtract))):
                        link(tt_(sv(12), sv(a1), t5[:, b1, :]))
                        link(tt_(sv(13), sv(a2), t5[:, b2, :]))
                        link(tt_(sv(12), sv(12), sv(13), op))
                        link(tt_(sv(o_), sv(12), sv(8)))
                    link(V.tensor_copy(lamR[:, :].rearrange("p (g x) -> p g x", g=G),
                                       lamr[:, 9, :].unsqueeze(2).to_broadcast([P, G, 2 * NS])))
                    lI = lamI[:, :].rearrange("p (g r s) -> p r g s", g=G, r=2)
                    li = lami[:, 9, :].unsqueeze(2).to_broadcast([P, G, NS])
                    V.tensor_scalar(lI[:, 0, :, :], li, -1.0, None, ALU.mult)
                    link(V.tensor_copy(lI[:, 1, :, :], li))
                    link(V.memset(h0[:, :], 0.0))
                    hv = h0[:, :].rearrange("p (g r s) -> p r g s", g=G, r=2)
                    link(V.tensor_copy(hv[:, 0, :, 1], t5[:, 3, :]))
                    V.tensor_copy(hv[:, 1, :, 1], t5[:, 4, :]).then_inc(tab_done, 1)
                elif k == "xn":
                    s = stg[1]
                    dve.wait_ge(rstd_done, ls(l, s))
                    V.tensor_scalar(xn[:, s, :], x[:, s, :], st[:, 4 + s:5 + s], None, ALU.mult).then_inc(xn_done, 1)
                elif k == "hT":
                    s = stg[1]
                    key = ("hT", l, s, 1)
                    side.filled(dve, key)
                    dve.wait_ge(ada_done, l + 1)
                    for i in range(4):
                        d = 4 + i
                        m = V.tensor_scalar(hT[:, s, d, :], side.bank(key)[:, P * i:P * i + P],
                                            gsc[:, l, d, s:s + 1], ada[:, l, d, s:s + 1], ALU.mult, ALU.add)
                    m.then_inc(side.freed(key), 1)
                elif k == "unit" and stg[1] == "cg":
                    for s in range(NS):
                        key, ka = (l, "cg", s), (l, "ca", s)
                        proj.filled(dve, ka)
                        th_ready(dve, key)
                        V.scalar_tensor_tensor(y2[:, s, :], th_view(key), 1.0, proj.bank(ka)[:, :],
                                               ALU.add, ALU.mult).then_inc(proj.freed(ka), 1)
                elif k == "unit" and stg[1] == "kv":
                    if l:
                        dve.wait_ge(out_done, 64 * l)
                    for s in range(NS):
                        key = (l, "kv", s)
                        proj.filled(dve, key)
                        V.tensor_copy(qk[:, s, HEADS * HD:QK], proj.bank(key)[:, 0:P])
                        V.tensor_copy(v[:, s, :], proj.bank(key)[:, P:2 * P]).then_inc(proj.freed(key), 1)
                elif k == "unit" and stg[1] in ("sg", "gg", "ag"):
                    for s in range(NS):
                        key = (l, stg[1], s)
                        th_ready(dve, key)
                        V.scalar_tensor_tensor(gates[:, GATE[stg[1]], s, :], th_view(key), 1.0, proj.bank(key)[:, :],
                                               ALU.add, ALU.mult).then_inc(proj.freed(key), 1)
                elif k == "unit" and stg[1] == "glua":
                    for s in range(NS):
                        key = (l, "glua", s)
                        proj.filled(dve, key)
                        th_ready(dve, (l, "glub", s))
                        V.scalar_tensor_tensor(qkt[:, 0:W], th_view((l, "glub", s)), 1.0, proj.bank(key)[:, :],
                                               ALU.add, ALU.mult).then_inc(proj.freed(key), 1)
                        proj.drained(dve, key)
                        tt_(gates[:, 0, s, :], gates[:, 0, s, :], qkt[:, 0:W]).then_inc(prodB, 1)
                        dve.wait_ge(prodB, ls(l, s))
                elif k == "UT":
                    dve.wait_ge(zeroed, N_ZERO)
                    for h in range(2):
                        key = ("UT", l, h)
                        side.filled(dve, key)
                        dst = Uz[64:128, 16 * h:16 * h + 16, :].rearrange("p (g a) q -> p a g q", a=2)[:, 1, :, :]
                        V.tensor_copy(dst, side.bank(key)[64:128, :].rearrange("p (g q) -> p g q", g=8)
                                      ).then_inc(side.freed(key), 1)
                elif k == "S":
                    for i in range(8):
                        key = ("S", l, i)
                        side.filled(dve, key)
                        dst = H[64:128, 1:NCHUNK + 1, 16 * i:16 * i + 16][:, ::-1, :].rearrange("p k x -> p x k")
                        V.tensor_copy(dst, side.bank(key)[64:128, :].rearrange("p (x k) -> p x k", k=NCHUNK)
                                      ).then_inc(side.freed(key), 1)
                elif k == "scan":
                    for i in range(5, 8):
                        side.drained(dve, ("S", l, i))
                    dve.wait_ge(tab_done, l + 1)
                    V.tensor_copy(H[:, 0, :], h0[:, :]).then_inc(h0_done, 1)
                    dve.wait_ge(h0_done, l + 1)
                    for c in range(NCHUNK):
                        hk = H[:, c, :]
                        swapped = hk.rearrange("p (g r s) -> p g r s", g=G, r=2)[:, :, ::-1, :]
                        link(tt_(scan_t[:, 0, :].rearrange("p (g r s) -> p g r s", g=G, r=2), swapped,
                                 lamI[:, :].rearrange("p (g r s) -> p g r s", g=G, r=2)))
                        link(tt_(scan_t[:, 1, :], hk, lamR[:, :]))
                        link(tt_(H[:, c + 1, :], H[:, c + 1, :], scan_t[:, 0, :], ALU.add))
                        if c < NCHUNK - 1:
                            link(tt_(H[:, c + 1, :], H[:, c + 1, :], scan_t[:, 1, :], ALU.add))
                        else:
                            tt_(H[:, c + 1, :], H[:, c + 1, :], scan_t[:, 1, :], ALU.add).then_inc(scan_done, 1)
                elif k == "qkn":
                    s = stg[1]
                    proj.drained(dve, (l, "q", s))
                    proj.drained(dve, (l, "kv", s))
                    dve.wait_ge(rows_in, 80 * (l + 1))
                    link(tt_(qkt[:, :], qk[:, s, :], qk[:, s, :]))
                    V.tensor_reduce(st[:, 16:26], qkt[:, :].rearrange("p (h d) -> p h d", d=HD), AX_X,
                                    ALU.add).then_inc(qk_sq, 1)
                    dve.wait_ge(qk_rs, ls(l, s))
                    q3 = qk[:, s, :].rearrange("p (h d) -> p h d", d=HD)
                    link(tt_(q3, q3, st[:, 48:58].unsqueeze(2).to_broadcast([P, HEADS + KV, HD])))
                    link(tt_(q3[:, 0:HEADS, :], q3[:, 0:HEADS, :], qkg[:, 0:1, :].to_broadcast([P, HEADS, HD])))
                    m = tt_(q3[:, HEADS:, :], q3[:, HEADS:, :], qkg[:, 1:2, :].to_broadcast([P, KV, HD]))
                    if s == 0:
                        m.then_inc(qk_done, 1)
                    else:
                        link(m)
                        dve.wait_ge(consts_in, 16 * 9)
                        link(tt_(qkt[:, :].rearrange("p (h d) -> p h d", d=HD), q3,
                                 rope[:, 0:1, :].to_broadcast([P, HEADS + KV, HD])))
                        r5 = prob[:, :, :].rearrange("p a b -> p (a b)")[:, 0:QK]
                        for a in range(2):
                            five = lambda t: t.rearrange("p (h f a c) -> p a h f c", f=2, a=2, c=16)
                            sin = rope[:, 1, :].rearrange("p (o f a c) -> p a o f c", o=1, f=2, a=2)[:, a]
                            link(tt_(five(r5)[:, a], five(qk[:, s, :])[:, 1 - a],
                                     sin.to_broadcast([P, HEADS + KV, 2, 16])))
                        tt_(qk[:, s, :], qkt[:, :], r5, ALU.add).then_inc(qk_done, 1)
                    dve.wait_ge(qk_done, ls(l, s))
                elif k == "qkT":
                    s = stg[1]
                    key = ("kT", l, s)
                    side.filled(dve, key)
                    dve.wait_ge(zeroed, N_ZERO)
                    V.tensor_copy(kz[s][64:128, 1, :], side.bank(key)[64:128, 0:P * (s + 1)]).then_inc(side.freed(key), 1)
                elif k == "conv":
                    t = stg[1]
                    for s in range(NS):
                        side.drained(dve, ("convT", l, s))
                    side.drained(dve, ("small", l, 1))
                    acc = cvacc[:, t, :, :]
                    for j in range(TAPS):
                        src = cvpad[:, t, :, j:j + P]
                        if j == 0:
                            m = V.tensor_scalar(acc, src, taps[:, t, 0:1], taps[:, t, TAPS:TAPS + 1], ALU.mult, ALU.add)
                        else:
                            m = V.scalar_tensor_tensor(acc, src, taps[:, t, j:j + 1], acc, ALU.mult, ALU.add)
                        if j < TAPS - 1:
                            link(m)
                    m.then_inc(conv_done, 1)
                elif k == "att":
                    s = stg[1]
                    nk = s + 1
                    for p in range(4 + 1):
                        if p < 4:
                            key = ("sc", l, s, p)
                            side.filled(dve, key)
                            link(V.tensor_reduce(st[:, 64 + 2 * p:66 + 2 * p],
                                                 side.bank(key)[:, 0:2 * nk * P].rearrange("p (a k) -> p a k", a=2),
                                                 AX_X, ALU.max))
                            V.tensor_scalar(nmx[:, s, p::4, 0], st[:, 64 + 2 * p:66 + 2 * p], -HD ** -0.5, None,
                                            ALU.mult).then_inc(nmax_done, 1)
                        if p >= 1:
                            key = ("pT", l, s, p - 1)
                            side.filled(dve, key)
                            if p - 1 >= 2:
                                dve.wait_ge(pv_read, 3 * (2 * l + s) + p - 2)
                            V.tensor_copy(probT[:, (p - 1) % 2, 0:2 * nk * P],
                                          side.bank(key)[:, 0:2 * nk * P]).then_inc(side.freed(key), 1)
                    key = ("pv", l, s)
                    long_.filled(dve, key)
                    link(V.reciprocal(st[:, 80:88], nmx[:, s, :, 1]))
                    tt_(qkt[:, 0:W].rearrange("p (h d) -> p h d", d=HD),
                        long_.bank(key)[:, :].rearrange("p (h d) -> p h d", d=HD),
                        st[:, 80:88].unsqueeze(2).to_broadcast([P, HEADS, HD])).then_inc(long_.freed(key), 1)
                    long_.drained(dve, key)
                    proj.drained(dve, (l, "ag", s))
                    tt_(gates[:, 2, s, :], gates[:, 2, s, :], qkt[:, 0:W]).then_inc(prodC, 1)
                    dve.wait_ge(prodC, ls(l, s))
                elif k == "Y":
                    dve.wait_ge(scan_done, l + 1)
                    for q in range(4):
                        if q >= 2:
                            side.filled(dve, ("Y", l, q - 2))
                        V.tensor_copy(HY[64:128, q % 2].rearrange("p g r s k -> p (g r s) k"),
                                      H[64:128, 0:NCHUNK, 32 * q:32 * q + 32][:, ::-1, :].rearrange("p k x -> p x k")
                                      ).then_inc(hy_bwd, 1)
                elif k == "gelu":
                    s = stg[1]
                    dve.wait_ge(y_in, 16 * 8 * (l + 1))
                    dve.wait_ge(rows_in, 80 * (l + 1))
                    yb, t = ytok[:, s, :], qkt[:, 0:W]
                    proj.drained(dve, (l, "ssm", s))
                    link(tt_(utok[:, s, :], utok[:, s, :], rows[:, 0, :]))
                    link(tt_(yb, yb, utok[:, s, :], ALU.add))
                    link(tt_(t, yb, yb))
                    link(V.tensor_scalar(t, t, GELU_A, 1.0, ALU.mult, ALU.add))
                    tt_(t, t, yb).then_inc(gelu_pre, 1)
                    th_ready(dve, (l, "gelu", s))
                    V.scalar_tensor_tensor(yb, th_view((l, "gelu", s)), 1.0, yb, ALU.add, ALU.mult).then_inc(gelu_done, 1)
                    dve.wait_ge(gelu_done, ls(l, s))
                elif k == "cback":
                    s = stg[1]
                    key = ("cback", l, s)
                    side.filled(dve, key)
                    link(V.bn_stats(st[:, 96:102], side.bank(key)[:, :]))
                    V.bn_aggr(st[:, 104:106], st[:, 96:102]).then_inc(ln_var, 1)
                    dve.wait_ge(ln_rs, ls(l, s))
                    t = qkt[:, 0:W]
                    V.tensor_scalar(t, side.bank(key)[:, :], st[:, 104:105], st[:, 112:113], ALU.subtract,
                                    ALU.mult).then_inc(side.freed(key), 1)
                    side.drained(dve, key)
                    link(tt_(t, t, rows[:, 1, :]))
                    tt_(t, t, rows[:, 2, :], ALU.add).then_inc(ln_pre, 1)
                    dve.wait_ge(ln_pre, ls(l, s))
                    th_ready(dve, (l, "ln", s))
                    link(V.scalar_tensor_tensor(t, th_view((l, "ln", s)), 1.0, t, ALU.add, ALU.mult))
                    proj.drained(dve, (l, "gg", s))
                    tt_(gates[:, 1, s, :], gates[:, 1, s, :], t).then_inc(prodA, 1)
                    dve.wait_ge(prodA, ls(l, s))
                elif k == "comb":
                    b, h = stg[1], stg[2]
                    for s in range(NS):
                        km, kb = (l, "me" + b + str(h), s), (l, "br" + b + str(h), s)
                        proj.filled(dve, kb)
                        th_ready(dve, km)
                        acc = mixed[:, s, W * h:W * h + W]
                        dst = acc if b == BRANCHES[0] else qkt[:, 0:W]
                        V.scalar_tensor_tensor(dst, th_view(km), 1.0, proj.bank(kb)[:, :], ALU.add,
                                               ALU.mult).then_inc(proj.freed(kb), 1)
                        proj.drained(dve, kb)
                        if b != BRANCHES[0]:
                            m = tt_(acc, acc, dst, ALU.add)
                            if b == BRANCHES[-1]:
                                m.then_inc(mixed_done, 1)
                                dve.wait_ge(mixed_done, 4 * l + 2 * h + s + 1)
                            else:
                                link(m)
                elif k == "mixT":
                    s = stg[1]
                    key = ("mixT", l, s, 1)
                    side.filled(dve, key)
                    V.tensor_scalar(hT[:, s, 4:8, :].rearrange("p t q -> p (t q)"), side.bank(key)[:, :], 0.5, None,
                                    ALU.mult).then_inc(side.freed(key), 1)
                elif k == "wout":
                    h = stg[1]
                    for s in range(NS):
                        kg, kw = (l, "gate" + str(h), s), (l, "wo" + str(h), s)
                        proj.filled(dve, kw)
                        th_ready(dve, kg)
                        tt_(qkt[:, 0:W], proj.bank(kw)[:, :], th_view(kg)).then_inc(proj.freed(kw), 1)
                        proj.drained(dve, kw)
                        tt_(x[:, s, W * h:W * h + W], x[:, s, W * h:W * h + W], qkt[:, 0:W], ALU.add).then_inc(x_done, 1)
                        dve.wait_ge(x_done, 4 * l + 2 * h + s + 1)

        @block.gpsimd
        def _(pool):
            Q = nc.gpsimd
            n_chain = [0]

            def link(ins):
                n_chain[0] += 1
                ins.then_inc(pool_chain, 1)
                pool.wait_ge(pool_chain, n_chain[0])

            def tt_(out, a, b, op=ALU.mult):
                return Q.tensor_tensor(out, a, b, op)

            def rsqrt_mean(dst, src, n, count, tmp, done):
                link(Q.tensor_scalar(tmp, src, 1.0 / n, EPS, ALU.mult, ALU.add))
                tt_(dst, tmp, st[:, 128:128 + count], ALU.pow).then_inc(done, 1)

            Q.memset(Uz[:, :, :], 0.0).then_inc(zeroed, 1)
            Q.memset(cvpad[:, :, :, :], 0.0).then_inc(zeroed, 1)
            Q.memset(kz[0][:, :, :], 0.0).then_inc(zeroed, 1)
            Q.memset(kz[1][:, :, :], 0.0).then_inc(zeroed, 1)
            link(Q.memset(st[:, 128:140], -0.5))
            for l, stg in todo:
                k = stg[0]
                if k == "small":
                    ll = stg[1]
                    pool.wait_ge(small_in, 16 * N_SMALL * (ll + 1))
                    Q.tensor_copy(a32[0:G, 2, :].rearrange("g (d p) -> g d p", d=2),
                                  ldt[0:G, :].unsqueeze(2).to_broadcast([G, 2, SP])).then_inc(ldt_spread, 1)
                elif k == "preP":
                    ll, half = stg[1], stg[2]
                    if half == 0:
                        pool.wait_ge(tab_done, ll + 1)
                        pool.wait_ge(b_in, 64 * (ll + 1))
                        side.filled(pool, ("small", ll, 4))
                        co = [ss[:, 10 + i, :].unsqueeze(2).to_broadcast([P, G, GC]) for i in range(2)]
                        t1, t2 = (tB[:, 512 * i:512 * i + 512].rearrange("p (g c) -> p g c", g=G) for i in range(2))
                        for r in range(2):
                            link(tt_(t1, co[0], braw[:, r, :, :]))
                            link(tt_(t2, co[1], braw[:, 1 - r, :, :]))
                            link(tt_(bbar[:, r, :, :], t1, t2, ALU.add if r else ALU.subtract))
                    else:
                        side.filled(pool, ("E", ll, 3))
                    g0 = 16 * half
                    lam = [t[:, L + 1:2 * L + 1, g0:g0 + 16].rearrange("p j g -> p g j").unsqueeze(3)
                           .to_broadcast([P, 16, L, GC]) for t in (lamr, lami)]
                    bb = [bbar[:, r, g0:g0 + 16, :].unsqueeze(2).to_broadcast([P, 16, L, GC]) for r in range(2)]
                    t1, t2 = (t[:, :].rearrange("p (g j c) -> p g j c", g=16, j=L) for t in (tA, tB))
                    for r in range(2):
                        link(tt_(t1, lam[0], bb[r]))
                        link(tt_(t2, lam[1], bb[1 - r]))
                        m = tt_(pre[:, r, :, :, :], t1, t2, ALU.add if r else ALU.subtract)
                        if r == 0:
                            link(m)
                        else:
                            m.then_inc(pre_done, 1)
                            pool.wait_ge(pre_done, 2 * ll + half + 1)
                elif k == "xn":
                    s = stg[1]
                    pool.wait_ge(sq_done, ls(l, s))
                    rsqrt_mean(st[:, 4 + s:5 + s], st[:, s:s + 1], D, 1, st[:, 8 + s:9 + s], rstd_done)
                elif k == "qkn":
                    s = stg[1]
                    pool.wait_ge(qk_sq, ls(l, s))
                    rsqrt_mean(st[:, 48:58], st[:, 16:26], HD, HEADS + KV, st[:, 32:42], qk_rs)
                elif k == "cback":
                    s = stg[1]
                    pool.wait_ge(ln_var, ls(l, s))
                    rsqrt_mean(st[:, 112:113], st[:, 105:106], 1.0, 1, st[:, 114:115], ln_rs)
                elif k == "cp":
                    side.filled(pool, ("S", l, 7))
                    side.drained(pool, ("small", l, 3))
                    side.drained(pool, ("small", l, 4))
                    for i0, n in ((0, 2), (2, 2), (4, 1)):
                        t1, t2 = (t[:, 0:512 * n].rearrange("p (i g c) -> p i g c", i=n, g=G) for t in (tA, tB))
                        lam = [t[:, i0:i0 + n, :].unsqueeze(3).to_broadcast([P, n, G, GC]) for t in (lamr, lami)]
                        cc = [cT[:, r:r + 1, :, :].to_broadcast([P, n, G, GC]) for r in range(2)]
                        for r in range(2):
                            link(tt_(t1, cc[r], lam[0]))
                            link(tt_(t2, cc[1 - r], lam[1]))
                            m = tt_(CP[:, r, i0:i0 + n, :, :], t1, t2, ALU.subtract if r else ALU.add)
                            if i0 == 4 and r == 1:
                                m.then_inc(cp_done, 1)
                                pool.wait_ge(cp_done, l + 1)
                            else:
                                link(m)
                    link(Q.memset(bz[:, :, :, :], 0.0))
                    for half in range(2):
                        if half:
                            side.filled(pool, ("K", l, 3))
                        g0 = 16 * half
                        link(Q.tensor_copy(bz[0:64, :, :, 0:GC], bbar[0:64, :, g0:g0 + 16, :]))
                        link(Q.tensor_copy(bz[64:128, :, :, GC:2 * GC], bbar[64:128, :, g0:g0 + 16, :]))
                        Q.tensor_copy(bz[:, :, :, 2 * GC:3 * GC], bbar[:, :, g0:g0 + 16, :]).then_inc(bz_done, 1)


OUTPUTS = (("y_prompt", (1, P, D)), ("y_sample", (1, P, D)), ("new_cache_k", (1, DEPTH, P, KV, HD)),
           ("new_cache_v", (1, DEPTH, P, KV, HD)), ("new_state_ssm_re", (1, DEPTH, 2, G, SP)),
           ("new_state_ssm_im", (1, DEPTH, 2, G, SP)))


def shape_constants():
    import numpy as np

    first = [[0, 1, 2, 3, 4], [3, 2, 1, 0], [L, 1]]
    second = [[0, 4, 3, 2, 1], [0, 1, 2, 3], [L, 1]]
    expo = np.zeros((P, NEXP), np.float32)
    expo[0:SP] = sum(first, [])
    expo[SP:P] = sum(second, [])
    grid_w, pairs = 64, HD // 4
    t = np.arange(P)
    inv = (10000.0 ** (-np.arange(pairs, dtype=np.float32) / pairs)).astype(np.float32)
    ang = np.stack([(t // grid_w)[:, None] * inv, (t % grid_w)[:, None] * inv], 1).astype(np.float32)
    rope = np.zeros((P, 2, 2, 2, pairs), np.float32)
    rope[:, 0, :, 0] = rope[:, 0, :, 1] = np.cos(ang)
    rope[:, 1, :, 0] = -np.sin(ang)
    rope[:, 1, :, 1] = np.sin(ang)
    return {"ident": np.eye(P, dtype=np.float32), "expo": expo, "rope": rope.reshape(P, 2, HD)}


def kernel(**inputs):
    import numpy as np
    import concourse.bacc as bacc
    from concourse.bass_utils import run_bass_kernel_spmd

    nc = bacc.Bacc("TRN2", target_bir_lowering=False, num_devices=1)
    arrays = {}

    def given(prefix, named):
        aps = {}
        for name, a in named.items():
            a = np.ascontiguousarray(a)
            arrays[prefix + name] = a
            aps[name] = nc.dram_tensor(prefix + name, a.shape, mybir.dt.from_np(a.dtype), kind="ExternalInput").ap()
        return aps

    A = given("in_", inputs)
    C = given("const_", shape_constants())
    O = {name: nc.dram_tensor("out_" + name, shape, F32, kind="ExternalOutput").ap() for name, shape in OUTPUTS}
    build(nc, A, C, O)
    r = run_bass_kernel_spmd(nc, [arrays], core_ids=[0])
    return tuple(r.results[0]["out_" + name] for name, _ in OUTPUTS)
```

```python
from contextlib import ExitStack

import concourse.bass as bass
from concourse import mybir

F32 = mybir.dt.float32
ALU = mybir.AluOpType
ACT = mybir.ActivationFunctionType
AX_X = mybir.AxisListType.X

P = 128
NS = 2
D = 1024
DT = D // P
DEPTH = 2
W = 512
WT = W // P
HEADS, KV, HD = 8, 2, 64
QK = (HEADS + KV) * HD
TAPS = 31
PAD = TAPS // 2
GC, G, SP = 16, 32, 64
L = 4
NCHUNK = P // L
GP = G // 2
ROW = G * 2 * NS
EPS = 1e-6
NEXP = 11
TWO_PI = 6.283185307179586
PI_PARTS = (6.28125, 0.0019350051879882812, 3.0199159819e-07)
MAGIC = 12582912.0

KT_SLAB = 2
RAW = 4

IN_UNITS = {"ssm": (1536, 512), "ca": (0, 512), "cg": (512, 512), "q": (2560, 512), "kv": (3072, 256),
            "sg": (2048, 512), "gg": (1024, 512), "ag": (3328, 512)}
MERGE0 = 3840
BRANCHES = ("C", "B", "A")
ADA_PARTS = 3
ADA_BANKS = D // W
MERGE_OF = {"A": 0, "B": 1, "C": 2}


def order(l):
    def nxt(*stage):
        return [stage] if l + 1 < DEPTH else []

    n = l + 1
    return ([("hT", 0), ("hT", 1), ("unit", "ssm")]
            + ([("preE", 0, 0), ("preP", 0, 1)] if l == 0 else [])
            + [("pack",), ("unit", "cg")] + ([("preE", 0, 1)] if l == 0 else [])
            + [("UT",), ("S",), ("cp",), ("bz", 0), ("scan", 0, 16, ()), ("unit", "ca"), ("convT", 0), ("convT", 1),
               ("unit", "q"), ("unit", "kv"), ("qkn", 0), ("qkn", 1), ("scan", 16, NCHUNK, (0, 1)),
               ("unit", "sg"), ("K", 0), ("bz", 1), ("unit", "gg"), ("K", 1), ("unit", "ag")]
            + ([("ada", 0, 2), ("adaT", 0, 2)] if l == 0 else [])
            + nxt("ada", n, 0) + [("Y",)] + nxt("adaT", n, 0)
            + [("qkT", 0), ("qkT", 1), ("att", 0)] + nxt("ada", n, 1)
            + [("att", 1)] + nxt("adaT", n, 1) + [("gelu", 0), ("gelu", 1), ("geT", 0), ("geT", 1)]
            + nxt("ada", n, 2) + nxt("adaT", n, 2)
            + [("brT", "C", 0), ("brT", "C", 1), ("conv", (2, 3)), ("comb", "C", 0), ("unit", "glub"), ("unit", "glua"),
               ("brT", "B", 0), ("brT", "B", 1), ("comb", "C", 1)]
            + nxt("small", n) + nxt("cT", n) + nxt("tab", n) + nxt("preP", n, 0)
            + [("comb", "B", 0), ("cback", 0), ("cback", 1), ("comb", "B", 1)]
            + nxt("preE", n, 0) + nxt("preP", n, 1)
            + [("brT", "A", 0), ("brT", "A", 1), ("comb", "A", 0)] + nxt("preE", n, 1) + [("comb", "A", 1)]
            + [("mixT", 0), ("mixT", 1), ("wout", 0), ("wout", 1)] + nxt("xn", n, 0) + nxt("xn", n, 1))


def stages():
    out = [(0, s) for s in (("cond",), ("ada", 0, 0), ("small", 0), ("xn", 0, 0), ("xn", 0, 1), ("tab", 0),
                            ("ada", 0, 1), ("adaT", 0, 0), ("adaT", 0, 1), ("cT", 0), ("preP", 0, 0))]
    for l in range(DEPTH):
        out += [(l, s) for s in order(l)]
    return out


def units_of(stage):
    if stage[0] == "unit":
        u = stage[1]
        if u in ("glua", "glub"):
            return [(u, WT, W)]
        return [(u, DT, IN_UNITS[u][1])]
    if stage[0] == "comb":
        return [("me" + stage[1] + str(stage[2]), DT, W), ("br" + stage[1] + str(stage[2]), WT, W)]
    if stage[0] == "wout":
        return [("wo" + str(stage[1]), DT, W)]
    return []


def side_uses(l, stage):
    k = stage[0]
    if k == "cond":
        return [(("cond",), 1)]
    if k == "small":
        return [(("small", stage[1], i), 1) for i in range(2)]
    if k == "cT":
        return [(("cT", stage[1], i), 1) for i in range(2)]
    if k == "adaT":
        return [(("adaT", stage[1], stage[2]), 1)]
    if k == "preE":
        return [(("E", stage[1], 4 * stage[2] + i), 1) for i in range(4)]
    if k == "hT":
        return [(("hT", l, stage[1], h), 1) for h in range(2)]
    if k == "UT":
        return [(("UT", l, h), 2) for h in range(2)]
    if k == "convT":
        return [(("convT", l, stage[1]), 1)]
    if k == "S":
        return [(("S", l, i), 2) for i in range(8)]
    if k == "qkT":
        return [(("qT", l, stage[1]), 1), (("kT", l, stage[1]), 2)]
    if k == "K":
        return [(("K", l, 4 * stage[1] + i), 1) for i in range(4)]
    if k == "att":
        s = stage[1]
        out = []
        for p in range(4 + 1):
            if p < 4:
                out.append((("sc", l, s, p), 1))
            if p >= 1:
                out.append((("pT", l, s, p - 1), 1))
        return out
    if k == "Y":
        return [(("Y", l, q), 1) for q in range(4)] + [(("fin", l), 1)]
    if k == "cback":
        return [(("cback", l, stage[1]), 1)]
    if k == "geT":
        return [(("geT", l, stage[1]), 1)]
    if k == "brT":
        return [(("brT", l, stage[1], stage[2]), 1)]
    if k == "mixT":
        return [(("mixT", l, stage[1], h), 1) for h in range(2)]
    if k == "wout":
        return [(("gate", l, stage[1], s), 1) for s in range(NS)]
    return []


class Ring:

    def __init__(self, name, banks, uses, sem):
        self.banks, self.full, self.free = banks, sem(name + "_full"), [sem(f"{name}_free{b}") for b in range(len(banks))]
        self.at, total = {}, [0] * len(banks)
        for n, (key, drains) in enumerate(uses):
            b = n % len(banks)
            self.at[key] = (n, b, total[b], total[b] + drains)
            total[b] += drains

    def bank(self, key):
        return self.banks[self.at[key][1]]

    def claim(self, pe, key):
        n, b, before, _ = self.at[key]
        if before:
            pe.wait_ge(self.free[b], before)

    def filled(self, eng, key):
        eng.wait_ge(self.full, self.at[key][0] + 1)

    def freed(self, key):
        return self.free[self.at[key][1]]

    def drained(self, eng, key):
        eng.wait_ge(self.free[self.at[key][1]], self.at[key][3])


def build(nc, A, C, O):
    with ExitStack() as ctx:
        def sb(name, shape):
            return ctx.enter_context(nc.sbuf_tensor(name, shape, F32))

        sems = {}

        def sem(name):
            if name not in sems:
                sems[name] = ctx.enter_context(nc.semaphore(name))
            return sems[name]

        todo = stages()

        ident = sb("ident", [P, P])
        expo = sb("expo", [P, NEXP])
        rope = sb("rope", [P, 2, HD])
        x = sb("x", [P, NS, D])
        H = sb("H", [P, NCHUNK + 1, ROW])
        xn = H[:, :, :].rearrange("p a b -> p (a b)")[:, 0:NS * D].rearrange("p (s d) -> p s d", s=NS)
        mixed = sb("mixed", [P, NS, D])
        y2 = mixed[:, :, 0:W]
        ytok = mixed[:, :, W:D]
        hT = sb("hT", [P, NS, DT, P])
        raw = sb("raw", [P, RAW, KT_SLAB * W])
        EC = sb("EC", [P, 2 * (L + 1) * W])
        E = EC[:, 0:2 * GP * P].rearrange("p (r g q) -> p r g q", r=2, g=GP)
        CP = EC[:, :].rearrange("p (r i g c) -> p r i g c", r=2, i=L + 1, g=G)
        M = sb("M", [P, L, GP, GC])
        pre = sb("pre", [P, 2, 16, L, GC])
        craw = pre[:, 0, :, :, :].rearrange("p g j c -> p (g j c)").rearrange("p (r t q) -> p r t q", r=2, t=4)
        tA = sb("tA", [P, 1024])
        tB = sb("tB", [P, 1024])
        braw = tA[:, :].rearrange("p (r g c) -> p r g c", r=2, g=G)
        bz = sb("bz", [P, 2, 16, 3 * GC])
        bbar = sb("bbar", [P, 2, G, GC])
        cT = sb("cT", [P, 2, G, GC])
        lamr = sb("lamr", [P, NEXP, G])
        lami = sb("lami", [P, NEXP, G])
        tt = [pre[:, 1, :, :, :].rearrange("p g j c -> p (g j c)")[:, 352 * i:352 * i + 352] for i in range(2)]
        bzf = bz[:, :, :, :].rearrange("p r g c -> p (r g c)")
        tt += [bzf[:, 352 * i:352 * i + 352] for i in range(4)]
        lamR = sb("lamR", [P, ROW])
        lamI = sb("lamI", [P, ROW])
        a32 = sb("a32", [P, 5, P])
        st32 = a32[:, 0:2, :]
        t5 = sb("t5", [P, 5, G])
        ss = sb("ss", [P, 16, G])
        wide = sb("wide", [P, (L + 1) * W])
        KTs = wide[0:3 * GC, :].rearrange("p (i a b) -> p i a b", i=L + 1, a=2)
        U64 = wide[0:NS * NCHUNK, 0:L * W].rearrange("p (j c) -> p j c", j=L)
        Uz = sb("Uz", [P, G, NS * NCHUNK])
        HY = sb("HY", [P, 2, 8, 2, NS, NCHUNK])
        HYf = HY[:, :, :, :, :, :].rearrange("p a g r s k -> p a (g r s k)")
        Ug = HY[0:NS * NCHUNK].rearrange("p a g r s k -> p (a g r s k)")
        geT = HYf[:, 0, :].rearrange("p (s t q) -> p s t q", s=NS, t=WT)
        utok = sb("utok", [P, NS, W])
        cvpad = sb("cvpad", [P, WT, NS, P + 2 * PAD])
        cvacc = sb("cvacc", [P, WT, NS, P])
        taps = sb("taps", [P, WT, TAPS + 1])
        taprow = sb("taprow", [P, W])
        rows = sb("rows", [P, 3, W])
        modrow = rows[:, 0, 0:P]
        condrow = rows[:, 0, P:2 * P]
        cond = sb("cond", [P, NS, DT])
        h0 = sb("h0", [P, ROW])
        modc = sb("modc", [P, DEPTH, 4 * DT])
        ada = sb("ada", [P, DEPTH, 3 * DT, NS])
        gsc = sb("gsc", [P, DEPTH, DT, NS])
        gates = sb("gates", [P, 3, NS, W])
        GATE = {"sg": 0, "gg": 1, "ag": 2}
        th = sb("th", [P, 4, W])
        adarow = th[:, 2:4, :].rearrange("p a b -> p (a b)")
        qk = sb("qk", [P, NS, QK])
        qkt = sb("qkt", [P, QK])
        v = sb("v", [P, NS, KV * HD])
        ck = sb("ck", [P, KV * HD])
        cv = sb("cv", [P, KV * HD])
        qT = sb("qT", [P, NS, 4, P])
        brT = {"C": qT, "B": HYf[:, 1, :].rearrange("p (s t q) -> p s t q", s=NS, t=WT),
               "A": cvacc[:, :, :, :].rearrange("p t s q -> p (t s q)").rearrange("p (s t q) -> p s t q", s=NS, t=WT)}
        kz = [sb("kz0", [P, KV, P]), sb("kz1", [P, KV, 2 * P])]
        prob, probT = (pre[:, r, :, :, :].rearrange("p g j c -> p (g j c)").rearrange("p (b k) -> p b k", b=2)
                       for r in range(2))
        qkg = sb("qkg", [P, 2, HD])
        st = sb("st", [P, 144])
        nmx = sb("nmx", [P, NS, HEADS, 2])
        scan_t = qkt[:, 0:2 * ROW].rearrange("p (a b) -> p a b", a=2)
        ldt = sb("ldt", [P, 2])

        proj_banks = [ctx.enter_context(nc.psum_tensor(f"proj{i}", [P, W], F32)) for i in range(4)]
        side_banks = [ctx.enter_context(nc.psum_tensor(f"side{i}", [P, W], F32)) for i in range(3)]
        long_banks = [ctx.enter_context(nc.psum_tensor("long0", [P, W], F32))]

        proj_uses = []
        for l, stg in todo:
            if stg[0] == "ada":
                proj_uses += [(stg + (b,), 1) for b in range(ADA_BANKS)]
            proj_uses += [((l, u, s), 1) for u, _, _ in units_of(stg) for s in range(NS)]
        proj = Ring("proj", proj_banks, proj_uses, sem)
        side = Ring("side", side_banks, [use for l, stg in todo for use in side_uses(l, stg)], sem)
        long_ = Ring("long", long_banks, [(("pv", l, stg[1]), 1) for l, stg in todo if stg[0] == "att"], sem)

        slabs = []

        def w_src(l, u):
            if u in IN_UNITS:
                c0, n = IN_UNITS[u]
                return A["w_in"][l, :, c0:c0 + n]
            if u[:2] == "gl":
                c0 = 0 if u == "glua" else W
                return A["w_ssm_glu"][l, :, c0:c0 + W]
            if u[:2] == "wo":
                return A["w_out"][l, :, W * int(u[2]):W * int(u[2]) + W]
            h = int(u[3])
            if u[:2] == "me":
                c0 = MERGE0 + D * MERGE_OF[u[2]] + W * h
                return A["w_in"][l, :, c0:c0 + W]
            name = {"A": "w_conv_out", "B": "w_ssm_out", "C": "w_attn_out"}[u[2]]
            return A[name][l, :, W * h:W * h + W]

        for l, stg in todo:
            if stg[0] == "ada":
                src = A["w_ada"][stg[1]].rearrange("(k p) n -> p k n", p=P)
                for kt in range(DT):
                    slabs.append((stg + (kt,), 1, D, src[:, kt:kt + 1, D * stg[2]:D * stg[2] + D]))
            for u, nk, n in units_of(stg):
                src = w_src(l, u).rearrange("(k p) n -> p k n", p=P)
                for kp in range(nk // KT_SLAB):
                    slabs.append(((l, u, kp), KT_SLAB, n, src[:, KT_SLAB * kp:KT_SLAB * kp + KT_SLAB, :]))
        slab_at = {s[0]: n for n, s in enumerate(slabs)}
        slab_in = [sem(f"slab_in{r}") for r in range(RAW)]
        slab_used = sem("slab_used")
        slab_read, n_used = [], 0
        for key, _, _, _ in slabs:
            if key[:-1] + (key[-1] + 1,) not in {q[0] for q in slabs}:
                last = ADA_BANKS - 1 if key[0] == "ada" else NS - 1
                slab_read.append((proj.full, proj.at[key[:-1] + (last,)][0] + 1))
            else:
                n_used += 1
                slab_read.append((slab_used, n_used))

        def slab_view(key):
            n = slab_at[key]
            _, nk, cols, _ = slabs[n]
            return raw[:, n % RAW, 0:nk * cols].rearrange("p (k n) -> p k n", k=nk)

        def slab_landed(eng, key):
            n = slab_at[key]
            eng.wait_ge(slab_in[n % RAW], 16 * (n // RAW + 1))

        consts_in = sem("consts_in")
        expo_in = sem("expo_in")
        rope_in = sem("rope_in")
        x_in = sem("x_in")
        N_SMALL = 7
        small_in = sem("small_in")
        c_in = sem("c_in")
        b_in = sem("b_in")
        rows_in = sem("rows_in")
        cache_in = sem("cache_in")
        zeroed = sem("zeroed")
        ldt_spread = sem("ldt_spread")
        sq_done = sem("sq_done")
        rstd_done = sem("rstd_done")
        xn_done = sem("xn_done")
        ada_done = sem("ada_done")
        cond_done = sem("cond_done")
        gelu_pre = sem("gelu_pre")
        ln_pre = sem("ln_pre")
        N_ZERO = 4
        tab_dt = sem("tab_dt")
        tab_pre = sem("tab_pre")
        tab_act = sem("tab_act")
        tab_done = sem("tab_done")
        pre_done = sem("pre_done")
        bbar_done = sem("bbar_done")
        cp_done = sem("cp_done")
        bz_done = sem("bz_done")
        th_done = sem("th_done")
        u_in = sem("u_in")
        u_packed = sem("u_packed")
        y_in = sem("y_in")
        m_in = sem("m_in")
        conv_done = sem("conv_done")
        h0_done = sem("h0_done")
        scan_done = sem("scan_done")
        hy_fwd = sem("hy_fwd")
        hy_bwd = sem("hy_bwd")
        pv_read = sem("pv_read")
        gelu_done = sem("gelu_done")
        qk_sq = sem("qk_sq")
        qk_rs = sem("qk_rs")
        qk_done = sem("qk_done")
        nmax_done = sem("nmax_done")
        ln_var = sem("ln_var")
        ln_rs = sem("ln_rs")
        prodA = sem("prodA")
        prodB = sem("prodB")
        prodC = sem("prodC")
        prods = {"A": prodA, "B": prodB, "C": prodC}
        mixed_done = sem("mixed_done")
        x_done = sem("x_done")
        fin_sb = sem("fin_sb")
        out_done = sem("out_done")
        OUTS = DEPTH * 4 + NS
        dve_chain = sem("dve_chain")
        act_chain = sem("act_chain")
        pool_chain = sem("pool_chain")

        def u_gate(l, h, s):
            return ("gate", l, h, s)

        def ls(l, s):
            return NS * l + s + 1

        th_list, n_th = [], 0
        for l, stg in todo:
            if stg == ("unit", "cg"):
                th_list += [((l, "cg", s), ("proj", (l, "cg", s)), ("proj", (l, "ca", s))) for s in range(NS)]
            elif stg == ("unit", "glub"):
                th_list += [((l, "glub", s), ("proj", (l, "glub", s)), ("proj", (l, "glua", s))) for s in range(NS)]
            elif stg[0] == "cback":
                n_th += 1
                th_list.append(((l, "ln", stg[1]), (th_done, n_th), (prodA, ls(l, stg[1]))))
            elif stg[0] == "comb":
                u = stg[1] + str(stg[2])
                th_list += [((l, "me" + u, s), ("proj", (l, "me" + u, s)), ("proj", (l, "br" + u, s)))
                            for s in range(NS)]
            elif stg[0] == "wout":
                th_list += [((l, "gate" + str(stg[1]), s), ("side", (u_gate(l, stg[1], s))),
                             ("proj", (l, "wo" + str(stg[1]), s))) for s in range(NS)]
        th_at = {k: n for n, (k, _, _) in enumerate(th_list)}

        def th_wait(eng, what):
            if what[0] == "proj":
                proj.drained(eng, what[1])
            elif what[0] == "side":
                side.drained(eng, what[1])
            else:
                eng.wait_ge(*what)

        def th_view(key):
            return th[:, th_at[key] % 4, :]

        def th_claim(act, key):
            if th_at[key] >= 4:
                th_wait(act, th_list[th_at[key] - 4][2])

        def th_ready(dve, key):
            th_wait(dve, th_list[th_at[key]][1])

        block = ctx.enter_context(nc.Block())

        @block.sync
        def _(sp):
            def small_loads(l):
                if l:
                    sp.wait_ge(out_done, 64 * l)
                    side.filled(sp, ("small", l - 1, 1))
                sp.dma_start(a32[0:G, 0, :].rearrange("g (d p) -> g d p", d=2),
                             A["ssm_a_re"][l].rearrange("d g p -> g d p")).then_inc(small_in, 16)
                sp.dma_start(a32[0:G, 1, :].rearrange("g (d p) -> g d p", d=2),
                             A["ssm_a_im"][l].rearrange("d g p -> g d p")).then_inc(small_in, 16)
                sp.dma_start(a32[0:G, 3, :].rearrange("g (d p) -> g d p", d=2),
                             A["state_ssm_re"][0, l].rearrange("d g p -> g d p")).then_inc(small_in, 16)
                sp.dma_start(a32[0:G, 4, :].rearrange("g (d p) -> g d p", d=2),
                             A["state_ssm_im"][0, l].rearrange("d g p -> g d p")).then_inc(small_in, 16)
                sp.dma_start(ldt[0:G, :], A["ssm_log_dt"][l].rearrange("d g -> g d"), allow_slow_non_contiguous=True).then_inc(small_in, 16)
                sp.dma_start(taprow[0:TAPS, :], A["conv_dw_w"][l]).then_inc(small_in, 16)
                sp.dma_start(taprow[TAPS:TAPS + 1, :], A["conv_dw_b"][l:l + 1, :]).then_inc(small_in, 16)

            def bc_loads(l):
                for r, nm in enumerate(("ssm_c_re", "ssm_c_im")):
                    for d in range(2):
                        if l and r == 0 and d == 0:
                            side.filled(sp, ("pT", l - 1, 1, 3))
                        sp.dma_start(craw[:, r, :, SP * d:SP * d + SP],
                                     A[nm][l, d].rearrange("(t g) c p -> (g c) t p", t=4)).then_inc(c_in, 16)
                if l:
                    sp.wait_ge(bz_done, 2 * l)
                for r, nm in enumerate(("ssm_b_re", "ssm_b_im")):
                    for d in range(2):
                        sp.dma_start(braw[SP * d:SP * d + SP, r, :, :],
                                     A[nm][l, d].rearrange("g p c -> p g c")).then_inc(b_in, 16)

            def mid_loads(l):
                if l == 0:
                    side.filled(sp, ("cond",))
                if l:
                    sp.wait_ge(prodA, NS * l)
                    sp.wait_ge(gelu_done, NS * l)
                    sp.wait_ge(qk_done, NS * l)
                    sp.wait_ge(long_.full, long_.at[("pv", l - 1, 1)][0] + 1)
                for i, nm in enumerate(("ssm_d", "conv_ln_g", "conv_ln_b")):
                    sp.dma_start(rows[:, i, :], A[nm][l:l + 1, :].to_broadcast([P, W])).then_inc(rows_in, 16)
                sp.dma_start(qkg[:, 0, :], A["q_norm_g"][l:l + 1, :].to_broadcast([P, HD])).then_inc(rows_in, 16)
                sp.dma_start(qkg[:, 1, :], A["k_norm_g"][l:l + 1, :].to_broadcast([P, HD])).then_inc(rows_in, 16)
                sp.dma_start(ck[:, :], A["cache_k"][0, l].rearrange("t h d -> t (h d)")).then_inc(cache_in, 16)
                sp.dma_start(cv[:, :], A["cache_v"][0, l].rearrange("t h d -> t (h d)")).then_inc(cache_in, 16)

            def results(l):
                sp.wait_ge(qk_done, ls(l, 0))
                sp.dma_start(O["new_cache_k"][0, l].rearrange("t h d -> t (h d)"),
                             qk[:, 0, HEADS * HD:QK]).then_inc(out_done, 16)
                proj.drained(sp, (l, "kv", 0))
                sp.dma_start(O["new_cache_v"][0, l].rearrange("t h d -> t (h d)"), v[:, 0, :]).then_inc(out_done, 16)
                side.drained(sp, ("fin", l))
                for r, nm in enumerate(("new_state_ssm_re", "new_state_ssm_im")):
                    sp.dma_start(O[nm][0, l].rearrange("d g p -> g d p"),
                                 st32[0:G, r, :].rearrange("g (d p) -> g d p", d=2)).then_inc(out_done, 16)

            def pack_u(l):
                if l:
                    sp.wait_ge(y_in, 16 * 8 * l)
                for s in range(NS):
                    proj.drained(sp, (l, "ssm", s))
                    for j in range(L):
                        sp.dma_start(U64[NCHUNK * s:NCHUNK * s + NCHUNK, j, :],
                                     utok[j::L, s, :]).then_inc(u_in, 16)

            def toeplitz(l):
                for i in range(5, 8):
                    side.drained(sp, ("K", l, i))
                Mf = M[:, :, :, :].rearrange("p t g c -> p t (g c)")
                for a in range(2):
                    for s0 in range(L):
                        rows_ = slice(64 * a + GC * s0, 64 * a + GC * s0 + GC)
                        if s0 < L - 1:
                            sp.dma_start(Mf[rows_, s0 + 1:L, :], KTs[0:GC, 1:L - s0, a, :]).then_inc(m_in, 16)
                        if s0:
                            sp.dma_start(Mf[rows_, 0:s0, :], KTs[GC:2 * GC, L + 1 - s0:L + 1, a, :]).then_inc(m_in, 16)
                        sp.dma_start(Mf[rows_, s0, :], KTs[2 * GC:3 * GC, 0, a, :]).then_inc(m_in, 16)

            def unpack_y(l):
                for q in range(1, 4):
                    side.drained(sp, ("Y", l, q))
                for s in range(NS):
                    for j in range(L):
                        sp.dma_start(ytok[j::L, s, :], U64[NCHUNK * s:NCHUNK * s + NCHUNK, j, :]).then_inc(y_in, 16)

            def slab(n):
                key, nk, cols, src = slabs[n]
                if n >= RAW:
                    sp.wait_ge(*slab_read[n - RAW])
                sp.dma_start(slab_view(key), src).then_inc(slab_in[n % RAW], 16)

            sp.dma_start(ident[:, :], C["ident"]).then_inc(consts_in, 16)
            sp.dma_start(condrow[0:DT, :], A["c_ctx"].rearrange("(t p) -> t p", p=P)).then_inc(consts_in, 16)
            sp.dma_start(condrow[DT:2 * DT, :], A["c"][0].rearrange("(t p) -> t p", p=P)).then_inc(consts_in, 16)
            for l in range(DEPTH):
                sp.dma_start(modrow[32 * l:32 * l + 24, :],
                             A["b_ada"][l].rearrange("(t p) -> t p", p=P)).then_inc(consts_in, 16)
                sp.dma_start(modrow[32 * l + 24:32 * l + 32, :],
                             A["norm_g"][l].rearrange("(t p) -> t p", p=P)).then_inc(consts_in, 16)
            first = RAW
            for n in range(first):
                slab(n)
            small_loads(0)
            sp.dma_start(expo[:, :], C["expo"]).then_inc(expo_in, 16)
            sp.dma_start(x[:, 0, :], A["x_prompt"][0]).then_inc(x_in, 16)
            sp.dma_start(x[:, 1, :], A["x_sample"][0]).then_inc(x_in, 16)
            sp.dma_start(rope[:, :, :], C["rope"]).then_inc(rope_in, 16)
            n = 0
            for l, stg in todo:
                keys = [stg + (kt,) for kt in range(DT)] if stg[0] == "ada" else []
                keys += [(l, u, kp) for u, nk, _ in units_of(stg) for kp in range(nk // KT_SLAB)]
                if stg == ("unit", "q"):
                    mid_loads(l)
                if stg[0] == "small" and stg[1]:
                    results(l)
                    small_loads(stg[1])
                    bc_loads(stg[1])
                if stg == ("ada", 0, 1):
                    bc_loads(0)
                for i, _ in enumerate(keys):
                    if stg == (("comb", BRANCHES[0], 0) if l == DEPTH - 1 else ("ada", l + 1, 1)) and i == RAW:
                        unpack_y(l)
                    if n >= first:
                        slab(n)
                    n += 1
                if stg == ("unit", "cg"):
                    pack_u(l)
                if stg == ("unit", "ag"):
                    toeplitz(l)
            results(DEPTH - 1)
            sp.wait_ge(x_done, 2 * NS * DEPTH)
            sp.dma_start(O["y_prompt"][0], x[:, 0, :]).then_inc(out_done, 16)
            sp.dma_start(O["y_sample"][0], x[:, 1, :]).then_inc(out_done, 16)
            sp.wait_ge(out_done, 16 * OUTS)


        @block.tensor
        def _(pe):
            T = nc.tensor

            def transpose(out, in_):
                k = in_.shape[0]
                return T.transpose(out, in_, ident[0:k, 0:k])

            for l, stg in todo:
                k = stg[0]
                if k == "cond":
                    pe.wait_ge(consts_in, 16 * 7)
                    side.claim(pe, ("cond",))
                    transpose(side.bank(("cond",))[:, 0:64], modrow[0:64, :])
                    transpose(side.bank(("cond",))[:, 64:80], condrow[0:2 * DT, :]).then_inc(side.full, 1)
                elif k == "small":
                    ll = stg[1]
                    key = lambda i: ("small", ll, i)
                    pe.wait_ge(small_in, 16 * N_SMALL * (ll + 1))
                    pe.wait_ge(ldt_spread, ll + 1)
                    side.claim(pe, key(0))
                    for i in range(5):
                        m = transpose(side.bank(key(0))[:, G * i:G * i + G], a32[0:G, i, :])
                    m.then_inc(side.full, 1)
                    side.claim(pe, key(1))
                    for t in range(WT):
                        m = transpose(side.bank(key(1))[:, 32 * t:32 * t + 32], taprow[0:32, P * t:P * t + P])
                    m.then_inc(side.full, 1)
                elif k == "cT":
                    ll = stg[1]
                    pe.wait_ge(c_in, 64 * (ll + 1))
                    for r in range(2):
                        key = ("cT", ll, r)
                        side.claim(pe, key)
                        for t in range(4):
                            m = transpose(side.bank(key)[:, P * t:P * t + P], craw[:, r, t, :])
                        m.then_inc(side.full, 1)
                elif k == "ada":
                    if stg[1:] == (0, 0):
                        pe.wait_ge(cond_done, 1)
                    for b in range(ADA_BANKS):
                        proj.claim(pe, stg + (b,))
                    for kt in range(DT):
                        slab_landed(pe, stg + (kt,))
                        w = slab_view(stg + (kt,))
                        for b in range(ADA_BANKS):
                            m = T.matmul(proj.bank(stg + (b,))[0:NS, :], cond[:, :, kt], w[:, 0, W * b:W * b + W],
                                         start=(kt == 0), stop=(kt == DT - 1))
                            if kt == DT - 1:
                                m.then_inc(proj.full, 1)
                        if kt < DT - 1:
                            m.then_inc(slab_used, 1)
                elif k == "adaT":
                    for b in range(ADA_BANKS):
                        proj.drained(pe, ("ada",) + stg[1:] + (b,))
                    side.claim(pe, stg)
                    for t in range(DT):
                        m = transpose(side.bank(stg)[:, NS * t:NS * t + NS], adarow[0:NS, P * t:P * t + P])
                    m.then_inc(side.full, 1)
                elif k == "preE":
                    ll, half = stg[1], stg[2]
                    pe.wait_ge(pre_done, 2 * ll + half + 1)
                    for r in range(2):
                        for q in range(2):
                            key = ("E", ll, 4 * half + 2 * r + q)
                            side.claim(pe, key)
                            for i in range(4):
                                g = 2 * (4 * q + i)
                                m = transpose(side.bank(key)[:, P * i:P * i + P],
                                              pre[:, r, g:g + 2, :, :].rearrange("p g j c -> p (g j c)"))
                            m.then_inc(side.full, 1)
                elif k == "hT":
                    s = stg[1]
                    pe.wait_ge(xn_done, ls(l, s))
                    for h in range(2):
                        key = ("hT", l, s, h)
                        side.claim(pe, key)
                        for i in range(4):
                            d = 4 * h + i
                            m = transpose(side.bank(key)[:, P * i:P * i + P], xn[:, s, P * d:P * d + P])
                        m.then_inc(side.full, 1)
                elif k == "UT":
                    pe.wait_ge(u_packed, l + 1)
                    for h in range(2):
                        key = ("UT", l, h)
                        side.claim(pe, key)
                        for i in range(8):
                            gp = 8 * h + i
                            m = transpose(side.bank(key)[:, 64 * i:64 * i + 64], Ug[:, P * gp:P * gp + P])
                        m.then_inc(side.full, 1)
                elif k == "convT":
                    s = stg[1]
                    proj.drained(pe, (l, "ca", s))
                    key = ("convT", l, s)
                    side.claim(pe, key)
                    for t in range(WT):
                        m = transpose(side.bank(key)[:, P * t:P * t + P], y2[:, s, P * t:P * t + P])
                    m.then_inc(side.full, 1)
                elif k == "S":
                    side.drained(pe, ("UT", l, 0))
                    side.drained(pe, ("UT", l, 1))
                    side.drained(pe, ("E", l, 5))
                    side.drained(pe, ("E", l, 6))
                    side.drained(pe, ("E", l, 7))
                    for i in range(8):
                        key = ("S", l, i)
                        side.claim(pe, key)
                        out = side.bank(key)[:, :].rearrange("p (g a r q) -> p g r a q", g=2, a=2, r=2)
                        for gg in range(2):
                            gp = 2 * i + gg
                            for r in range(2):
                                m = T.matmul(out[:, gg, r, :, :], E[:, r, gp, :], Uz[:, 2 * gp:2 * gp + 2, :],
                                             start=True, stop=True)
                        m.then_inc(side.full, 1)
                elif k == "K":
                    half = stg[1]
                    pe.wait_ge(cp_done, l + 1)
                    pe.wait_ge(bz_done, 2 * l + half + 1)
                    for i in range(4 * half, 4 * half + 4):
                        key = ("K", l, i)
                        side.claim(pe, key)
                        for b in range(4):
                            g = 4 * i + b
                            for r in range(2):
                                m = T.matmul(side.bank(key)[0:48, 80 * b:80 * b + 80], bz[:, r, g % 16, :],
                                             CP[:, r, :, g, :], start=(r == 0), stop=(r == 1))
                        m.then_inc(side.full, 1)
                elif k == "qkT":
                    s = stg[1]
                    pe.wait_ge(qk_done, ls(l, s))
                    key = ("qT", l, s)
                    side.claim(pe, key)
                    for p in range(4):
                        m = transpose(side.bank(key)[:, P * p:P * p + P], qk[:, s, P * p:P * p + P])
                    m.then_inc(side.full, 1)
                    key = ("kT", l, s)
                    side.claim(pe, key)
                    m = transpose(side.bank(key)[:, 0:P], qk[:, s, HEADS * HD:QK])
                    if s == 1:
                        pe.wait_ge(cache_in, 32 * (l + 1))
                        m = transpose(side.bank(key)[:, P:2 * P], ck[:, :])
                    m.then_inc(side.full, 1)
                elif k == "att":
                    s = stg[1]
                    nk = s + 1
                    side.drained(pe, ("qT", l, s))
                    side.drained(pe, ("kT", l, s))
                    proj.drained(pe, (l, "kv", s))
                    long_.claim(pe, ("pv", l, s))

                    def scores(p):
                        key = ("sc", l, s, p)
                        side.claim(pe, key)
                        T.matmul(side.bank(key)[:, 0:2 * nk * P], qT[:, s, p, :],
                                 kz[s][:, :, :].rearrange("p a k -> p (a k)"), start=True, stop=True).then_inc(side.full, 1)

                    def probs_t(p):
                        key = ("pT", l, s, p)
                        side.claim(pe, key)
                        side.drained(pe, ("sc", l, s, p))
                        for i in range(2 * nk):
                            m = transpose(side.bank(key)[:, P * i:P * i + P], prob[:, p % 2, P * i:P * i + P])
                        m.then_inc(side.full, 1)

                    def values(p):
                        side.drained(pe, ("pT", l, s, p))
                        for a in range(2):
                            h = p + 4 * a
                            for kt in range(nk):
                                vv = (v[:, s, :] if kt == 0 else cv[:, :])[:, HD * a:HD * a + HD]
                                m = T.matmul(long_.bank(("pv", l, s))[:, HD * h:HD * h + HD],
                                             probT[:, p % 2, P * (nk * a + kt):P * (nk * a + kt) + P], vv,
                                             start=(kt == 0), stop=(kt == nk - 1))
                        return m

                    for p in range(6):
                        if p < 4:
                            scores(p)
                        if 1 <= p < 5:
                            probs_t(p - 1)
                        if p >= 2:
                            m = values(p - 2)
                            m.then_inc(long_.full, 1) if p == 5 else m.then_inc(pv_read, 1)
                elif k == "Y":
                    pe.wait_ge(m_in, 16 * 20 * (l + 1))
                    for q in range(4):
                        key = ("Y", l, q)
                        side.claim(pe, key)
                        pe.wait_ge(hy_fwd, 4 * l + q + 1)
                        pe.wait_ge(hy_bwd, 4 * l + q + 1)
                        for gi in range(8):
                            g = 8 * q + gi
                            o = side.bank(key)[0:64, 64 * gi:64 * gi + 64]
                            T.matmul(o, Uz[:, g, :], M[:, :, g // 2, :], start=True, stop=False)
                            for r in range(2):
                                m = T.matmul(o, HY[:, q % 2, gi, r, :, :].rearrange("p s k -> p (s k)"),
                                             CP[:, r, 1:L + 1, g, :], start=False, stop=(r == 1))
                        m.then_inc(side.full, 1)
                    key = ("fin", l)
                    side.claim(pe, key)
                    for r in range(2):
                        src = H[:, NCHUNK, :].rearrange("p (g r s) -> p r s g", g=G, r=2)[:, r, 0, :]
                        m = transpose(side.bank(key)[0:G, P * r:P * r + P], src)
                    m.then_inc(side.full, 1)
                elif k == "cback":
                    s = stg[1]
                    if s == 0:
                        pe.wait_ge(conv_done, WT * (l + 1))
                    key = ("cback", l, s)
                    side.claim(pe, key)
                    for t in range(WT):
                        m = transpose(side.bank(key)[:, P * t:P * t + P], cvacc[:, t, s, :])
                    m.then_inc(side.full, 1)
                elif k == "geT":
                    s = stg[1]
                    pe.wait_ge(gelu_done, ls(l, s))
                    key = ("geT", l, s)
                    side.claim(pe, key)
                    for t in range(WT):
                        m = transpose(side.bank(key)[:, P * t:P * t + P], ytok[:, s, P * t:P * t + P])
                    m.then_inc(side.full, 1)
                elif k == "brT":
                    b, s = stg[1], stg[2]
                    pe.wait_ge(prods[b], ls(l, s))
                    src = gates[:, {"A": 1, "B": 0, "C": 2}[b], s, :]
                    key = ("brT", l, b, s)
                    side.claim(pe, key)
                    for t in range(WT):
                        m = transpose(side.bank(key)[:, P * t:P * t + P], src[:, P * t:P * t + P])
                    m.then_inc(side.full, 1)
                elif k == "mixT":
                    s = stg[1]
                    pe.wait_ge(mixed_done, NS * 2 * l + 2 * NS)
                    for h in range(2):
                        key = ("mixT", l, s, h)
                        side.claim(pe, key)
                        for i in range(4):
                            d = 4 * h + i
                            m = transpose(side.bank(key)[:, P * i:P * i + P], mixed[:, s, P * d:P * d + P])
                        m.then_inc(side.full, 1)
                if k in ("unit", "comb", "wout"):
                    for u, nk, n in units_of(stg):
                        if u == "ssm":
                            for s in range(NS):
                                for h in range(2):
                                    side.drained(pe, ("hT", l, s, h))
                            lhs = hT
                        elif u in ("glua", "glub"):
                            for s in range(NS):
                                side.drained(pe, ("geT", l, s))
                            lhs = geT
                        elif u[:2] == "br":
                            for s in range(NS):
                                side.drained(pe, ("brT", l, u[2], s))
                            lhs = brT[u[2]]
                        elif u[:2] == "wo":
                            for s in range(NS):
                                for h in range(2):
                                    side.drained(pe, ("mixT", l, s, h))
                            lhs = hT
                        else:
                            lhs = hT
                        for s in range(NS):
                            proj.claim(pe, (l, u, s))
                        for kp in range(nk // KT_SLAB):
                            slab_landed(pe, (l, u, kp))
                            w = slab_view((l, u, kp))
                            for s in range(NS):
                                for i in range(KT_SLAB):
                                    kt = KT_SLAB * kp + i
                                    last = kt == nk - 1
                                    m = T.matmul(proj.bank((l, u, s))[:, 0:n], lhs[:, s, kt, :], w[:, i, :],
                                                 start=(kt == 0), stop=last)
                                if last:
                                    m.then_inc(proj.full, 1)
                            if not last:
                                m.then_inc(slab_used, 1)
                    if k == "wout":
                        h = stg[1]
                        side.drained(pe, ("adaT", l, 2))
                        for s in range(NS):
                            key = ("gate", l, h, s)
                            side.claim(pe, key)
                            for i in range(4):
                                col = ada[:, l, 2 * DT + 4 * h + i, s:s + 1]
                                m = T.matmul(side.bank(key)[:, P * i:P * i + P], col.to_broadcast([P, P]), ident[:, :],
                                             start=True, stop=True)
                            m.then_inc(side.full, 1)

        @block.scalar
        def _(act):
            S = nc.scalar
            n_chain = [0]

            def link(ins):
                n_chain[0] += 1
                ins.then_inc(act_chain, 1)
                act.wait_ge(act_chain, n_chain[0])

            for l, stg in todo:
                k = stg[0]
                if k == "cond":
                    side.filled(act, ("cond",))
                    S.activation(cond[:, :, :].rearrange("p s t -> p (s t)"), side.bank(("cond",))[:, 64:80],
                                 ACT.Silu).then_inc(cond_done, 1)
                elif k == "ada":
                    if stg[1:] != (0, 0):
                        part = ADA_PARTS * stg[1] + stg[2] - 1
                        side.filled(act, ("adaT", part // ADA_PARTS, part % ADA_PARTS))
                    for b in range(ADA_BANKS):
                        key = stg + (b,)
                        proj.filled(act, key)
                        S.activation(adarow[0:NS, W * b:W * b + W], proj.bank(key)[0:NS, :],
                                     ACT.Copy).then_inc(proj.freed(key), 1)
                elif k == "cT":
                    ll = stg[1]
                    if ll:
                        act.wait_ge(cp_done, ll)
                    for r in range(2):
                        key = ("cT", ll, r)
                        side.filled(act, key)
                        S.activation(cT[:, r, :, :].rearrange("p g c -> p (g c)"), side.bank(key)[:, :], ACT.Copy,
                                     scale=1.0 - 2.0 * r).then_inc(side.freed(key), 1)
                elif k == "tab":
                    ll = stg[1]
                    side.drained(act, ("small", ll, 0))
                    S.activation(ss[:, 0, :], t5[:, 2, :], ACT.Exp).then_inc(tab_dt, 1)
                    act.wait_ge(tab_pre, ll + 1)
                    S.activation(tt[0], tt[0], ACT.Exp)
                    S.activation(ss[:, 3, :], ss[:, 1, :], ACT.Tanh, scale=0.5)
                    S.activation(ss[:, 4, :], tt[3][:, 10 * G:11 * G], ACT.Sin, scale=0.5)
                    link(S.activation(tt[5], tt[5], ACT.Sin))
                    S.activation(tt[3], tt[3], ACT.Sin).then_inc(tab_act, 1)
                elif k == "preE":
                    ll, half = stg[1], stg[2]
                    for r in range(2):
                        for q in range(2):
                            key = ("E", ll, 4 * half + 2 * r + q)
                            side.filled(act, key)
                            g0 = 8 * half + 4 * q
                            S.activation(E[:, r, g0:g0 + 4, :].rearrange("p g q -> p (g q)"), side.bank(key)[:, :],
                                         ACT.Copy).then_inc(side.freed(key), 1)
                elif k == "xn":
                    l, s = stg[1], stg[2]
                    if l == 0:
                        act.wait_ge(x_in, 32)
                    else:
                        act.wait_ge(x_done, 4 * l)
                        side.filled(act, ("fin", l - 1))
                        act.wait_ge(hy_fwd, 4 * l)
                        act.wait_ge(hy_bwd, 4 * l)
                    S.activation(xn[:, s, :], x[:, s, :], ACT.Square,
                                 accum_out=st[:, s:s + 1]).then_inc(sq_done, 1)
                elif k == "hT":
                    s = stg[1]
                    key = ("hT", l, s, 0)
                    side.filled(act, key)
                    act.wait_ge(ada_done, l + 1)
                    for i in range(4):
                        m = S.activation(hT[:, s, i, :], side.bank(key)[:, P * i:P * i + P], ACT.Identity,
                                         bias=ada[:, l, i, s:s + 1], scale=gsc[:, l, i, s:s + 1])
                    m.then_inc(side.freed(key), 1)
                elif k == "unit" and stg[1] in ("ssm", "q"):
                    if stg[1] == "ssm" and l:
                        act.wait_ge(gelu_done, NS * l)
                    for s in range(NS):
                        key = (l, stg[1], s)
                        proj.filled(act, key)
                        dst, src = utok[:, s, :], proj.bank(key)[:, :]
                        if stg[1] == "q":
                            dst = qk[:, s, 0:W].rearrange("p (h a d) -> p a h d", h=4, a=2)
                            src = src.rearrange("p (a h d) -> p a h d", a=2, h=4)
                        S.activation(dst, src, ACT.Copy).then_inc(proj.freed(key), 1)
                elif k == "unit" and stg[1] in ("cg", "glub"):
                    for s in range(NS):
                        key = (l, stg[1], s)
                        proj.filled(act, key)
                        th_claim(act, key)
                        S.activation(th_view(key), proj.bank(key)[:, :], ACT.Tanh, scale=0.5).then_inc(proj.freed(key), 1)
                elif k == "unit" and stg[1] in ("sg", "gg", "ag"):
                    for s in range(NS):
                        key = (l, stg[1], s)
                        proj.filled(act, key)
                        S.activation(gates[:, GATE[stg[1]], s, :], proj.bank(key)[:, :],
                                     ACT.Silu).then_inc(proj.freed(key), 1)
                elif k == "comb":
                    if stg == ("comb", BRANCHES[0], 0) and l + 1 < DEPTH:
                        side.filled(act, ("adaT", l + 1, ADA_PARTS - 1))
                    for s in range(NS):
                        key = (l, "me" + stg[1] + str(stg[2]), s)
                        proj.filled(act, key)
                        th_claim(act, key)
                        S.activation(th_view(key), proj.bank(key)[:, :], ACT.Tanh, scale=0.5).then_inc(proj.freed(key), 1)
                elif k == "pack":
                    act.wait_ge(u_in, 16 * 8 * (l + 1))
                    S.activation(Ug[:, :].rearrange("p (g j c) -> p g j c", g=G, j=L),
                                 U64.rearrange("p j (g c) -> p g j c", g=G), ACT.Copy).then_inc(u_packed, 1)
                elif k == "UT":
                    act.wait_ge(zeroed, N_ZERO)
                    for h in range(2):
                        key = ("UT", l, h)
                        side.filled(act, key)
                        dst = Uz[0:64, 16 * h:16 * h + 16, :].rearrange("p (g a) q -> p a g q", a=2)[:, 0, :, :]
                        S.activation(dst, side.bank(key)[0:64, :].rearrange("p (g q) -> p g q", g=8),
                                     ACT.Copy).then_inc(side.freed(key), 1)
                elif k == "convT":
                    s = stg[1]
                    key = ("convT", l, s)
                    side.filled(act, key)
                    act.wait_ge(zeroed, N_ZERO)
                    S.activation(cvpad[:, :, s, PAD:PAD + P], side.bank(key)[:, :].rearrange("p (t q) -> p t q", t=WT),
                                 ACT.Copy, scale=0.5).then_inc(side.freed(key), 1)
                elif k == "S":
                    for i in range(8):
                        key = ("S", l, i)
                        side.filled(act, key)
                        dst = H[0:64, 1:NCHUNK + 1, 16 * i:16 * i + 16].rearrange("p k x -> p x k")
                        S.activation(dst, side.bank(key)[0:64, :].rearrange("p (x k) -> p x k", k=NCHUNK),
                                     ACT.Copy).then_inc(side.freed(key), 1)
                elif k == "qkT":
                    s = stg[1]
                    key = ("qT", l, s)
                    side.filled(act, key)
                    S.activation(qT[:, s, :, :].rearrange("p a q -> p (a q)"), side.bank(key)[:, :],
                                 ACT.Copy).then_inc(side.freed(key), 1)
                    key = ("kT", l, s)
                    side.filled(act, key)
                    act.wait_ge(zeroed, N_ZERO)
                    S.activation(kz[s][0:64, 0, :], side.bank(key)[0:64, 0:P * (s + 1)],
                                 ACT.Copy).then_inc(side.freed(key), 1)
                elif k == "K":
                    for i in range(4 * stg[1], 4 * stg[1] + 4):
                        key = ("K", l, i)
                        side.filled(act, key)
                        src = side.bank(key)[0:48, 0:320].rearrange("p (g a i c) -> p a i g c", g=2, a=2, i=L + 1)
                        for a in range(2):
                            dst = KTs[:, :, a, 32 * i:32 * i + 32].rearrange("p i (g c) -> p i g c", g=2)
                            m = S.activation(dst, src[:, a, :, :, :], ACT.Copy)
                        m.then_inc(side.freed(key), 1)
                elif k == "att":
                    s = stg[1]
                    nk = s + 1
                    for p in range(4):
                        key = ("sc", l, s, p)
                        side.filled(act, key)
                        act.wait_ge(nmax_done, 4 * (2 * l + s) + p + 1)
                        if p >= 2:
                            side.filled(act, ("pT", l, s, p - 2))
                        for a in range(2):
                            h = p + 4 * a
                            m = S.activation(prob[:, p % 2, nk * P * a:nk * P * a + nk * P],
                                             side.bank(key)[:, nk * P * a:nk * P * a + nk * P], ACT.Exp,
                                             bias=nmx[:, s, h, 0:1], scale=HD ** -0.5, accum_out=nmx[:, s, h, 1:2])
                        m.then_inc(side.freed(key), 1)
                elif k == "Y":
                    act.wait_ge(scan_done, l + 1)
                    for q in range(4 + 1):
                        if q < 4:
                            if q >= 2:
                                side.filled(act, ("Y", l, q - 2))
                            S.activation(HY[0:64, q % 2].rearrange("p g r s k -> p (g r s) k"),
                                         H[0:64, 0:NCHUNK, 32 * q:32 * q + 32].rearrange("p k x -> p x k"),
                                         ACT.Copy).then_inc(hy_fwd, 1)
                        if q >= 1:
                            key = ("Y", l, q - 1)
                            side.filled(act, key)
                            dst = U64.rearrange("p j (g c) -> p g j c", g=G)[:, 8 * (q - 1):8 * q, :, :]
                            S.activation(dst, side.bank(key)[0:64, :].rearrange("p (g j c) -> p g j c", g=8, j=L),
                                         ACT.Copy).then_inc(side.freed(key), 1)
                    key = ("fin", l)
                    side.filled(act, key)
                    S.activation(st32[0:G, :, :].rearrange("p r q -> p (r q)"), side.bank(key)[0:G, 0:2 * P],
                                 ACT.Copy).then_inc(side.freed(key), 1)
                elif k == "gelu":
                    s = stg[1]
                    act.wait_ge(gelu_pre, ls(l, s))
                    S.activation(ytok[:, s, :], ytok[:, s, :], ACT.Gelu_apprx_tanh).then_inc(gelu_done, 1)
                elif k == "cback":
                    key = (l, "ln", stg[1])
                    act.wait_ge(ln_pre, ls(l, stg[1]))
                    th_claim(act, key)
                    S.activation(th_view(key), qkt[:, 0:W], ACT.Silu).then_inc(th_done, 1)
                elif k == "geT":
                    s = stg[1]
                    key = ("geT", l, s)
                    side.filled(act, key)
                    S.activation(geT[:, s, :, :].rearrange("p t q -> p (t q)"), side.bank(key)[:, :],
                                 ACT.Copy).then_inc(side.freed(key), 1)
                elif k == "brT":
                    b, s = stg[1], stg[2]
                    key = ("brT", l, b, s)
                    side.filled(act, key)
                    S.activation(brT[b][:, s, :, :].rearrange("p t q -> p (t q)"), side.bank(key)[:, :], ACT.Copy,
                                 scale=0.5 if b == "B" else 1.0).then_inc(side.freed(key), 1)
                elif k == "mixT":
                    s = stg[1]
                    key = ("mixT", l, s, 0)
                    side.filled(act, key)
                    S.activation(hT[:, s, 0:4, :].rearrange("p t q -> p (t q)"), side.bank(key)[:, :], ACT.Copy,
                                 scale=0.5).then_inc(side.freed(key), 1)
                elif k == "wout":
                    h = stg[1]
                    for s in range(NS):
                        key, gk = (l, "gate" + str(h), s), ("gate", l, h, s)
                        side.filled(act, gk)
                        th_claim(act, key)
                        S.activation(th_view(key), side.bank(gk)[:, :], ACT.Copy).then_inc(side.freed(gk), 1)

        @block.vector
        def _(dve):
            V = nc.vector
            n_chain = [0]

            def link(ins):
                n_chain[0] += 1
                ins.then_inc(dve_chain, 1)
                dve.wait_ge(dve_chain, n_chain[0])

            def tt_(out, a, b, op=ALU.mult):
                return V.tensor_tensor(out, a, b, op)

            made = {}

            def needs(*operands):
                at = max([made.get(o, 0) for o in operands])
                if at:
                    dve.wait_ge(dve_chain, at)

            def makes(operand, ins):
                n_chain[0] += 1
                ins.then_inc(dve_chain, 1)
                made[operand] = n_chain[0]

            def scan_step(l, c, i):
                four = lambda t: t.rearrange("p (g r s) -> p g r s", g=G, r=2)
                h, h1 = H[:, c, :], H[:, c + 1, :]
                if i == 0:
                    needs("h")
                    makes("cross", tt_(four(scan_t[:, 0, :]), four(h)[:, :, ::-1, :], four(lamI[:, :])))
                elif i == 1:
                    makes("straight", tt_(scan_t[:, 1, :], h, lamR[:, :]))
                elif i == 2:
                    needs("cross")
                    makes("h", tt_(h1, h1, scan_t[:, 0, :], ALU.add))
                else:
                    needs("h", "straight")
                    m = tt_(h1, h1, scan_t[:, 1, :], ALU.add)
                    if c < NCHUNK - 1:
                        makes("h", m)
                    else:
                        m.then_inc(scan_done, 1)

            def conv_ready(l):
                for s in range(NS):
                    side.drained(dve, ("convT", l, s))
                side.drained(dve, ("small", l, 1))

            def conv_tap(t, j):
                acc, src = cvacc[:, t, :, :], cvpad[:, t, :, j:j + P]
                if j == 0:
                    m = V.tensor_scalar(acc, src, taps[:, t, 0:1], taps[:, t, TAPS:TAPS + 1], ALU.mult, ALU.add)
                else:
                    needs(("sum", t))
                    m = V.scalar_tensor_tensor(acc, src, taps[:, t, j:j + 1], acc, ALU.mult, ALU.add)
                if j < TAPS - 1:
                    makes(("sum", t), m)
                else:
                    m.then_inc(conv_done, 1)

            for l, stg in todo:
                k = stg[0]
                if k == "cond":
                    key = ("cond",)
                    side.filled(dve, key)
                    dve.wait_ge(cond_done, 1)
                    V.tensor_copy(modc[:, :, :].rearrange("p l t -> p (l t)"),
                                  side.bank(key)[:, 0:64]).then_inc(side.freed(key), 1)
                elif k == "small":
                    ll = stg[1]
                    key = ("small", ll, 0)
                    side.filled(dve, key)
                    V.tensor_copy(t5[:, :, :].rearrange("p i g -> p (i g)"),
                                  side.bank(key)[:, 0:5 * G]).then_inc(side.freed(key), 1)
                    key = ("small", ll, 1)
                    side.filled(dve, key)
                    V.tensor_copy(taps[:, :, :].rearrange("p t j -> p (t j)"),
                                  side.bank(key)[:, 0:WT * 32]).then_inc(side.freed(key), 1)
                elif k == "adaT":
                    ll, c = stg[1], stg[2]
                    side.filled(dve, stg)
                    side.drained(dve, ("cond",))
                    part = slice(DT * c, DT * c + DT)
                    tt_(ada[:, ll, part, :], side.bank(stg)[:, 0:NS * DT].rearrange("p (t s) -> p t s", s=NS),
                        modc[:, ll, part].unsqueeze(2).to_broadcast([P, DT, NS]), ALU.add).then_inc(side.freed(stg), 1)
                    if c == 1:
                        side.drained(dve, stg)
                        V.scalar_tensor_tensor(gsc[:, ll, :, :], ada[:, ll, part, :], 1.0,
                                               modc[:, ll, 24:32].unsqueeze(2).to_broadcast([P, DT, NS]),
                                               ALU.add, ALU.mult).then_inc(ada_done, 1)
                elif k == "tab":
                    ll = stg[1]
                    if ll:
                        dve.wait_ge(cp_done, ll)
                        side.filled(dve, ("K", ll - 1, 7))
                        side.filled(dve, ("E", ll - 1, 7))
                    side.drained(dve, ("small", ll, 0))
                    dve.wait_ge(expo_in, 16)
                    dve.wait_ge(tab_dt, ll + 1)
                    tt_(ss[:, 1, :], t5[:, 0, :], ss[:, 0, :])
                    link(tt_(ss[:, 2, :], t5[:, 1, :], ss[:, 0, :]))
                    ex = expo[:, :].unsqueeze(2).to_broadcast([P, NEXP, G])
                    v3 = [t.rearrange("p (e g) -> p e g", e=NEXP) for t in tt]
                    tt_(v3[0], ss[:, 1:2, :].to_broadcast([P, NEXP, G]), ex)
                    link(tt_(v3[1], ss[:, 2:3, :].to_broadcast([P, NEXP, G]), ex))
                    link(V.tensor_scalar(tt[2], tt[1], 1.0 / TWO_PI, None, ALU.mult))
                    link(V.tensor_scalar(tt[4], tt[2], 0.25, None, ALU.add))
                    link(V.tensor_scalar(tt[2], tt[2], MAGIC, None, ALU.add))
                    link(V.tensor_scalar(tt[2], tt[2], MAGIC, None, ALU.subtract))
                    link(V.tensor_scalar(tt[4], tt[4], MAGIC, None, ALU.add))
                    link(V.tensor_scalar(tt[4], tt[4], MAGIC, None, ALU.subtract))
                    for turns, out in ((tt[2], tt[3]), (tt[4], tt[5])):
                        src = tt[1]
                        for part in PI_PARTS:
                            link(V.scalar_tensor_tensor(out, turns, -part, src, ALU.mult, ALU.add))
                            src = out
                    link(V.tensor_scalar(tt[5], tt[5], TWO_PI / 4, None, ALU.add))
                    link(V.tensor_scalar(tt[5], tt[5], 3.1415925, -3.1415925, ALU.min, ALU.max))
                    V.tensor_scalar(tt[3], tt[3], 3.1415925, -3.1415925, ALU.min, ALU.max).then_inc(tab_pre, 1)
                    dve.wait_ge(tab_act, ll + 1)
                    link(tt_(lamr[:, :, :].rearrange("p e g -> p (e g)"), tt[0], tt[5]))
                    link(tt_(lami[:, :, :].rearrange("p e g -> p (e g)"), tt[0], tt[3]))
                    sv = lambda i: ss[:, i, :]
                    cosy, siny = v3[5][:, 10, :], v3[3][:, 10, :]
                    link(V.tensor_scalar(sv(5), sv(3), -1.0, 1.0, ALU.mult, ALU.add))
                    link(V.reciprocal(sv(5), sv(5)))
                    link(V.scalar_tensor_tensor(sv(5), sv(5), 2.0, sv(3), ALU.mult, ALU.mult))
                    link(V.scalar_tensor_tensor(sv(6), sv(4), -2.0, sv(4), ALU.mult, ALU.mult))
                    link(tt_(sv(7), sv(5), cosy))
                    link(tt_(sv(6), sv(6), sv(7), ALU.add))
                    link(V.scalar_tensor_tensor(sv(7), sv(5), 1.0, siny, ALU.add, ALU.mult))
                    link(tt_(sv(8), t5[:, 0, :], t5[:, 0, :]))
                    link(tt_(sv(9), t5[:, 1, :], t5[:, 1, :]))
                    link(tt_(sv(8), sv(8), sv(9), ALU.add))
                    link(V.reciprocal(sv(8), sv(8)))
                    for o_, (a1, b1, a2, b2, op) in ((10, (6, 0, 7, 1, ALU.add)), (11, (7, 0, 6, 1, ALU.subtract))):
                        link(tt_(sv(12), sv(a1), t5[:, b1, :]))
                        link(tt_(sv(13), sv(a2), t5[:, b2, :]))
                        link(tt_(sv(12), sv(12), sv(13), op))
                        link(tt_(sv(o_), sv(12), sv(8)))
                    link(V.tensor_copy(lamR[:, :].rearrange("p (g x) -> p g x", g=G),
                                       lamr[:, 9, :].unsqueeze(2).to_broadcast([P, G, 2 * NS])))
                    lI = lamI[:, :].rearrange("p (g r s) -> p r g s", g=G, r=2)
                    li = lami[:, 9, :].unsqueeze(2).to_broadcast([P, G, NS])
                    V.tensor_scalar(lI[:, 0, :, :], li, -1.0, None, ALU.mult)
                    link(V.tensor_copy(lI[:, 1, :, :], li))
                    link(V.memset(h0[:, :], 0.0))
                    hv = h0[:, :].rearrange("p (g r s) -> p r g s", g=G, r=2)
                    link(V.tensor_copy(hv[:, 0, :, 1], t5[:, 3, :]))
                    V.tensor_copy(hv[:, 1, :, 1], t5[:, 4, :]).then_inc(tab_done, 1)
                elif k == "xn":
                    l, s = stg[1], stg[2]
                    dve.wait_ge(rstd_done, ls(l, s))
                    V.tensor_scalar(xn[:, s, :], x[:, s, :], st[:, 4 + s:5 + s], None, ALU.mult).then_inc(xn_done, 1)
                elif k == "hT":
                    s = stg[1]
                    key = ("hT", l, s, 1)
                    side.filled(dve, key)
                    dve.wait_ge(ada_done, l + 1)
                    for i in range(4):
                        d = 4 + i
                        m = V.tensor_scalar(hT[:, s, d, :], side.bank(key)[:, P * i:P * i + P],
                                            gsc[:, l, d, s:s + 1], ada[:, l, d, s:s + 1], ALU.mult, ALU.add)
                    m.then_inc(side.freed(key), 1)
                elif k == "unit" and stg[1] == "ca":
                    for s in range(NS):
                        key, ka = (l, "cg", s), (l, "ca", s)
                        proj.filled(dve, ka)
                        th_ready(dve, key)
                        V.scalar_tensor_tensor(y2[:, s, :], th_view(key), 1.0, proj.bank(ka)[:, :],
                                               ALU.add, ALU.mult).then_inc(proj.freed(ka), 1)
                elif k == "unit" and stg[1] == "kv":
                    if l:
                        dve.wait_ge(out_done, 64 * l)
                    for s in range(NS):
                        key = (l, "kv", s)
                        proj.filled(dve, key)
                        V.tensor_copy(qk[:, s, HEADS * HD:QK], proj.bank(key)[:, 0:P])
                        V.tensor_copy(v[:, s, :], proj.bank(key)[:, P:2 * P]).then_inc(proj.freed(key), 1)
                elif k == "unit" and stg[1] == "glua":
                    for s in range(NS):
                        key = (l, "glua", s)
                        proj.filled(dve, key)
                        th_ready(dve, (l, "glub", s))
                        V.scalar_tensor_tensor(qkt[:, 0:W], th_view((l, "glub", s)), 1.0, proj.bank(key)[:, :],
                                               ALU.add, ALU.mult).then_inc(proj.freed(key), 1)
                        proj.drained(dve, key)
                        proj.drained(dve, (l, "sg", s))
                        tt_(gates[:, 0, s, :], gates[:, 0, s, :], qkt[:, 0:W]).then_inc(prodB, 1)
                        dve.wait_ge(prodB, ls(l, s))
                elif k == "UT":
                    dve.wait_ge(zeroed, N_ZERO)
                    for h in range(2):
                        key = ("UT", l, h)
                        side.filled(dve, key)
                        dst = Uz[64:128, 16 * h:16 * h + 16, :].rearrange("p (g a) q -> p a g q", a=2)[:, 1, :, :]
                        V.tensor_copy(dst, side.bank(key)[64:128, :].rearrange("p (g q) -> p g q", g=8)
                                      ).then_inc(side.freed(key), 1)
                elif k == "S":
                    for i in range(8):
                        key = ("S", l, i)
                        side.filled(dve, key)
                        dst = H[64:128, 1:NCHUNK + 1, 16 * i:16 * i + 16][:, ::-1, :].rearrange("p k x -> p x k")
                        V.tensor_copy(dst, side.bank(key)[64:128, :].rearrange("p (x k) -> p x k", k=NCHUNK)
                                      ).then_inc(side.freed(key), 1)
                elif k == "scan":
                    _, c0, c1, tiles = stg
                    if c0 == 0:
                        for i in range(6, 8):
                            side.drained(dve, ("S", l, i))
                        dve.wait_ge(tab_done, l + 1)
                        V.tensor_copy(H[:, 0, :], h0[:, :]).then_inc(h0_done, 1)
                        dve.wait_ge(h0_done, l + 1)
                    taps_left = [(t, j) for t in tiles for j in range(TAPS)]
                    if tiles:
                        conv_ready(l)
                    for c in range(c0, c1):
                        for i in range(4):
                            scan_step(l, c, i)
                            if taps_left:
                                conv_tap(*taps_left.pop(0))
                    for t, j in taps_left:
                        conv_tap(t, j)
                    if c1 == NCHUNK:
                        dve.wait_ge(scan_done, l + 1)
                elif k == "qkn":
                    s = stg[1]
                    proj.drained(dve, (l, "q", s))
                    proj.drained(dve, (l, "kv", s))
                    dve.wait_ge(rows_in, 80 * (l + 1))
                    link(tt_(qkt[:, :], qk[:, s, :], qk[:, s, :]))
                    V.tensor_reduce(st[:, 16:26], qkt[:, :].rearrange("p (h d) -> p h d", d=HD), AX_X,
                                    ALU.add).then_inc(qk_sq, 1)
                    dve.wait_ge(qk_rs, ls(l, s))
                    q3 = qk[:, s, :].rearrange("p (h d) -> p h d", d=HD)
                    link(tt_(q3, q3, st[:, 48:58].unsqueeze(2).to_broadcast([P, HEADS + KV, HD])))
                    link(tt_(q3[:, 0:HEADS, :], q3[:, 0:HEADS, :], qkg[:, 0:1, :].to_broadcast([P, HEADS, HD])))
                    m = tt_(q3[:, HEADS:, :], q3[:, HEADS:, :], qkg[:, 1:2, :].to_broadcast([P, KV, HD]))
                    if s == 0:
                        m.then_inc(qk_done, 1)
                    else:
                        link(m)
                        dve.wait_ge(rope_in, 16)
                        link(tt_(qkt[:, :].rearrange("p (h d) -> p h d", d=HD), q3,
                                 rope[:, 0:1, :].to_broadcast([P, HEADS + KV, HD])))
                        r5 = prob[:, :, :].rearrange("p a b -> p (a b)")[:, 0:QK]
                        for a in range(2):
                            five = lambda t: t.rearrange("p (h f a c) -> p a h f c", f=2, a=2, c=16)
                            sin = rope[:, 1, :].rearrange("p (o f a c) -> p a o f c", o=1, f=2, a=2)[:, a]
                            link(tt_(five(r5)[:, a], five(qk[:, s, :])[:, 1 - a],
                                     sin.to_broadcast([P, HEADS + KV, 2, 16])))
                        tt_(qk[:, s, :], qkt[:, :], r5, ALU.add).then_inc(qk_done, 1)
                    dve.wait_ge(qk_done, ls(l, s))
                elif k == "qkT":
                    s = stg[1]
                    key = ("kT", l, s)
                    side.filled(dve, key)
                    dve.wait_ge(zeroed, N_ZERO)
                    V.tensor_copy(kz[s][64:128, 1, :], side.bank(key)[64:128, 0:P * (s + 1)]).then_inc(side.freed(key), 1)
                elif k == "conv":
                    conv_ready(l)
                    for j in range(TAPS):
                        for t in stg[1]:
                            conv_tap(t, j)
                elif k == "att":
                    s = stg[1]
                    nk = s + 1
                    for p in range(4 + 1):
                        if p < 4:
                            key = ("sc", l, s, p)
                            side.filled(dve, key)
                            link(V.tensor_reduce(st[:, 64 + 2 * p:66 + 2 * p],
                                                 side.bank(key)[:, 0:2 * nk * P].rearrange("p (a k) -> p a k", a=2),
                                                 AX_X, ALU.max))
                            V.tensor_scalar(nmx[:, s, p::4, 0], st[:, 64 + 2 * p:66 + 2 * p], -HD ** -0.5, None,
                                            ALU.mult).then_inc(nmax_done, 1)
                        if p >= 1:
                            key = ("pT", l, s, p - 1)
                            side.filled(dve, key)
                            if p - 1 >= 2:
                                dve.wait_ge(pv_read, 3 * (2 * l + s) + p - 2)
                            V.tensor_copy(probT[:, (p - 1) % 2, 0:2 * nk * P],
                                          side.bank(key)[:, 0:2 * nk * P]).then_inc(side.freed(key), 1)
                    key = ("pv", l, s)
                    long_.filled(dve, key)
                    link(V.reciprocal(st[:, 80:88], nmx[:, s, :, 1]))
                    tt_(qkt[:, 0:W].rearrange("p (h d) -> p h d", d=HD),
                        long_.bank(key)[:, :].rearrange("p (h d) -> p h d", d=HD),
                        st[:, 80:88].unsqueeze(2).to_broadcast([P, HEADS, HD])).then_inc(long_.freed(key), 1)
                    long_.drained(dve, key)
                    proj.drained(dve, (l, "ag", s))
                    tt_(gates[:, 2, s, :], gates[:, 2, s, :], qkt[:, 0:W]).then_inc(prodC, 1)
                    dve.wait_ge(prodC, ls(l, s))
                elif k == "Y":
                    dve.wait_ge(scan_done, l + 1)
                    for q in range(4):
                        if q >= 2:
                            side.filled(dve, ("Y", l, q - 2))
                        V.tensor_copy(HY[64:128, q % 2].rearrange("p g r s k -> p (g r s) k"),
                                      H[64:128, 0:NCHUNK, 32 * q:32 * q + 32][:, ::-1, :].rearrange("p k x -> p x k")
                                      ).then_inc(hy_bwd, 1)
                elif k == "gelu":
                    s = stg[1]
                    dve.wait_ge(y_in, 16 * 8 * (l + 1))
                    dve.wait_ge(rows_in, 80 * (l + 1))
                    proj.drained(dve, (l, "ssm", s))
                    link(tt_(utok[:, s, :], utok[:, s, :], rows[:, 0, :]))
                    tt_(ytok[:, s, :], ytok[:, s, :], utok[:, s, :], ALU.add).then_inc(gelu_pre, 1)
                elif k == "cback":
                    s = stg[1]
                    key = ("cback", l, s)
                    side.filled(dve, key)
                    link(V.bn_stats(st[:, 96:102], side.bank(key)[:, :]))
                    V.bn_aggr(st[:, 104:106], st[:, 96:102]).then_inc(ln_var, 1)
                    dve.wait_ge(ln_rs, ls(l, s))
                    t = qkt[:, 0:W]
                    V.tensor_scalar(t, side.bank(key)[:, :], st[:, 104:105], st[:, 112:113], ALU.subtract,
                                    ALU.mult).then_inc(side.freed(key), 1)
                    side.drained(dve, key)
                    link(tt_(t, t, rows[:, 1, :]))
                    tt_(t, t, rows[:, 2, :], ALU.add).then_inc(ln_pre, 1)
                    dve.wait_ge(ln_pre, ls(l, s))
                    th_ready(dve, (l, "ln", s))
                    proj.drained(dve, (l, "gg", s))
                    tt_(gates[:, 1, s, :], gates[:, 1, s, :], th_view((l, "ln", s))).then_inc(prodA, 1)
                    dve.wait_ge(prodA, ls(l, s))
                elif k == "comb":
                    b, h = stg[1], stg[2]
                    for s in range(NS):
                        km, kb = (l, "me" + b + str(h), s), (l, "br" + b + str(h), s)
                        proj.filled(dve, kb)
                        th_ready(dve, km)
                        acc = mixed[:, s, W * h:W * h + W]
                        dst = acc if b == BRANCHES[0] else qkt[:, 0:W]
                        V.scalar_tensor_tensor(dst, th_view(km), 1.0, proj.bank(kb)[:, :], ALU.add,
                                               ALU.mult).then_inc(proj.freed(kb), 1)
                        proj.drained(dve, kb)
                        if b != BRANCHES[0]:
                            m = tt_(acc, acc, dst, ALU.add)
                            if b == BRANCHES[-1]:
                                m.then_inc(mixed_done, 1)
                                dve.wait_ge(mixed_done, 4 * l + 2 * h + s + 1)
                            else:
                                link(m)
                elif k == "mixT":
                    s = stg[1]
                    key = ("mixT", l, s, 1)
                    side.filled(dve, key)
                    V.tensor_scalar(hT[:, s, 4:8, :].rearrange("p t q -> p (t q)"), side.bank(key)[:, :], 0.5, None,
                                    ALU.mult).then_inc(side.freed(key), 1)
                elif k == "wout":
                    h = stg[1]
                    for s in range(NS):
                        kg, kw = (l, "gate" + str(h), s), (l, "wo" + str(h), s)
                        proj.filled(dve, kw)
                        th_ready(dve, kg)
                        tt_(qkt[:, 0:W], proj.bank(kw)[:, :], th_view(kg)).then_inc(proj.freed(kw), 1)
                        proj.drained(dve, kw)
                        tt_(x[:, s, W * h:W * h + W], x[:, s, W * h:W * h + W], qkt[:, 0:W], ALU.add).then_inc(x_done, 1)
                        dve.wait_ge(x_done, 4 * l + 2 * h + s + 1)

        @block.gpsimd
        def _(pool):
            Q = nc.gpsimd
            n_chain = [0]

            def link(ins):
                n_chain[0] += 1
                ins.then_inc(pool_chain, 1)
                pool.wait_ge(pool_chain, n_chain[0])

            def tt_(out, a, b, op=ALU.mult):
                return Q.tensor_tensor(out, a, b, op)

            def rsqrt_mean(dst, src, n, count, tmp, done):
                link(Q.tensor_scalar(tmp, src, 1.0 / n, EPS, ALU.mult, ALU.add))
                tt_(dst, tmp, st[:, 128:128 + count], ALU.pow).then_inc(done, 1)

            Q.memset(Uz[:, :, :], 0.0).then_inc(zeroed, 1)
            Q.memset(cvpad[:, :, :, :], 0.0).then_inc(zeroed, 1)
            Q.memset(kz[0][:, :, :], 0.0).then_inc(zeroed, 1)
            Q.memset(kz[1][:, :, :], 0.0).then_inc(zeroed, 1)
            link(Q.memset(st[:, 128:140], -0.5))
            for l, stg in todo:
                k = stg[0]
                if k == "small":
                    ll = stg[1]
                    pool.wait_ge(small_in, 16 * N_SMALL * (ll + 1))
                    Q.tensor_copy(a32[0:G, 2, :].rearrange("g (d p) -> g d p", d=2),
                                  ldt[0:G, :].unsqueeze(2).to_broadcast([G, 2, SP])).then_inc(ldt_spread, 1)
                elif k == "preP":
                    ll, half = stg[1], stg[2]
                    if half == 0:
                        pool.wait_ge(tab_done, ll + 1)
                        pool.wait_ge(b_in, 64 * (ll + 1))
                        side.filled(pool, ("cT", ll, 1))
                        co = [ss[:, 10 + i, :].unsqueeze(2).to_broadcast([P, G, GC]) for i in range(2)]
                        t1, t2 = (tB[:, 512 * i:512 * i + 512].rearrange("p (g c) -> p g c", g=G) for i in range(2))
                        for r in range(2):
                            link(tt_(t1, co[0], braw[:, r, :, :]))
                            link(tt_(t2, co[1], braw[:, 1 - r, :, :]))
                            link(tt_(bbar[:, r, :, :], t1, t2, ALU.add if r else ALU.subtract))
                    else:
                        side.filled(pool, ("E", ll, 3))
                    g0 = 16 * half
                    lam = [t[:, L + 1:2 * L + 1, g0:g0 + 16].rearrange("p j g -> p g j").unsqueeze(3)
                           .to_broadcast([P, 16, L, GC]) for t in (lamr, lami)]
                    bb = [bbar[:, r, g0:g0 + 16, :].unsqueeze(2).to_broadcast([P, 16, L, GC]) for r in range(2)]
                    t1, t2 = (t[:, :].rearrange("p (g j c) -> p g j c", g=16, j=L) for t in (tA, tB))
                    for r in range(2):
                        link(tt_(t1, lam[0], bb[r]))
                        link(tt_(t2, lam[1], bb[1 - r]))
                        m = tt_(pre[:, r, :, :, :], t1, t2, ALU.add if r else ALU.subtract)
                        if r == 0:
                            link(m)
                        else:
                            m.then_inc(pre_done, 1)
                            pool.wait_ge(pre_done, 2 * ll + half + 1)
                elif k == "xn":
                    l, s = stg[1], stg[2]
                    pool.wait_ge(sq_done, ls(l, s))
                    rsqrt_mean(st[:, 4 + s:5 + s], st[:, s:s + 1], D, 1, st[:, 8 + s:9 + s], rstd_done)
                elif k == "qkn":
                    s = stg[1]
                    pool.wait_ge(qk_sq, ls(l, s))
                    rsqrt_mean(st[:, 48:58], st[:, 16:26], HD, HEADS + KV, st[:, 32:42], qk_rs)
                elif k == "cback":
                    s = stg[1]
                    pool.wait_ge(ln_var, ls(l, s))
                    rsqrt_mean(st[:, 112:113], st[:, 105:106], 1.0, 1, st[:, 114:115], ln_rs)
                elif k == "cp":
                    side.filled(pool, ("S", l, 7))
                    side.drained(pool, ("cT", l, 0))
                    side.drained(pool, ("cT", l, 1))
                    for i0, n in ((0, 2), (2, 2), (4, 1)):
                        t1, t2 = (t[:, 0:512 * n].rearrange("p (i g c) -> p i g c", i=n, g=G) for t in (tA, tB))
                        lam = [t[:, i0:i0 + n, :].unsqueeze(3).to_broadcast([P, n, G, GC]) for t in (lamr, lami)]
                        cc = [cT[:, r:r + 1, :, :].to_broadcast([P, n, G, GC]) for r in range(2)]
                        for r in range(2):
                            link(tt_(t1, cc[r], lam[0]))
                            link(tt_(t2, cc[1 - r], lam[1]))
                            m = tt_(CP[:, r, i0:i0 + n, :, :], t1, t2, ALU.subtract if r else ALU.add)
                            if i0 == 4 and r == 1:
                                m.then_inc(cp_done, 1)
                                pool.wait_ge(cp_done, l + 1)
                            else:
                                link(m)
                    link(Q.memset(bz[:, :, :, :], 0.0))
                elif k == "bz":
                    half = stg[1]
                    g0 = 16 * half
                    if half:
                        side.filled(pool, ("K", l, 3))
                    link(Q.tensor_copy(bz[0:64, :, :, 0:GC], bbar[0:64, :, g0:g0 + 16, :]))
                    link(Q.tensor_copy(bz[64:128, :, :, GC:2 * GC], bbar[64:128, :, g0:g0 + 16, :]))
                    Q.tensor_copy(bz[:, :, :, 2 * GC:3 * GC], bbar[:, :, g0:g0 + 16, :]).then_inc(bz_done, 1)


OUTPUTS = (("y_prompt", (1, P, D)), ("y_sample", (1, P, D)), ("new_cache_k", (1, DEPTH, P, KV, HD)),
           ("new_cache_v", (1, DEPTH, P, KV, HD)), ("new_state_ssm_re", (1, DEPTH, 2, G, SP)),
           ("new_state_ssm_im", (1, DEPTH, 2, G, SP)))


def shape_constants():
    import numpy as np

    first = [[0, 1, 2, 3, 4], [3, 2, 1, 0], [L, 1]]
    second = [[0, 4, 3, 2, 1], [0, 1, 2, 3], [L, 1]]
    expo = np.zeros((P, NEXP), np.float32)
    expo[0:SP] = sum(first, [])
    expo[SP:P] = sum(second, [])
    grid_w, pairs = 64, HD // 4
    t = np.arange(P)
    inv = (10000.0 ** (-np.arange(pairs, dtype=np.float32) / pairs)).astype(np.float32)
    ang = np.stack([(t // grid_w)[:, None] * inv, (t % grid_w)[:, None] * inv], 1).astype(np.float32)
    rope = np.zeros((P, 2, 2, 2, pairs), np.float32)
    rope[:, 0, :, 0] = rope[:, 0, :, 1] = np.cos(ang)
    rope[:, 1, :, 0] = -np.sin(ang)
    rope[:, 1, :, 1] = np.sin(ang)
    return {"ident": np.eye(P, dtype=np.float32), "expo": expo, "rope": rope.reshape(P, 2, HD)}


def kernel(**inputs):
    import numpy as np
    import concourse.bacc as bacc
    from concourse.bass_utils import run_bass_kernel_spmd

    nc = bacc.Bacc("TRN2", target_bir_lowering=False, num_devices=1)
    arrays = {}

    def given(prefix, named):
        aps = {}
        for name, a in named.items():
            a = np.ascontiguousarray(a)
            arrays[prefix + name] = a
            aps[name] = nc.dram_tensor(prefix + name, a.shape, mybir.dt.from_np(a.dtype), kind="ExternalInput").ap()
        return aps

    A = given("in_", inputs)
    C = given("const_", shape_constants())
    O = {name: nc.dram_tensor("out_" + name, shape, F32, kind="ExternalOutput").ap() for name, shape in OUTPUTS}
    build(nc, A, C, O)
    r = run_bass_kernel_spmd(nc, [arrays], core_ids=[0])
    return tuple(r.results[0]["out_" + name] for name, _ in OUTPUTS)
```

```python
from contextlib import ExitStack

import concourse.bass as bass
from concourse import mybir

F32 = mybir.dt.float32
F32R = mybir.dt.float32r
ALU = mybir.AluOpType
ACT = mybir.ActivationFunctionType
AX_X = mybir.AxisListType.X

P = 128
NS = 2
D = 1024
DT = D // P
DEPTH = 2
W = 512
WT = W // P
HEADS, KV, HD = 8, 2, 64
QK = (HEADS + KV) * HD
TAPS = 31
PAD = TAPS // 2
GC, G, SP = 16, 32, 64
L = 4
NCHUNK = P // L
GP = G // 2
ROW = G * 2 * NS
EPS = 1e-6
NEXP = 11
TWO_PI = 6.283185307179586
PI_PARTS = (6.28125, 0.0019350051879882812, 3.0199159819e-07)
MAGIC = 12582912.0

KT_SLAB = 2
RAW = 4

IN_UNITS = {"ssm": (1536, 512), "ca": (0, 512), "cg": (512, 512), "q": (2560, 512), "kv": (3072, 256),
            "sg": (2048, 512), "gg": (1024, 512), "ag": (3328, 512)}
MERGE0 = 3840
BRANCHES = ("B", "C", "A")
ADA_PARTS = 3
ADA_BANKS = D // W
MERGE_OF = {"A": 0, "B": 1, "C": 2}
EARLY = ("cg", "ssm", "ca")
CHUNK_ROOMS = 3
LAST_COMB = ("comb", BRANCHES[-1], 1)
OVER_EDGE = ("ada", DEPTH - 1, ADA_PARTS - 1)
IN_ATT = ("ada", DEPTH - 1, 0)


def order(l):
    def nxt(*stage):
        return [stage] if l + 1 < DEPTH else []

    def last(*stage):
        return [] if l + 1 < DEPTH else [stage]

    n = l + 1
    return ([("hT", 0), ("hT", 1), ("early", 0), ("early", 1), ("chunks", "cg")]
            + ([("adaEnd", l, 2)] if l else []) + [("unit", "cg")] + ([("adaT", l, 2)] if l else [])
            + ([("preE", 0, 0), ("preP", 0, 1)] if l == 0 else [])
            + [("unit", "ssm"), ("unit", "ca"), ("pack",)] + ([("preE", 0, 1)] if l == 0 else [])
            + [("bz", 0), ("UT",), ("S",), ("cp",), ("convT", 0), ("convT", 1), ("scan", 0, 16, ()),
               ("unit", "q"), ("unit", "kv"), ("scan", 16, NCHUNK, (0, 1)),
               ("unit", "sg"), ("K", 0), ("bz", 1), ("qkn", 0), ("qkn", 1)]
            + [("unit", "gg"), ("K", 1), ("unit", "ag"), ("Y",), ("qkT", 0), ("qkT", 1), ("att", 0)]
            + nxt("small", n) + nxt("tab", n) + nxt("ada", n, 0) + nxt("adaT", n, 0)
            + [("gelu", 0), ("gelu", 1)] + nxt("ada", n, 1) + [("geT", 0), ("geT", 1)] + nxt("adaT", n, 1)
            + last("split", 0) + last("split", 1) + [("att", 1), ("unit", "glub"), ("unit", "glua")]
            + (nxt("split", 0) + nxt("split", 1) + nxt("conv", 10, 21, None))
            + ([("ada", 0, 2)] if l == 0 else []) + nxt("cT", n) + ([("adaT", 0, 2)] if l == 0 else [])
            + nxt("preP", n, 0) + [("chunks", "meB0"), ("brT", "B", 0), ("brT", "B", 1)]
            + nxt("conv", 21, 26, "B0") + last("conv", 10, 17, "B0") + [("comb", "B", 0)]
            + [("brT", "C", 0), ("brT", "C", 1)] + nxt("conv", 26, TAPS, "B1") + last("conv", 17, 24, "B1")
            + [("comb", "B", 1)] + nxt("taps", n)
            + nxt("preE", n, 0) + nxt("preP", n, 1) + last("conv", 24, TAPS, "C0")
            + [("comb", "C", 0), ("cback", 0), ("cback", 1), ("comb", "C", 1)] + nxt("preE", n, 1)
            + [("brT", "A", 0), ("brT", "A", 1), ("comb", "A", 0), ("comb", "A", 1)]
            + [("wout", 0), ("wout", 1)] + nxt("xn", n, 0) + nxt("xn", n, 1) + nxt("ada", n, 2))



def stages():
    out = [(0, s) for s in (("cond",), ("small", 0), ("tab", 0), ("taps", 0), ("ada", 0, 0), ("xn", 0, 0), ("xn", 0, 1),
                            ("ada", 0, 1), ("adaT", 0, 0), ("adaT", 0, 1), ("cT", 0), ("preP", 0, 0))]
    for l in range(DEPTH):
        out += [(l, s) for s in order(l)]
    return out


def units_of(stage):
    if stage[0] == "unit":
        u = stage[1]
        if u in ("glua", "glub"):
            return [(u, WT, W)]
        return [(u, DT, IN_UNITS[u][1])]
    if stage[0] == "comb":
        return [("me" + stage[1] + str(stage[2]), DT, W), ("br" + stage[1] + str(stage[2]), WT, W)]
    if stage[0] == "wout":
        return [("wo" + str(stage[1]), DT, W)]
    return []


def split_unit(u):
    return u[:2] in ("me", "br", "wo") or u in EARLY


def side_uses(l, stage):
    k = stage[0]
    if k == "cond":
        return [(("cond",), 1)]
    if k == "small":
        return [(("small", stage[1]), 1)]
    if k == "taps":
        return [(("taps", stage[1]), 1)]
    if k == "cT":
        return [(("cT", stage[1], i), 1) for i in range(2)]
    if k == "adaT":
        return [(("adaT", stage[1], stage[2]), 1)]
    if k == "preE":
        return [(("E", stage[1], 4 * stage[2] + i), 1) for i in range(4)]
    if k == "hT":
        return [(("hT", l, stage[1], h), 1) for h in range(2)]
    if k == "UT":
        return [(("UT", l, h), 2) for h in range(2)]
    if k == "convT":
        return [(("convT", l, stage[1]), 1)]
    if k == "S":
        return [(("S", l, i), 2) for i in range(8)]
    if k == "qkT":
        return [(("qT", l, stage[1]), 1), (("kT", l, stage[1]), 2)]
    if k == "K":
        return [(("K", l, 4 * stage[1] + i), 1) for i in range(4)]
    if k == "att":
        s = stage[1]
        out = []
        for p in range(4 + 1):
            if p < 4:
                out.append((("sc", l, s, p), 1))
            if p >= 1:
                out.append((("pT", l, s, p - 1), 1))
        return out
    if k == "Y":
        return [(("Y", l, q), 1) for q in range(4)] + [(("fin", l), 1)]
    if k == "cback":
        return [(("cback", l, stage[1]), 1)]
    if k == "geT":
        return [(("geT", l, stage[1]), 1)]
    if k == "brT":
        return [(("brT", l, stage[1], stage[2]), 1)]
    if stage == LAST_COMB:
        return [(("mixT", l, s, 0), 1) for s in range(NS)]
    if k == "wout":
        merged = [(("mixT", l, s, 1), 1) for s in range(NS)] if stage[1] == 0 else []
        return merged + [(("gate", l, stage[1], s), 1) for s in range(NS)]
    return []


class Ring:

    def __init__(self, name, banks, uses, sem):
        self.banks, self.full, self.free = banks, sem(name + "_full"), [sem(f"{name}_free{b}") for b in range(len(banks))]
        self.at, total = {}, [0] * len(banks)
        for n, (key, drains) in enumerate(uses):
            b = n % len(banks)
            self.at[key] = (n, b, total[b], total[b] + drains)
            total[b] += drains

    def bank(self, key):
        return self.banks[self.at[key][1]]

    def claim(self, pe, key):
        n, b, before, _ = self.at[key]
        if before:
            pe.wait_ge(self.free[b], before)

    def filled(self, eng, key):
        eng.wait_ge(self.full, self.at[key][0] + 1)

    def freed(self, key):
        return self.free[self.at[key][1]]

    def drained(self, eng, key):
        eng.wait_ge(self.free[self.at[key][1]], self.at[key][3])


def build(nc, A, C, O):
    with ExitStack() as ctx:
        def sb(name, shape):
            return ctx.enter_context(nc.sbuf_tensor(name, shape, F32))

        def shared(name, shape):
            with nc.sbuf_tensor(name, shape, F32) as plain:
                pass
            words = 1
            for d in shape[1:]:
                words *= d
            return plain, ctx.enter_context(nc.sbuf_tensor(name + "_split", [P, words], F32R))

        sems = {}

        def sem(name):
            if name not in sems:
                sems[name] = ctx.enter_context(nc.semaphore(name))
            return sems[name]

        todo = stages()

        ident = sb("ident", [P, P])
        expo = sb("expo", [P, NEXP])
        rope = sb("rope", [P, 2, HD])
        x = sb("x", [P, NS, D])
        H, Hs = shared("H", [P, NCHUNK + 1, ROW])
        xn = H[:, :, :].rearrange("p a b -> p (a b)")[:, 0:NS * D].rearrange("p (s d) -> p s d", s=NS)
        mixed, mixeds = shared("mixed", [P, NS, D])
        y2 = mixed[:, :, 0:W]
        ytok = mixed[:, :, W:D]
        hT = sb("hT", [P, NS, DT, P])
        raw = sb("raw", [P, RAW, KT_SLAB * W])
        EC = sb("EC", [P, 2 * (L + 1) * W])
        E = EC[:, 0:2 * GP * P].rearrange("p (r g q) -> p r g q", r=2, g=GP)
        CP = EC[:, :].rearrange("p (r i g c) -> p r i g c", r=2, i=L + 1, g=G)
        qM, qMs = shared("qM", [P, 2, D])
        qT = qM[:, 0, :].rearrange("p (s a q) -> p s a q", s=NS, a=4)
        M = qM[:, 1, :].rearrange("p (j g c) -> p j g c", j=L, g=GP)
        pre = sb("pre", [P, 2, 16, L, GC])
        craw = pre[:, 0, :, :, :].rearrange("p g j c -> p (g j c)").rearrange("p (r t q) -> p r t q", r=2, t=4)
        tA = sb("tA", [P, 1024])
        tB = sb("tB", [P, 1024])
        braw = tA[:, :].rearrange("p (r g c) -> p r g c", r=2, g=G)
        bz = sb("bz", [P, 2, 16, 3 * GC])
        bbar = sb("bbar", [P, 2, G, GC])
        cT = sb("cT", [P, 2, G, GC])
        lamr = sb("lamr", [P, NEXP, G])
        lami = sb("lami", [P, NEXP, G])
        tt = [tB[:, 352 * i:352 * i + 352] for i in range(2)]
        bzf = bz[:, :, :, :].rearrange("p r g c -> p (r g c)")
        tt += [bzf[:, 352 * i:352 * i + 352] for i in range(4)]
        lamR = sb("lamR", [P, ROW])
        lamI = sb("lamI", [P, ROW])
        a32 = sb("a32", [P, 5, P])
        st32 = a32[:, 0:2, :]
        t5 = sb("t5", [P, 5, G])
        ss = sb("ss", [P, 16, G])
        wide, wides = shared("wide", [P, (L + 1) * W])
        KTs = wide[0:3 * GC, :].rearrange("p (i a b) -> p i a b", i=L + 1, a=2)
        U64 = wide[0:NS * NCHUNK, 0:L * W].rearrange("p (j c) -> p j c", j=L)
        Uz = sb("Uz", [P, G, NS * NCHUNK])
        HY, HYs = shared("HY", [P, 2, 8, 2, NS, NCHUNK])
        HYf = HY[:, :, :, :, :, :].rearrange("p a g r s k -> p a (g r s k)")
        Ug = HY[0:NS * NCHUNK].rearrange("p a g r s k -> p (a g r s k)")
        geT = HYf[:, 0, :].rearrange("p (s t q) -> p s t q", s=NS, t=WT)
        utok, utoks = shared("utok", [P, NS, W])
        cvpad = sb("cvpad", [P, WT, NS, P + 2 * PAD])
        cvacc = sb("cvacc", [P, WT, NS, P])
        taps = sb("taps", [P, WT, TAPS + 1])
        taprow = sb("taprow", [P, W])
        rows = sb("rows", [P, 3, W])
        modrow = rows[:, 0, 0:P]
        condrow = rows[:, 0, P:2 * P]
        cond = sb("cond", [P, NS, DT])
        h0 = sb("h0", [P, ROW])
        modc = sb("modc", [P, DEPTH, 4 * DT])
        ada = sb("ada", [P, DEPTH, 3 * DT, NS])
        gsc = sb("gsc", [P, DEPTH, DT, NS])
        gates, gatess = shared("gates", [P, 3, NS, W])
        GATE = {"sg": 0, "gg": 1, "ag": 2}
        th = sb("th", [P, 4, W])
        adarow = th[:, 2:4, :].rearrange("p a b -> p (a b)")
        qk = sb("qk", [P, NS, QK])
        qkt = sb("qkt", [P, QK])
        v = sb("v", [P, NS, KV * HD])
        ck = sb("ck", [P, KV * HD])
        cv = sb("cv", [P, KV * HD])

        def high_low(room, kts):
            n = NS * kts * P
            return [room[:, n * i:n * i + n].rearrange("p (s t q) -> p s t q", s=NS, t=kts) for i in range(2)]

        hTs = high_low(Hs, DT)
        brTs = {"C": high_low(qMs, WT), "B": high_low(HYs, WT), "A": high_low(qMs, WT)}
        mixTs = [high_low(HYs, WT), high_low(Hs, WT)]
        late_room = [wides[:, 0:2 * W], wides[:, 2 * W:4 * W], utoks[:, 0:2 * W]]
        early_room = [qMs[:, 0:2 * W], qMs[:, 2 * W:4 * W], gatess[:, 4 * W:6 * W]]
        hTe = [room[:, 0:2 * D].rearrange("p (s t q) -> p s t q", s=NS, t=DT) for room in (mixeds, gatess)]
        kz = [sb("kz0", [P, KV, P]), sb("kz1", [P, KV, 2 * P])]
        prob, probT = (pre[:, r, :, :, :].rearrange("p g j c -> p (g j c)").rearrange("p (b k) -> p b k", b=2)
                       for r in range(2))
        qkg = sb("qkg", [P, 2, HD])
        st = sb("st", [P, 144])
        nmx = sb("nmx", [P, NS, HEADS, 2])
        scan_t = qkt[:, 0:2 * ROW].rearrange("p (a b) -> p a b", a=2)
        ldt = sb("ldt", [P, 2])

        proj_banks = [ctx.enter_context(nc.psum_tensor(f"proj{i}", [P, W], F32)) for i in range(4)]
        side_banks = [ctx.enter_context(nc.psum_tensor(f"side{i}", [P, W], F32)) for i in range(3)]
        long_banks = [ctx.enter_context(nc.psum_tensor("long0", [P, W], F32))]

        proj_uses = []
        for l, stg in todo:
            if stg[0] == "ada":
                proj_uses += [(stg + (b,), 1) for b in range(ADA_BANKS)]
            proj_uses += [((l, u, s), 1) for u, _, _ in units_of(stg) for s in range(NS)]
        proj = Ring("proj", proj_banks, proj_uses, sem)
        side = Ring("side", side_banks, [use for l, stg in todo for use in side_uses(l, stg)], sem)
        long_ = Ring("long", long_banks, [(("pv", l, stg[1]), 1) for l, stg in todo if stg[0] == "att"], sem)

        slabs = []

        def w_src(l, u):
            if u in IN_UNITS:
                c0, n = IN_UNITS[u]
                return A["w_in"][l, :, c0:c0 + n]
            if u[:2] == "gl":
                c0 = 0 if u == "glua" else W
                return A["w_ssm_glu"][l, :, c0:c0 + W]
            if u[:2] == "wo":
                return A["w_out"][l, :, W * int(u[2]):W * int(u[2]) + W]
            h = int(u[3])
            if u[:2] == "me":
                c0 = MERGE0 + D * MERGE_OF[u[2]] + W * h
                return A["w_in"][l, :, c0:c0 + W]
            name = {"A": "w_conv_out", "B": "w_ssm_out", "C": "w_attn_out"}[u[2]]
            return A[name][l, :, W * h:W * h + W]

        for l, stg in todo:
            if stg[0] == "ada":
                src = A["w_ada"][stg[1]].rearrange("(k p) n -> p k n", p=P)
                for kt in range(DT):
                    slabs.append((stg + (kt,), 1, D, src[:, kt:kt + 1, D * stg[2]:D * stg[2] + D]))
            for u, nk, n in units_of(stg):
                src = w_src(l, u).rearrange("(k p) n -> p k n", p=P)
                for kp in range(nk // KT_SLAB):
                    slabs.append(((l, u, kp), KT_SLAB, n, src[:, KT_SLAB * kp:KT_SLAB * kp + KT_SLAB, :]))
        slab_at = {s[0]: n for n, s in enumerate(slabs)}
        slab_in = [sem(f"slab_in{r}") for r in range(RAW)]
        slab_used = sem("slab_used")
        chunks = [(l, u, kt) for l, stg in todo for u, nk, _ in units_of(stg) if split_unit(u) for kt in range(nk)]
        chunk_at = {key: m for m, key in enumerate(chunks)}
        chunk_hi = sem("chunk_hi")
        chunk_lo = sem("chunk_lo")
        chunk_used = sem("chunk_used")
        chunk_read, n_used = [], 0
        for l, u, kt in chunks:
            if (l, u, kt + 1) in chunk_at:
                n_used += 1
                chunk_read.append((chunk_used, n_used))
            else:
                chunk_read.append((proj.full, proj.at[(l, u, NS - 1)][0] + 1))

        def chunk_parts(m):
            room = (early_room if chunks[m][1] in EARLY else late_room)[m % CHUNK_ROOMS]
            return room[:, 0:W], room[:, W:2 * W]

        def chunk_raw(m):
            l, u, kt = chunks[m]
            return slab_view((l, u, kt // KT_SLAB))[:, kt % KT_SLAB, :]

        def ahead(l, u, beside=2):
            m = max(i for i, c in enumerate(chunks) if c[:2] == (l, u)) + 1
            room = 0 if m == len(chunks) or (chunks[m][1] in EARLY) != (u in EARLY) else beside
            return m + room

        slab_read, n_used = [], 0
        for key, _, _, _ in slabs:
            if key[0] != "ada" and split_unit(key[1]):
                slab_read.append((chunk_lo, chunk_at[(key[0], key[1], KT_SLAB * key[2] + KT_SLAB - 1)] + 1))
            elif key[:-1] + (key[-1] + 1,) not in {q[0] for q in slabs}:
                last = ADA_BANKS - 1 if key[0] == "ada" else NS - 1
                slab_read.append((proj.full, proj.at[key[:-1] + (last,)][0] + 1))
            else:
                n_used += 1
                slab_read.append((slab_used, n_used))

        def slab_view(key):
            n = slab_at[key]
            _, nk, cols, _ = slabs[n]
            return raw[:, n % RAW, 0:nk * cols].rearrange("p (k n) -> p k n", k=nk)

        def slab_landed(eng, key):
            n = slab_at[key]
            eng.wait_ge(slab_in[n % RAW], 16 * (n // RAW + 1))

        split_hi = sem("split_hi")
        split_lo = sem("split_lo")
        early_lo = sem("early_lo")
        consts_in = sem("consts_in")
        expo_in = sem("expo_in")
        rope_in = sem("rope_in")
        x_in = sem("x_in")
        N_SMALL = 7
        small_in = sem("small_in")
        c_in = sem("c_in")
        b_in = sem("b_in")
        rows_in = sem("rows_in")
        cache_in = sem("cache_in")
        zeroed = sem("zeroed")
        ldt_spread = sem("ldt_spread")
        sq_done = sem("sq_done")
        rstd_done = sem("rstd_done")
        xn_done = sem("xn_done")
        ada_done = sem("ada_done")
        cond_done = sem("cond_done")
        gelu_pre = sem("gelu_pre")
        ln_pre = sem("ln_pre")
        N_ZERO = 4
        tab_dt = sem("tab_dt")
        tab_pre = sem("tab_pre")
        tab_act = sem("tab_act")
        tab_done = sem("tab_done")
        pre_done = sem("pre_done")
        cp_done = sem("cp_done")
        bz_done = sem("bz_done")
        th_done = sem("th_done")
        u_in = sem("u_in")
        u_packed = sem("u_packed")
        y_in = sem("y_in")
        m_in = sem("m_in")
        conv_done = sem("conv_done")
        h0_done = sem("h0_done")
        scan_done = sem("scan_done")
        hy_fwd = sem("hy_fwd")
        hy_bwd = sem("hy_bwd")
        pv_read = sem("pv_read")
        gelu_done = sem("gelu_done")
        qk_sq = sem("qk_sq")
        qk_rs = sem("qk_rs")
        qk_done = sem("qk_done")
        nmax_done = sem("nmax_done")
        ln_var = sem("ln_var")
        ln_rs = sem("ln_rs")
        prodA = sem("prodA")
        prodB = sem("prodB")
        prodC = sem("prodC")
        prods = {"A": prodA, "B": prodB, "C": prodC}
        mixed_done = sem("mixed_done")
        x_done = sem("x_done")
        out_done = sem("out_done")
        OUTS = DEPTH * 4 + NS
        dve_chain = sem("dve_chain")
        act_chain = sem("act_chain")
        pool_chain = sem("pool_chain")

        def u_gate(l, h, s):
            return ("gate", l, h, s)

        def ls(l, s):
            return NS * l + s + 1

        th_list, n_th = [], 0
        for l, stg in todo:
            if stg == ("unit", "cg"):
                th_list += [((l, "cg", s), ("proj", (l, "cg", s)), ("proj", (l, "ca", s))) for s in range(NS)]
            elif stg == ("unit", "glub"):
                th_list += [((l, "glub", s), ("proj", (l, "glub", s)), ("proj", (l, "glua", s))) for s in range(NS)]
            elif stg[0] == "cback":
                n_th += 1
                th_list.append(((l, "ln", stg[1]), (th_done, n_th), (prodA, ls(l, stg[1]))))
            elif stg[0] == "comb":
                u = stg[1] + str(stg[2])
                th_list += [((l, "me" + u, s), ("proj", (l, "me" + u, s)), ("proj", (l, "br" + u, s)))
                            for s in range(NS)]
            elif stg[0] == "wout":
                th_list += [((l, "gate" + str(stg[1]), s), ("side", (u_gate(l, stg[1], s))),
                             ("proj", (l, "wo" + str(stg[1]), s))) for s in range(NS)]
        th_at = {k: n for n, (k, _, _) in enumerate(th_list)}
        ada_parts = [stg for _, stg in todo if stg[0] == "ada"]
        parts = []
        for l, stg in todo:
            if stg[0] in ("early", "split", "brT"):
                parts.append((l,) + stg)
            elif stg in (LAST_COMB, ("wout", 0)):
                parts += [(l, "mixT", s, int(stg != LAST_COMB)) for s in range(NS)]
        part_at = {key: n for n, key in enumerate(parts)}

        def th_wait(eng, what):
            if what[0] == "proj":
                proj.drained(eng, what[1])
            elif what[0] == "side":
                side.drained(eng, what[1])
            else:
                eng.wait_ge(*what)

        def th_view(key):
            return th[:, th_at[key] % 4, :]

        def th_claim(act, key):
            if th_at[key] >= 4:
                th_wait(act, th_list[th_at[key] - 4][2])

        def th_ready(dve, key):
            th_wait(dve, th_list[th_at[key]][1])

        def toeplitz(eng, l):
            for i in range(5, 8):
                side.drained(eng, ("K", l, i))
            Mf = M[:, :, :, :].rearrange("p t g c -> p t (g c)")
            for a in range(2):
                for s0 in range(L):
                    rows_ = slice(64 * a + GC * s0, 64 * a + GC * s0 + GC)
                    if s0 < L - 1:
                        eng.dma_start(Mf[rows_, s0 + 1:L, :], KTs[0:GC, 1:L - s0, a, :]).then_inc(m_in, 16)
                    if s0:
                        eng.dma_start(Mf[rows_, 0:s0, :], KTs[GC:2 * GC, L + 1 - s0:L + 1, a, :]).then_inc(m_in, 16)
                    eng.dma_start(Mf[rows_, s0, :], KTs[2 * GC:3 * GC, 0, a, :]).then_inc(m_in, 16)

        block = ctx.enter_context(nc.Block())

        @block.sync
        def _(sp):
            def small_loads(l):
                if l:
                    sp.wait_ge(out_done, 64 * l)
                    side.filled(sp, ("taps", l - 1))
                sp.dma_start(a32[0:G, 0, :].rearrange("g (d p) -> g d p", d=2),
                             A["ssm_a_re"][l].rearrange("d g p -> g d p")).then_inc(small_in, 16)
                sp.dma_start(a32[0:G, 1, :].rearrange("g (d p) -> g d p", d=2),
                             A["ssm_a_im"][l].rearrange("d g p -> g d p")).then_inc(small_in, 16)
                sp.dma_start(a32[0:G, 3, :].rearrange("g (d p) -> g d p", d=2),
                             A["state_ssm_re"][0, l].rearrange("d g p -> g d p")).then_inc(small_in, 16)
                sp.dma_start(a32[0:G, 4, :].rearrange("g (d p) -> g d p", d=2),
                             A["state_ssm_im"][0, l].rearrange("d g p -> g d p")).then_inc(small_in, 16)
                sp.dma_start(ldt[0:G, :], A["ssm_log_dt"][l].rearrange("d g -> g d"), allow_slow_non_contiguous=True).then_inc(small_in, 16)
                sp.dma_start(taprow[0:TAPS, :], A["conv_dw_w"][l]).then_inc(small_in, 16)
                sp.dma_start(taprow[TAPS:TAPS + 1, :], A["conv_dw_b"][l:l + 1, :]).then_inc(small_in, 16)

            def c_loads(l):
                for r, nm in enumerate(("ssm_c_re", "ssm_c_im")):
                    for d in range(2):
                        if l and r == 0 and d == 0:
                            side.filled(sp, ("pT", l - 1, 1, 3))
                        sp.dma_start(craw[:, r, :, SP * d:SP * d + SP],
                                     A[nm][l, d].rearrange("(t g) c p -> (g c) t p", t=4)).then_inc(c_in, 16)

            def b_loads(l):
                if l:
                    sp.wait_ge(bz_done, 2 * l)
                for r, nm in enumerate(("ssm_b_re", "ssm_b_im")):
                    for d in range(2):
                        sp.dma_start(braw[SP * d:SP * d + SP, r, :, :],
                                     A[nm][l, d].rearrange("g p c -> p g c")).then_inc(b_in, 16)

            def mid_loads(l):
                if l == 0:
                    side.filled(sp, ("cond",))
                if l:
                    sp.wait_ge(prodA, NS * l)
                    sp.wait_ge(gelu_done, NS * l)
                    sp.wait_ge(qk_done, NS * l)
                    sp.wait_ge(long_.full, long_.at[("pv", l - 1, 1)][0] + 1)
                for i, nm in enumerate(("ssm_d", "conv_ln_g", "conv_ln_b")):
                    sp.dma_start(rows[:, i, :], A[nm][l:l + 1, :].to_broadcast([P, W])).then_inc(rows_in, 16)
                sp.dma_start(qkg[:, 0, :], A["q_norm_g"][l:l + 1, :].to_broadcast([P, HD])).then_inc(rows_in, 16)
                sp.dma_start(qkg[:, 1, :], A["k_norm_g"][l:l + 1, :].to_broadcast([P, HD])).then_inc(rows_in, 16)
                sp.dma_start(ck[:, :], A["cache_k"][0, l].rearrange("t h d -> t (h d)")).then_inc(cache_in, 16)
                sp.dma_start(cv[:, :], A["cache_v"][0, l].rearrange("t h d -> t (h d)")).then_inc(cache_in, 16)

            def results(l):
                sp.wait_ge(qk_done, ls(l, 0))
                sp.dma_start(O["new_cache_k"][0, l].rearrange("t h d -> t (h d)"),
                             qk[:, 0, HEADS * HD:QK]).then_inc(out_done, 16)
                proj.drained(sp, (l, "kv", 0))
                sp.dma_start(O["new_cache_v"][0, l].rearrange("t h d -> t (h d)"), v[:, 0, :]).then_inc(out_done, 16)
                side.drained(sp, ("fin", l))
                for r, nm in enumerate(("new_state_ssm_re", "new_state_ssm_im")):
                    sp.dma_start(O[nm][0, l].rearrange("d g p -> g d p"),
                                 st32[0:G, r, :].rearrange("g (d p) -> g d p", d=2)).then_inc(out_done, 16)

            def pack_u(l):
                if l:
                    sp.wait_ge(y_in, 16 * 8 * l)
                for s in range(NS):
                    proj.drained(sp, (l, "ssm", s))
                    for j in range(L):
                        sp.dma_start(U64[NCHUNK * s:NCHUNK * s + NCHUNK, j, :],
                                     utok[j::L, s, :]).then_inc(u_in, 16)

            def unpack_y(l):
                for q in range(1, 4):
                    side.drained(sp, ("Y", l, q))
                for s in range(NS):
                    for j in range(L):
                        sp.dma_start(ytok[j::L, s, :], U64[NCHUNK * s:NCHUNK * s + NCHUNK, j, :]).then_inc(y_in, 16)

            def slab(n):
                key, nk, cols, src = slabs[n]
                if n >= RAW:
                    sp.wait_ge(*slab_read[n - RAW])
                sp.dma_start(slab_view(key), src).then_inc(slab_in[n % RAW], 16)

            sp.dma_start(ident[:, :], C["ident"]).then_inc(consts_in, 16)
            sp.dma_start(condrow[0:DT, :], A["c_ctx"].rearrange("(t p) -> t p", p=P)).then_inc(consts_in, 16)
            sp.dma_start(condrow[DT:2 * DT, :], A["c"][0].rearrange("(t p) -> t p", p=P)).then_inc(consts_in, 16)
            for l in range(DEPTH):
                sp.dma_start(modrow[32 * l:32 * l + 24, :],
                             A["b_ada"][l].rearrange("(t p) -> t p", p=P)).then_inc(consts_in, 16)
                sp.dma_start(modrow[32 * l + 24:32 * l + 32, :],
                             A["norm_g"][l].rearrange("(t p) -> t p", p=P)).then_inc(consts_in, 16)
            small_loads(0)
            sp.dma_start(expo[:, :], C["expo"]).then_inc(expo_in, 16)
            first = RAW
            for n in range(first):
                slab(n)
            sp.dma_start(x[:, 0, :], A["x_prompt"][0]).then_inc(x_in, 16)
            sp.dma_start(x[:, 1, :], A["x_sample"][0]).then_inc(x_in, 16)
            sp.dma_start(rope[:, :, :], C["rope"]).then_inc(rope_in, 16)
            n = 0
            for l, stg in todo:
                keys = [stg + (kt,) for kt in range(DT)] if stg[0] == "ada" else []
                keys += [(l, u, kp) for u, nk, _ in units_of(stg) for kp in range(nk // KT_SLAB)]
                if stg == ("unit", "q"):
                    mid_loads(l)
                for i, _ in enumerate(keys):
                    if stg == ("ada", l + 1, 0) and i == RAW:
                        results(l)
                        small_loads(l + 1)
                        unpack_y(l)
                        b_loads(l + 1)
                    if stg == ("ada", 0, 2) and i == RAW:
                        c_loads(1)
                    if n >= first:
                        slab(n)
                    n += 1
                if stg == ("ada", 0, 1):
                    c_loads(0)
                    b_loads(0)
                if stg == ("unit", "ca"):
                    pack_u(l)
                if stg == ("unit", "ag") and l == DEPTH - 1:
                    toeplitz(sp, l)
                if stg == ("unit", "glua") and l == DEPTH - 1:
                    unpack_y(l)
            results(DEPTH - 1)
            sp.wait_ge(x_done, 2 * NS * DEPTH - 1)
            sp.dma_start(O["y_prompt"][0], x[:, 0, :]).then_inc(out_done, 16)
            sp.wait_ge(x_done, 2 * NS * DEPTH)
            sp.dma_start(O["y_sample"][0], x[:, 1, :]).then_inc(out_done, 16)
            sp.wait_ge(out_done, 16 * OUTS)


        @block.tensor
        def _(pe):
            T = nc.tensor

            def ada_slab(stg, kt):
                if stg[1:] == (0, 0) and kt == 0:
                    pe.wait_ge(cond_done, 1)
                if kt == 0:
                    for b in range(ADA_BANKS):
                        proj.claim(pe, stg + (b,))
                slab_landed(pe, stg + (kt,))
                w = slab_view(stg + (kt,))
                for b in range(ADA_BANKS):
                    m = T.matmul(proj.bank(stg + (b,))[0:NS, :], cond[:, :, kt], w[:, 0, W * b:W * b + W],
                                 start=(kt == 0), stop=(kt == DT - 1))
                    if kt == DT - 1:
                        m.then_inc(proj.full, 1)
                if kt < DT - 1:
                    m.then_inc(slab_used, 1)

            def merged(l, h):
                pe.wait_ge(mixed_done, NS * (2 * l + h + 1))
                for s in range(NS):
                    key = ("mixT", l, s, h)
                    side.claim(pe, key)
                    for i in range(4):
                        d = 4 * h + i
                        m = transpose(side.bank(key)[:, P * i:P * i + P], mixed[:, s, P * d:P * d + P])
                    m.then_inc(side.full, 1)

            def plain_slab(l, u, kp, nk, n, lhs):
                slab_landed(pe, (l, u, kp))
                w = slab_view((l, u, kp))
                for s in range(NS):
                    for i in range(KT_SLAB):
                        kt = KT_SLAB * kp + i
                        last = kt == nk - 1
                        m = T.matmul(proj.bank((l, u, s))[:, 0:n], lhs[:, s, kt, :], w[:, i, :],
                                     start=(kt == 0), stop=last)
                    if last:
                        m.then_inc(proj.full, 1)
                if not last:
                    m.then_inc(slab_used, 1)

            def transpose(out, in_):
                k = in_.shape[0]
                return T.transpose(out, in_, ident[0:k, 0:k])

            for l, stg in todo:
                k = stg[0]
                if k == "cond":
                    pe.wait_ge(consts_in, 16 * 7)
                    side.claim(pe, ("cond",))
                    transpose(side.bank(("cond",))[:, 0:64], modrow[0:64, :])
                    transpose(side.bank(("cond",))[:, 64:80], condrow[0:2 * DT, :]).then_inc(side.full, 1)
                elif k == "small":
                    ll = stg[1]
                    key = ("small", ll)
                    pe.wait_ge(small_in, 16 * N_SMALL * (ll + 1))
                    pe.wait_ge(ldt_spread, ll + 1)
                    side.claim(pe, key)
                    for i in range(5):
                        m = transpose(side.bank(key)[:, G * i:G * i + G], a32[0:G, i, :])
                    m.then_inc(side.full, 1)
                elif k == "taps":
                    key = ("taps", stg[1])
                    side.claim(pe, key)
                    for t in range(WT):
                        m = transpose(side.bank(key)[:, 32 * t:32 * t + 32], taprow[0:32, P * t:P * t + P])
                    m.then_inc(side.full, 1)
                elif k == "cT":
                    ll = stg[1]
                    pe.wait_ge(c_in, 64 * (ll + 1))
                    for r in range(2):
                        key = ("cT", ll, r)
                        side.claim(pe, key)
                        for t in range(4):
                            m = transpose(side.bank(key)[:, P * t:P * t + P], craw[:, r, t, :])
                        m.then_inc(side.full, 1)
                elif k in ("ada", "adaEnd"):
                    kts = range(DT)
                    if k == "adaEnd" or stg == IN_ATT:
                        kts = kts[DT // 2:]
                    elif stg == OVER_EDGE:
                        kts = kts[:DT // 2]
                    for kt in kts:
                        ada_slab(("ada",) + stg[1:], kt)
                elif k == "adaT":
                    for b in range(ADA_BANKS):
                        proj.drained(pe, ("ada",) + stg[1:] + (b,))
                    side.claim(pe, stg)
                    for t in range(DT):
                        m = transpose(side.bank(stg)[:, NS * t:NS * t + NS], adarow[0:NS, P * t:P * t + P])
                    m.then_inc(side.full, 1)
                elif k == "preE":
                    ll, half = stg[1], stg[2]
                    pe.wait_ge(pre_done, 2 * ll + half + 1)
                    for r in range(2):
                        for q in range(2):
                            key = ("E", ll, 4 * half + 2 * r + q)
                            side.claim(pe, key)
                            for i in range(4):
                                g = 2 * (4 * q + i)
                                m = transpose(side.bank(key)[:, P * i:P * i + P],
                                              pre[:, r, g:g + 2, :, :].rearrange("p g j c -> p (g j c)"))
                            m.then_inc(side.full, 1)
                elif k == "hT":
                    s = stg[1]
                    pe.wait_ge(xn_done, ls(l, s))
                    for h in range(2):
                        key = ("hT", l, s, h)
                        side.claim(pe, key)
                        for i in range(4):
                            d = 4 * h + i
                            m = transpose(side.bank(key)[:, P * i:P * i + P], xn[:, s, P * d:P * d + P])
                        m.then_inc(side.full, 1)
                elif k == "UT":
                    pe.wait_ge(u_packed, l + 1)
                    for h in range(2):
                        key = ("UT", l, h)
                        side.claim(pe, key)
                        for i in range(8):
                            gp = 8 * h + i
                            m = transpose(side.bank(key)[:, 64 * i:64 * i + 64], Ug[:, P * gp:P * gp + P])
                        m.then_inc(side.full, 1)
                elif k == "convT":
                    s = stg[1]
                    proj.drained(pe, (l, "ca", s))
                    key = ("convT", l, s)
                    side.claim(pe, key)
                    for t in range(WT):
                        m = transpose(side.bank(key)[:, P * t:P * t + P], y2[:, s, P * t:P * t + P])
                    m.then_inc(side.full, 1)
                elif k == "S":
                    side.drained(pe, ("UT", l, 0))
                    side.drained(pe, ("UT", l, 1))
                    side.drained(pe, ("E", l, 5))
                    side.drained(pe, ("E", l, 6))
                    side.drained(pe, ("E", l, 7))
                    for i in range(8):
                        key = ("S", l, i)
                        side.claim(pe, key)
                        out = side.bank(key)[:, :].rearrange("p (g a r q) -> p g r a q", g=2, a=2, r=2)
                        for gg in range(2):
                            gp = 2 * i + gg
                            for r in range(2):
                                m = T.matmul(out[:, gg, r, :, :], E[:, r, gp, :], Uz[:, 2 * gp:2 * gp + 2, :],
                                             start=True, stop=True)
                        m.then_inc(side.full, 1)
                elif k == "K":
                    half = stg[1]
                    pe.wait_ge(cp_done, l + 1)
                    pe.wait_ge(bz_done, 2 * l + half + 1)
                    for i in range(4 * half, 4 * half + 4):
                        key = ("K", l, i)
                        side.claim(pe, key)
                        for b in range(4):
                            g = 4 * i + b
                            for r in range(2):
                                m = T.matmul(side.bank(key)[0:48, 80 * b:80 * b + 80], bz[:, r, g % 16, :],
                                             CP[:, r, :, g, :], start=(r == 0), stop=(r == 1))
                        m.then_inc(side.full, 1)
                elif k == "qkT":
                    s = stg[1]
                    pe.wait_ge(qk_done, ls(l, s))
                    key = ("qT", l, s)
                    side.claim(pe, key)
                    for p in range(4):
                        m = transpose(side.bank(key)[:, P * p:P * p + P], qk[:, s, P * p:P * p + P])
                    m.then_inc(side.full, 1)
                    key = ("kT", l, s)
                    side.claim(pe, key)
                    m = transpose(side.bank(key)[:, 0:P], qk[:, s, HEADS * HD:QK])
                    if s == 1:
                        pe.wait_ge(cache_in, 32 * (l + 1))
                        m = transpose(side.bank(key)[:, P:2 * P], ck[:, :])
                    m.then_inc(side.full, 1)
                elif k == "att":
                    s = stg[1]
                    nk = s + 1
                    side.drained(pe, ("qT", l, s))
                    side.drained(pe, ("kT", l, s))
                    proj.drained(pe, (l, "kv", s))
                    long_.claim(pe, ("pv", l, s))

                    def scores(p):
                        key = ("sc", l, s, p)
                        side.claim(pe, key)
                        T.matmul(side.bank(key)[:, 0:2 * nk * P], qT[:, s, p, :],
                                 kz[s][:, :, :].rearrange("p a k -> p (a k)"), start=True, stop=True).then_inc(side.full, 1)

                    def probs_t(p):
                        key = ("pT", l, s, p)
                        side.claim(pe, key)
                        side.drained(pe, ("sc", l, s, p))
                        for i in range(2 * nk):
                            m = transpose(side.bank(key)[:, P * i:P * i + P], prob[:, p % 2, P * i:P * i + P])
                        m.then_inc(side.full, 1)

                    def values(p):
                        side.drained(pe, ("pT", l, s, p))
                        for a in range(2):
                            h = p + 4 * a
                            for kt in range(nk):
                                vv = (v[:, s, :] if kt == 0 else cv[:, :])[:, HD * a:HD * a + HD]
                                m = T.matmul(long_.bank(("pv", l, s))[:, HD * h:HD * h + HD],
                                             probT[:, p % 2, P * (nk * a + kt):P * (nk * a + kt) + P], vv,
                                             start=(kt == 0), stop=(kt == nk - 1))
                        return m

                    for p in range(6):
                        if p < 4:
                            scores(p)
                        if 1 <= p < 5:
                            probs_t(p - 1)
                        if p >= 2:
                            m = values(p - 2)
                            m.then_inc(long_.full, 1) if p == 5 else m.then_inc(pv_read, 1)
                        if s == 0 and l + 1 < DEPTH and p < DT // 2:
                            ada_slab(IN_ATT, p)
                        if s == 1 and p < 2 * WT // KT_SLAB:
                            u, kp = (("glub", "glua")[p // 2], p % 2)
                            if p == 0:
                                for s_ in range(NS):
                                    side.drained(pe, ("geT", l, s_))
                            if kp == 0:
                                for s_ in range(NS):
                                    proj.claim(pe, (l, u, s_))
                            plain_slab(l, u, kp, WT, W, geT)
                elif k == "Y":
                    pe.wait_ge(m_in, 16 * 20 * (l + 1))
                    for q in range(4):
                        key = ("Y", l, q)
                        side.claim(pe, key)
                        pe.wait_ge(hy_fwd, 4 * l + q + 1)
                        pe.wait_ge(hy_bwd, 4 * l + q + 1)
                        for gi in range(8):
                            g = 8 * q + gi
                            o = side.bank(key)[0:64, 64 * gi:64 * gi + 64]
                            T.matmul(o, Uz[:, g, :], M[:, :, g // 2, :], start=True, stop=False)
                            for r in range(2):
                                m = T.matmul(o, HY[:, q % 2, gi, r, :, :].rearrange("p s k -> p (s k)"),
                                             CP[:, r, 1:L + 1, g, :], start=False, stop=(r == 1))
                        m.then_inc(side.full, 1)
                    key = ("fin", l)
                    side.claim(pe, key)
                    for r in range(2):
                        src = H[:, NCHUNK, :].rearrange("p (g r s) -> p r s g", g=G, r=2)[:, r, 0, :]
                        m = transpose(side.bank(key)[0:G, P * r:P * r + P], src)
                    m.then_inc(side.full, 1)
                elif k == "cback":
                    s = stg[1]
                    if s == 0:
                        pe.wait_ge(conv_done, WT * (l + 1))
                    key = ("cback", l, s)
                    side.claim(pe, key)
                    for t in range(WT):
                        m = transpose(side.bank(key)[:, P * t:P * t + P], cvacc[:, t, s, :])
                    m.then_inc(side.full, 1)
                elif k == "geT":
                    s = stg[1]
                    pe.wait_ge(gelu_done, ls(l, s))
                    key = ("geT", l, s)
                    side.claim(pe, key)
                    for t in range(WT):
                        m = transpose(side.bank(key)[:, P * t:P * t + P], ytok[:, s, P * t:P * t + P])
                    m.then_inc(side.full, 1)
                elif k == "brT":
                    b, s = stg[1], stg[2]
                    pe.wait_ge(prods[b], ls(l, s))
                    src = gates[:, {"A": 1, "B": 0, "C": 2}[b], s, :]
                    key = ("brT", l, b, s)
                    side.claim(pe, key)
                    for t in range(WT):
                        m = transpose(side.bank(key)[:, P * t:P * t + P], src[:, P * t:P * t + P])
                    m.then_inc(side.full, 1)
                if k in ("unit", "comb", "wout") and stg[1] not in ("glub", "glua"):
                    for u, nk, n in units_of(stg):
                        if u in EARLY:
                            if u == EARLY[0]:
                                pe.wait_ge(early_lo, ls(l, NS - 1))
                            lhs = hTe
                        elif u[:2] == "br":
                            for s in range(NS):
                                side.drained(pe, ("brT", l, u[2], s))
                            lhs = brTs[u[2]]
                        elif u[:2] == "me":
                            pe.wait_ge(split_lo, ls(l, NS - 1))
                            lhs = hTs
                        else:
                            lhs = hT
                        if stg == LAST_COMB and u[:2] == "br":
                            merged(l, 0)
                        for s in range(NS):
                            proj.claim(pe, (l, u, s))
                        if split_unit(u):
                            for kt in range(nk):
                                last = kt == nk - 1
                                m_ = chunk_at[(l, u, kt)]
                                if u == "wo0" and kt == WT - 1:
                                    merged(l, 1)
                                pe.wait_ge(chunk_lo, m_ + 1)
                                whi, wlo = chunk_parts(m_)
                                if u == "wo0" and kt % WT == 0:
                                    for s in range(NS):
                                        side.drained(pe, ("mixT", l, s, kt // WT))
                                for s in range(NS):
                                    bank = proj.bank((l, u, s))
                                    hi, lo = ((mixTs[kt // WT][i][:, s, kt % WT, :] for i in range(2)) if u[:2] == "wo"
                                              else (lhs[i][:, s, kt, :] for i in range(2)))
                                    T.matmul(bank[:, :], hi, whi, start=(kt == 0), stop=False)
                                    T.matmul(bank[:, :], hi, wlo, start=False, stop=False)
                                    m = T.matmul(bank[:, :], lo, whi, start=False, stop=last)
                                    if last:
                                        m.then_inc(proj.full, 1)
                                if not last:
                                    m.then_inc(chunk_used, 1)
                            continue
                        for kp in range(nk // KT_SLAB):
                            plain_slab(l, u, kp, nk, n, lhs)
                    if k == "wout":
                        h = stg[1]
                        side.drained(pe, ("adaT", l, 2))
                        for s in range(NS):
                            key = ("gate", l, h, s)
                            side.claim(pe, key)
                            for i in range(4):
                                col = ada[:, l, 2 * DT + 4 * h + i, s:s + 1]
                                m = T.matmul(side.bank(key)[:, P * i:P * i + P], col.to_broadcast([P, P]), ident[:, :],
                                             start=True, stop=True)
                            m.then_inc(side.full, 1)

        @block.scalar
        def _(act):
            S = nc.scalar
            n_chain = [0]

            def link(ins):
                n_chain[0] += 1
                ins.then_inc(act_chain, 1)
                act.wait_ge(act_chain, n_chain[0])

            def merged_high(l, h):
                for s in range(NS):
                    key = ("mixT", l, s, h)
                    side.filled(act, key)
                    S.activation(mixTs[h][0][:, s, :, :].rearrange("p t q -> p (t q)"), side.bank(key)[:, :],
                                 ACT.Copy, scale=0.5).then_inc(split_hi, 1)

            highs = [0]

            def high_parts(upto):
                for m in range(highs[0], upto):
                    l_, u, kt = chunks[m]
                    slab_landed(act, (l_, u, kt // KT_SLAB))
                    if u == "me" + BRANCHES[0] + "0" and kt == 0:
                        act.wait_ge(y_in, 16 * 8 * (l_ + 1))
                        act.wait_ge(gelu_pre, NS * (l_ + 1))
                    if m >= CHUNK_ROOMS:
                        act.wait_ge(*chunk_read[m - CHUNK_ROOMS])
                    S.activation(chunk_parts(m)[0], chunk_raw(m), ACT.Copy).then_inc(chunk_hi, 1)
                    highs[0] = m + 1

            for l, stg in todo:
                k = stg[0]
                if k == "cond":
                    side.filled(act, ("cond",))
                    S.activation(cond[:, :, :].rearrange("p s t -> p (s t)"), side.bank(("cond",))[:, 64:80],
                                 ACT.Silu).then_inc(cond_done, 1)
                elif k in ("ada", "adaEnd") and stg != OVER_EDGE:
                    stg = ("ada",) + stg[1:]
                    if ada_parts.index(stg):
                        side.filled(act, ("adaT",) + ada_parts[ada_parts.index(stg) - 1][1:])
                    for u in {("ada", 0, 2): ("glua",), OVER_EDGE: ("wo0", "wo1")}.get(stg, ()):
                        for s in range(NS):
                            proj.drained(act, (0, u, s))
                    for b in range(ADA_BANKS):
                        key = stg + (b,)
                        proj.filled(act, key)
                        S.activation(adarow[0:NS, W * b:W * b + W], proj.bank(key)[0:NS, :],
                                     ACT.Copy).then_inc(proj.freed(key), 1)
                elif k == "cT":
                    ll = stg[1]
                    if ll:
                        act.wait_ge(cp_done, ll)
                    for r in range(2):
                        key = ("cT", ll, r)
                        side.filled(act, key)
                        S.activation(cT[:, r, :, :].rearrange("p g c -> p (g c)"), side.bank(key)[:, :], ACT.Copy,
                                     scale=1.0 - 2.0 * r).then_inc(side.freed(key), 1)
                elif k == "tab":
                    ll = stg[1]
                    side.drained(act, ("small", ll))
                    S.activation(ss[:, 0, :], t5[:, 2, :], ACT.Exp).then_inc(tab_dt, 1)
                    act.wait_ge(tab_pre, ll + 1)
                    S.activation(tt[0], tt[0], ACT.Exp)
                    S.activation(ss[:, 3, :], ss[:, 1, :], ACT.Tanh, scale=0.5)
                    S.activation(ss[:, 4, :], tt[3][:, 10 * G:11 * G], ACT.Sin, scale=0.5)
                    link(S.activation(tt[5], tt[5], ACT.Sin))
                    S.activation(tt[3], tt[3], ACT.Sin).then_inc(tab_act, 1)
                elif k == "preE":
                    ll, half = stg[1], stg[2]
                    for r in range(2):
                        for q in range(2):
                            key = ("E", ll, 4 * half + 2 * r + q)
                            side.filled(act, key)
                            g0 = 8 * half + 4 * q
                            S.activation(E[:, r, g0:g0 + 4, :].rearrange("p g q -> p (g q)"), side.bank(key)[:, :],
                                         ACT.Copy).then_inc(side.freed(key), 1)
                elif k == "xn":
                    l, s = stg[1], stg[2]
                    if l == 0:
                        act.wait_ge(x_in, 32)
                    else:
                        act.wait_ge(x_done, 4 * l - 1 + s)
                        side.filled(act, ("fin", l - 1))
                        act.wait_ge(hy_fwd, 4 * l)
                        act.wait_ge(hy_bwd, 4 * l)
                    S.activation(xn[:, s, :], x[:, s, :], ACT.Square,
                                 accum_out=st[:, s:s + 1]).then_inc(sq_done, 1)
                elif k == "hT":
                    s = stg[1]
                    key = ("hT", l, s, 0)
                    side.filled(act, key)
                    act.wait_ge(ada_done, l + 1)
                    for i in range(4):
                        m = S.activation(hT[:, s, i, :], side.bank(key)[:, P * i:P * i + P], ACT.Identity,
                                         bias=ada[:, l, i, s:s + 1], scale=gsc[:, l, i, s:s + 1])
                    m.then_inc(side.freed(key), 1)
                elif k == "unit" and stg[1] == "ca":
                    high_parts(ahead(l, "ca"))
                elif k == "unit" and stg[1] == "kv":
                    if l:
                        act.wait_ge(out_done, 64 * l)
                    for s in range(NS):
                        key = (l, "kv", s)
                        proj.filled(act, key)
                        S.activation(qk[:, s, HEADS * HD:QK], proj.bank(key)[:, 0:P], ACT.Copy)
                        S.activation(v[:, s, :], proj.bank(key)[:, P:2 * P], ACT.Copy).then_inc(proj.freed(key), 1)
                elif k == "unit" and stg[1] in ("ssm", "q"):
                    if stg[1] == "ssm":
                        high_parts(ahead(l, "ssm"))
                        if l:
                            act.wait_ge(gelu_done, NS * l)
                    for s in range(NS):
                        key = (l, stg[1], s)
                        proj.filled(act, key)
                        dst, src = utok[:, s, :], proj.bank(key)[:, :]
                        if stg[1] == "q":
                            dst = qk[:, s, 0:W].rearrange("p (h a d) -> p a h d", h=4, a=2)
                            src = src.rearrange("p (a h d) -> p a h d", a=2, h=4)
                        S.activation(dst, src, ACT.Copy).then_inc(proj.freed(key), 1)
                elif k == "unit" and stg[1] in ("cg", "glub"):
                    if stg[1] == "cg":
                        high_parts(ahead(l, "cg"))
                        if l:
                            side.filled(act, ("adaT", l, 2))
                    if stg[1] == "glub" and l + 1 < DEPTH:
                        side.filled(act, ("adaT", l + 1, 1))
                    for s in range(NS):
                        key = (l, stg[1], s)
                        proj.filled(act, key)
                        th_claim(act, key)
                        S.activation(th_view(key), proj.bank(key)[:, :], ACT.Tanh, scale=0.5).then_inc(proj.freed(key), 1)
                elif k == "unit" and stg[1] in ("sg", "gg", "ag"):
                    for s in range(NS):
                        key = (l, stg[1], s)
                        proj.filled(act, key)
                        S.activation(gates[:, GATE[stg[1]], s, :], proj.bank(key)[:, :],
                                     ACT.Silu).then_inc(proj.freed(key), 1)
                elif k == "comb":
                    if stg == ("comb", BRANCHES[0], 0) and l == 0:
                        side.filled(act, ("adaT", 0, 2))
                    unit = stg[1] + str(stg[2])
                    high_parts(ahead(l, "me" + unit))
                    for s in range(NS):
                        key = (l, "me" + unit, s)
                        proj.filled(act, key)
                        th_claim(act, key)
                        S.activation(th_view(key), proj.bank(key)[:, :], ACT.Tanh, scale=0.5).then_inc(proj.freed(key), 1)
                    if stg == LAST_COMB:
                        merged_high(l, 0)
                    high_parts(ahead(l, "br" + unit, CHUNK_ROOMS))
                elif k == "chunks":
                    high_parts(chunk_at[(l, stg[1], 0)] + CHUNK_ROOMS)
                elif k == "early":
                    s = stg[1]
                    side.drained(act, ("hT", l, s, 0))
                    side.drained(act, ("hT", l, s, 1))
                    S.activation(hTe[0][:, s, :, :], hT[:, s, :, :], ACT.Copy).then_inc(split_hi, 1)
                elif k == "split":
                    s = stg[1]
                    if s == 0:
                        side.filled(act, ("fin", l))
                        act.wait_ge(hy_fwd, 4 * (l + 1))
                        act.wait_ge(hy_bwd, 4 * (l + 1))
                        for s_ in range(NS):
                            side.drained(act, ("hT", l, s_, 1))
                    S.activation(hTs[0][:, s, :, :], hT[:, s, :, :], ACT.Copy).then_inc(split_hi, 1)
                elif k == "pack":
                    act.wait_ge(u_in, 16 * 8 * (l + 1))
                    S.activation(Ug[:, :].rearrange("p (g j c) -> p g j c", g=G, j=L),
                                 U64.rearrange("p j (g c) -> p g j c", g=G), ACT.Copy).then_inc(u_packed, 1)
                elif k == "UT":
                    act.wait_ge(zeroed, N_ZERO)
                    for h in range(2):
                        key = ("UT", l, h)
                        side.filled(act, key)
                        dst = Uz[0:64, 16 * h:16 * h + 16, :].rearrange("p (g a) q -> p a g q", a=2)[:, 0, :, :]
                        S.activation(dst, side.bank(key)[0:64, :].rearrange("p (g q) -> p g q", g=8),
                                     ACT.Copy).then_inc(side.freed(key), 1)
                elif k == "convT":
                    s = stg[1]
                    key = ("convT", l, s)
                    side.filled(act, key)
                    act.wait_ge(zeroed, N_ZERO)
                    S.activation(cvpad[:, :, s, PAD:PAD + P], side.bank(key)[:, :].rearrange("p (t q) -> p t q", t=WT),
                                 ACT.Copy, scale=0.5).then_inc(side.freed(key), 1)
                elif k == "S":
                    for i in range(8):
                        key = ("S", l, i)
                        side.filled(act, key)
                        dst = H[0:64, 1:NCHUNK + 1, 16 * i:16 * i + 16].rearrange("p k x -> p x k")
                        S.activation(dst, side.bank(key)[0:64, :].rearrange("p (x k) -> p x k", k=NCHUNK),
                                     ACT.Copy).then_inc(side.freed(key), 1)
                elif k == "qkT":
                    s = stg[1]
                    key = ("qT", l, s)
                    side.filled(act, key)
                    S.activation(qT[:, s, :, :].rearrange("p a q -> p (a q)"), side.bank(key)[:, :],
                                 ACT.Copy).then_inc(side.freed(key), 1)
                    key = ("kT", l, s)
                    side.filled(act, key)
                    act.wait_ge(zeroed, N_ZERO)
                    S.activation(kz[s][0:64, 0, :], side.bank(key)[0:64, 0:P * (s + 1)],
                                 ACT.Copy).then_inc(side.freed(key), 1)
                elif k == "K":
                    for i in range(4 * stg[1], 4 * stg[1] + 4):
                        key = ("K", l, i)
                        side.filled(act, key)
                        src = side.bank(key)[0:48, 0:320].rearrange("p (g a i c) -> p a i g c", g=2, a=2, i=L + 1)
                        for a in range(2):
                            dst = KTs[:, :, a, 32 * i:32 * i + 32].rearrange("p i (g c) -> p i g c", g=2)
                            m = S.activation(dst, src[:, a, :, :, :], ACT.Copy)
                        m.then_inc(side.freed(key), 1)
                    if stg[1] == 1 and l < DEPTH - 1:
                        toeplitz(act, l)
                elif k == "att":
                    s = stg[1]
                    nk = s + 1
                    for p in range(4):
                        key = ("sc", l, s, p)
                        side.filled(act, key)
                        act.wait_ge(nmax_done, 4 * (2 * l + s) + p + 1)
                        if p >= 2:
                            side.filled(act, ("pT", l, s, p - 2))
                        for a in range(2):
                            h = p + 4 * a
                            m = S.activation(prob[:, p % 2, nk * P * a:nk * P * a + nk * P],
                                             side.bank(key)[:, nk * P * a:nk * P * a + nk * P], ACT.Exp,
                                             bias=nmx[:, s, h, 0:1], scale=HD ** -0.5, accum_out=nmx[:, s, h, 1:2])
                        m.then_inc(side.freed(key), 1)
                elif k == "Y":
                    act.wait_ge(scan_done, l + 1)
                    for q in range(4 + 1):
                        if q < 4:
                            if q >= 2:
                                side.filled(act, ("Y", l, q - 2))
                            S.activation(HY[0:64, q % 2].rearrange("p g r s k -> p (g r s) k"),
                                         H[0:64, 0:NCHUNK, 32 * q:32 * q + 32].rearrange("p k x -> p x k"),
                                         ACT.Copy).then_inc(hy_fwd, 1)
                        if q >= 1:
                            key = ("Y", l, q - 1)
                            side.filled(act, key)
                            dst = U64.rearrange("p j (g c) -> p g j c", g=G)[:, 8 * (q - 1):8 * q, :, :]
                            S.activation(dst, side.bank(key)[0:64, :].rearrange("p (g j c) -> p g j c", g=8, j=L),
                                         ACT.Copy).then_inc(side.freed(key), 1)
                    key = ("fin", l)
                    side.filled(act, key)
                    S.activation(st32[0:G, :, :].rearrange("p r q -> p (r q)"), side.bank(key)[0:G, 0:2 * P],
                                 ACT.Copy).then_inc(side.freed(key), 1)
                elif k == "gelu":
                    s = stg[1]
                    act.wait_ge(gelu_pre, ls(l, s))
                    S.activation(ytok[:, s, :], ytok[:, s, :], ACT.Gelu_apprx_tanh).then_inc(gelu_done, 1)
                elif k == "cback":
                    key = (l, "ln", stg[1])
                    high_parts(chunk_at[(l, "meC1", 0)] + (12 if stg[1] else 7))
                    act.wait_ge(ln_pre, ls(l, stg[1]))
                    th_claim(act, key)
                    S.activation(th_view(key), qkt[:, 0:W], ACT.Silu).then_inc(th_done, 1)
                elif k == "geT":
                    s = stg[1]
                    key = ("geT", l, s)
                    side.filled(act, key)
                    S.activation(geT[:, s, :, :].rearrange("p t q -> p (t q)"), side.bank(key)[:, :],
                                 ACT.Copy).then_inc(side.freed(key), 1)
                elif k == "brT":
                    b, s = stg[1], stg[2]
                    key = ("brT", l, b, s)
                    side.filled(act, key)
                    S.activation(brTs[b][0][:, s, :, :].rearrange("p t q -> p (t q)"), side.bank(key)[:, :], ACT.Copy,
                                 scale=0.5 if b == "B" else 1.0).then_inc(split_hi, 1)
                elif k == "wout":
                    h = stg[1]
                    if h == 0:
                        high_parts(chunk_at[(l, "wo0", 0)] + WT + 1)
                        merged_high(l, 1)
                    high_parts(ahead(l, "wo" + str(h)))
                    for s in range(NS):
                        key, gk = (l, "gate" + str(h), s), ("gate", l, h, s)
                        side.filled(act, gk)
                        th_claim(act, key)
                        S.activation(th_view(key), side.bank(gk)[:, :], ACT.Copy).then_inc(side.freed(gk), 1)

        @block.vector
        def _(dve):
            V = nc.vector
            n_chain = [0]
            lows = [0]

            def link(ins):
                n_chain[0] += 1
                ins.then_inc(dve_chain, 1)
                dve.wait_ge(dve_chain, n_chain[0])

            def tt_(out, a, b, op=ALU.mult):
                return V.tensor_tensor(out, a, b, op)


            def low_parts(upto):
                for m in range(lows[0], upto):
                    hi, lo = chunk_parts(m)
                    dve.wait_ge(chunk_hi, m + 1)
                    tt_(lo, chunk_raw(m), hi.bitcast(F32), ALU.subtract).then_inc(chunk_lo, 1)
                    lows[0] = m + 1

            def merged_low(l, h):
                for s in range(NS):
                    key = ("mixT", l, s, h)
                    dve.wait_ge(split_hi, part_at[(l, "mixT", s, h)] + 1)
                    flat = lambda i: mixTs[h][i][:, s, :, :].rearrange("p t q -> p (t q)")
                    V.scalar_tensor_tensor(flat(1), side.bank(key)[:, :], 0.5, flat(0).bitcast(F32),
                                           ALU.mult, ALU.subtract).then_inc(side.freed(key), 1)

            made = {}

            def needs(*operands):
                at = max([made.get(o, 0) for o in operands])
                if at:
                    dve.wait_ge(dve_chain, at)

            def makes(operand, ins):
                n_chain[0] += 1
                ins.then_inc(dve_chain, 1)
                made[operand] = n_chain[0]

            def scan_step(l, c, i):
                four = lambda t: t.rearrange("p (g r s) -> p g r s", g=G, r=2)
                h, h1 = H[:, c, :], H[:, c + 1, :]
                if i == 0:
                    needs("h")
                    makes("cross", tt_(four(scan_t[:, 0, :]), four(h)[:, :, ::-1, :], four(lamI[:, :])))
                elif i == 1:
                    makes("straight", tt_(scan_t[:, 1, :], h, lamR[:, :]))
                elif i == 2:
                    needs("cross")
                    makes("h", tt_(h1, h1, scan_t[:, 0, :], ALU.add))
                else:
                    needs("h", "straight")
                    m = tt_(h1, h1, scan_t[:, 1, :], ALU.add)
                    if c < NCHUNK - 1:
                        makes("h", m)
                    else:
                        m.then_inc(scan_done, 1)

            def conv_ready(l):
                for s in range(NS):
                    side.drained(dve, ("convT", l, s))
                side.drained(dve, ("taps", l))

            def conv_tap(t, j):
                acc, src = cvacc[:, t, :, :], cvpad[:, t, :, j:j + P]
                if j == 0:
                    m = V.tensor_scalar(acc, src, taps[:, t, 0:1], taps[:, t, TAPS:TAPS + 1], ALU.mult, ALU.add)
                else:
                    needs(("sum", t))
                    m = V.scalar_tensor_tensor(acc, src, taps[:, t, j:j + 1], acc, ALU.mult, ALU.add)
                if j < TAPS - 1:
                    makes(("sum", t), m)
                else:
                    m.then_inc(conv_done, 1)

            for l, stg in todo:
                k = stg[0]
                if k == "cond":
                    key = ("cond",)
                    side.filled(dve, key)
                    dve.wait_ge(cond_done, 1)
                    V.tensor_copy(modc[:, :, :].rearrange("p l t -> p (l t)"),
                                  side.bank(key)[:, 0:64]).then_inc(side.freed(key), 1)
                elif k == "small":
                    ll = stg[1]
                    key = ("small", ll)
                    side.filled(dve, key)
                    V.tensor_copy(t5[:, :, :].rearrange("p i g -> p (i g)"),
                                  side.bank(key)[:, 0:5 * G]).then_inc(side.freed(key), 1)
                elif k == "taps":
                    ll = stg[1]
                    key = ("taps", ll)
                    side.filled(dve, key)
                    if ll:
                        dve.wait_ge(conv_done, WT * ll)
                    V.tensor_copy(taps[:, :, :].rearrange("p t j -> p (t j)"),
                                  side.bank(key)[:, 0:WT * 32]).then_inc(side.freed(key), 1)
                elif k == "adaT":
                    ll, c = stg[1], stg[2]
                    side.filled(dve, stg)
                    side.drained(dve, ("cond",))
                    part = slice(DT * c, DT * c + DT)
                    tt_(ada[:, ll, part, :], side.bank(stg)[:, 0:NS * DT].rearrange("p (t s) -> p t s", s=NS),
                        modc[:, ll, part].unsqueeze(2).to_broadcast([P, DT, NS]), ALU.add).then_inc(side.freed(stg), 1)
                    if c == 1:
                        side.drained(dve, stg)
                        V.scalar_tensor_tensor(gsc[:, ll, :, :], ada[:, ll, part, :], 1.0,
                                               modc[:, ll, 24:32].unsqueeze(2).to_broadcast([P, DT, NS]),
                                               ALU.add, ALU.mult).then_inc(ada_done, 1)
                elif k == "tab":
                    ll = stg[1]
                    if ll:
                        dve.wait_ge(cp_done, ll)
                        side.filled(dve, ("K", ll - 1, 7))
                        side.filled(dve, ("E", ll - 1, 7))
                    side.drained(dve, ("small", ll))
                    dve.wait_ge(expo_in, 16)
                    dve.wait_ge(tab_dt, ll + 1)
                    tt_(ss[:, 1, :], t5[:, 0, :], ss[:, 0, :])
                    link(tt_(ss[:, 2, :], t5[:, 1, :], ss[:, 0, :]))
                    ex = expo[:, :].unsqueeze(2).to_broadcast([P, NEXP, G])
                    v3 = [t.rearrange("p (e g) -> p e g", e=NEXP) for t in tt]
                    tt_(v3[0], ss[:, 1:2, :].to_broadcast([P, NEXP, G]), ex)
                    link(tt_(v3[1], ss[:, 2:3, :].to_broadcast([P, NEXP, G]), ex))
                    link(V.tensor_scalar(tt[2], tt[1], 1.0 / TWO_PI, None, ALU.mult))
                    link(V.tensor_scalar(tt[4], tt[2], 0.25, None, ALU.add))
                    link(V.tensor_scalar(tt[2], tt[2], MAGIC, None, ALU.add))
                    link(V.tensor_scalar(tt[2], tt[2], MAGIC, None, ALU.subtract))
                    link(V.tensor_scalar(tt[4], tt[4], MAGIC, None, ALU.add))
                    link(V.tensor_scalar(tt[4], tt[4], MAGIC, None, ALU.subtract))
                    for turns, out in ((tt[2], tt[3]), (tt[4], tt[5])):
                        src = tt[1]
                        for part in PI_PARTS:
                            link(V.scalar_tensor_tensor(out, turns, -part, src, ALU.mult, ALU.add))
                            src = out
                    link(V.tensor_scalar(tt[5], tt[5], TWO_PI / 4, None, ALU.add))
                    link(V.tensor_scalar(tt[5], tt[5], 3.1415925, -3.1415925, ALU.min, ALU.max))
                    V.tensor_scalar(tt[3], tt[3], 3.1415925, -3.1415925, ALU.min, ALU.max).then_inc(tab_pre, 1)
                    dve.wait_ge(tab_act, ll + 1)
                    link(tt_(lamr[:, :, :].rearrange("p e g -> p (e g)"), tt[0], tt[5]))
                    link(tt_(lami[:, :, :].rearrange("p e g -> p (e g)"), tt[0], tt[3]))
                    sv = lambda i: ss[:, i, :]
                    cosy, siny = v3[5][:, 10, :], v3[3][:, 10, :]
                    link(V.tensor_scalar(sv(5), sv(3), -1.0, 1.0, ALU.mult, ALU.add))
                    link(V.reciprocal(sv(5), sv(5)))
                    link(V.scalar_tensor_tensor(sv(5), sv(5), 2.0, sv(3), ALU.mult, ALU.mult))
                    link(V.scalar_tensor_tensor(sv(6), sv(4), -2.0, sv(4), ALU.mult, ALU.mult))
                    link(tt_(sv(7), sv(5), cosy))
                    link(tt_(sv(6), sv(6), sv(7), ALU.add))
                    link(V.scalar_tensor_tensor(sv(7), sv(5), 1.0, siny, ALU.add, ALU.mult))
                    link(tt_(sv(8), t5[:, 0, :], t5[:, 0, :]))
                    link(tt_(sv(9), t5[:, 1, :], t5[:, 1, :]))
                    link(tt_(sv(8), sv(8), sv(9), ALU.add))
                    link(V.reciprocal(sv(8), sv(8)))
                    for o_, (a1, b1, a2, b2, op) in ((10, (6, 0, 7, 1, ALU.add)), (11, (7, 0, 6, 1, ALU.subtract))):
                        link(tt_(sv(12), sv(a1), t5[:, b1, :]))
                        link(tt_(sv(13), sv(a2), t5[:, b2, :]))
                        link(tt_(sv(12), sv(12), sv(13), op))
                        link(tt_(sv(o_), sv(12), sv(8)))
                    link(V.tensor_copy(lamR[:, :].rearrange("p (g x) -> p g x", g=G),
                                       lamr[:, 9, :].unsqueeze(2).to_broadcast([P, G, 2 * NS])))
                    lI = lamI[:, :].rearrange("p (g r s) -> p r g s", g=G, r=2)
                    li = lami[:, 9, :].unsqueeze(2).to_broadcast([P, G, NS])
                    V.tensor_scalar(lI[:, 0, :, :], li, -1.0, None, ALU.mult)
                    link(V.tensor_copy(lI[:, 1, :, :], li))
                    link(V.memset(h0[:, :], 0.0))
                    hv = h0[:, :].rearrange("p (g r s) -> p r g s", g=G, r=2)
                    link(V.tensor_copy(hv[:, 0, :, 1], t5[:, 3, :]))
                    V.tensor_copy(hv[:, 1, :, 1], t5[:, 4, :]).then_inc(tab_done, 1)
                elif k == "xn":
                    l, s = stg[1], stg[2]
                    dve.wait_ge(rstd_done, ls(l, s))
                    V.tensor_scalar(xn[:, s, :], x[:, s, :], st[:, 4 + s:5 + s], None, ALU.mult).then_inc(xn_done, 1)
                elif k == "hT":
                    s = stg[1]
                    key = ("hT", l, s, 1)
                    side.filled(dve, key)
                    dve.wait_ge(ada_done, l + 1)
                    for i in range(4):
                        d = 4 + i
                        m = V.tensor_scalar(hT[:, s, d, :], side.bank(key)[:, P * i:P * i + P],
                                            gsc[:, l, d, s:s + 1], ada[:, l, d, s:s + 1], ALU.mult, ALU.add)
                    m.then_inc(side.freed(key), 1)
                elif k == "unit" and stg[1] == "ca":
                    low_parts(ahead(l, "ca"))
                    for s in range(NS):
                        key, ka = (l, "cg", s), (l, "ca", s)
                        proj.filled(dve, ka)
                        th_ready(dve, key)
                        V.scalar_tensor_tensor(y2[:, s, :], th_view(key), 1.0, proj.bank(ka)[:, :],
                                               ALU.add, ALU.mult).then_inc(proj.freed(ka), 1)
                elif k == "unit" and stg[1] in ("cg", "ssm"):
                    low_parts(ahead(l, stg[1]))
                elif k == "unit" and stg[1] == "glua":
                    for s in range(NS):
                        key = (l, "glua", s)
                        proj.filled(dve, key)
                        th_ready(dve, (l, "glub", s))
                        V.scalar_tensor_tensor(qkt[:, 0:W], th_view((l, "glub", s)), 1.0, proj.bank(key)[:, :],
                                               ALU.add, ALU.mult).then_inc(proj.freed(key), 1)
                        proj.drained(dve, key)
                        proj.drained(dve, (l, "sg", s))
                        tt_(gates[:, 0, s, :], gates[:, 0, s, :], qkt[:, 0:W]).then_inc(prodB, 1)
                        dve.wait_ge(prodB, ls(l, s))
                elif k == "UT":
                    dve.wait_ge(zeroed, N_ZERO)
                    for h in range(2):
                        key = ("UT", l, h)
                        side.filled(dve, key)
                        dst = Uz[64:128, 16 * h:16 * h + 16, :].rearrange("p (g a) q -> p a g q", a=2)[:, 1, :, :]
                        V.tensor_copy(dst, side.bank(key)[64:128, :].rearrange("p (g q) -> p g q", g=8)
                                      ).then_inc(side.freed(key), 1)
                elif k == "S":
                    for i in range(8):
                        key = ("S", l, i)
                        side.filled(dve, key)
                        dst = H[64:128, 1:NCHUNK + 1, 16 * i:16 * i + 16][:, ::-1, :].rearrange("p k x -> p x k")
                        V.tensor_copy(dst, side.bank(key)[64:128, :].rearrange("p (x k) -> p x k", k=NCHUNK)
                                      ).then_inc(side.freed(key), 1)
                elif k == "scan":
                    _, c0, c1, tiles = stg
                    if c0 == 0:
                        for i in range(6, 8):
                            side.drained(dve, ("S", l, i))
                        dve.wait_ge(tab_done, l + 1)
                        V.tensor_copy(H[:, 0, :], h0[:, :]).then_inc(h0_done, 1)
                        dve.wait_ge(h0_done, l + 1)
                    taps_left = [(t, j) for t in tiles for j in range(TAPS)]
                    if tiles:
                        conv_ready(l)
                    for c in range(c0, c1):
                        for i in range(4):
                            scan_step(l, c, i)
                            if taps_left:
                                conv_tap(*taps_left.pop(0))
                    for t, j in taps_left:
                        conv_tap(t, j)
                    if c1 == NCHUNK:
                        dve.wait_ge(scan_done, l + 1)
                elif k == "qkn":
                    s = stg[1]
                    proj.drained(dve, (l, "q", s))
                    proj.drained(dve, (l, "kv", s))
                    dve.wait_ge(rows_in, 80 * (l + 1))
                    link(tt_(qkt[:, :], qk[:, s, :], qk[:, s, :]))
                    V.tensor_reduce(st[:, 16:26], qkt[:, :].rearrange("p (h d) -> p h d", d=HD), AX_X,
                                    ALU.add).then_inc(qk_sq, 1)
                    dve.wait_ge(qk_rs, ls(l, s))
                    q3 = qk[:, s, :].rearrange("p (h d) -> p h d", d=HD)
                    link(tt_(q3, q3, st[:, 48:58].unsqueeze(2).to_broadcast([P, HEADS + KV, HD])))
                    link(tt_(q3[:, 0:HEADS, :], q3[:, 0:HEADS, :], qkg[:, 0:1, :].to_broadcast([P, HEADS, HD])))
                    m = tt_(q3[:, HEADS:, :], q3[:, HEADS:, :], qkg[:, 1:2, :].to_broadcast([P, KV, HD]))
                    if s == 0:
                        m.then_inc(qk_done, 1)
                    else:
                        link(m)
                        dve.wait_ge(rope_in, 16)
                        link(tt_(qkt[:, :].rearrange("p (h d) -> p h d", d=HD), q3,
                                 rope[:, 0:1, :].to_broadcast([P, HEADS + KV, HD])))
                        r5 = prob[:, :, :].rearrange("p a b -> p (a b)")[:, 0:QK]
                        for a in range(2):
                            five = lambda t: t.rearrange("p (h f a c) -> p a h f c", f=2, a=2, c=16)
                            sin = rope[:, 1, :].rearrange("p (o f a c) -> p a o f c", o=1, f=2, a=2)[:, a]
                            link(tt_(five(r5)[:, a], five(qk[:, s, :])[:, 1 - a],
                                     sin.to_broadcast([P, HEADS + KV, 2, 16])))
                        tt_(qk[:, s, :], qkt[:, :], r5, ALU.add).then_inc(qk_done, 1)
                    dve.wait_ge(qk_done, ls(l, s))
                elif k == "qkT":
                    s = stg[1]
                    key = ("kT", l, s)
                    side.filled(dve, key)
                    dve.wait_ge(zeroed, N_ZERO)
                    V.tensor_copy(kz[s][64:128, 1, :], side.bank(key)[64:128, 0:P * (s + 1)]).then_inc(side.freed(key), 1)
                elif k == "conv":
                    end = 0 if stg[3] is None else chunk_at[(l, "br" + stg[3], WT - 1)] + 1
                    for j in range(stg[1], stg[2]):
                        for t in (2, 3):
                            conv_tap(t, j)
                        if lows[0] < end:
                            low_parts(lows[0] + 1)
                elif k == "att":
                    s = stg[1]
                    nk = s + 1
                    for p in range(4 + 1):
                        if p < 4:
                            key = ("sc", l, s, p)
                            side.filled(dve, key)
                            link(V.tensor_reduce(st[:, 64 + 2 * p:66 + 2 * p],
                                                 side.bank(key)[:, 0:2 * nk * P].rearrange("p (a k) -> p a k", a=2),
                                                 AX_X, ALU.max))
                            V.tensor_scalar(nmx[:, s, p::4, 0], st[:, 64 + 2 * p:66 + 2 * p], -HD ** -0.5, None,
                                            ALU.mult).then_inc(nmax_done, 1)
                        if p >= 1:
                            key = ("pT", l, s, p - 1)
                            side.filled(dve, key)
                            if p - 1 >= 2:
                                dve.wait_ge(pv_read, 3 * (2 * l + s) + p - 2)
                            V.tensor_copy(probT[:, (p - 1) % 2, 0:2 * nk * P],
                                          side.bank(key)[:, 0:2 * nk * P]).then_inc(side.freed(key), 1)
                        if s == 1:
                            for j in (2 * p, 2 * p + 1):
                                for t in (2, 3):
                                    conv_tap(t, j)
                    key = ("pv", l, s)
                    long_.filled(dve, key)
                    link(V.reciprocal(st[:, 80:88], nmx[:, s, :, 1]))
                    tt_(qkt[:, 0:W].rearrange("p (h d) -> p h d", d=HD),
                        long_.bank(key)[:, :].rearrange("p (h d) -> p h d", d=HD),
                        st[:, 80:88].unsqueeze(2).to_broadcast([P, HEADS, HD])).then_inc(long_.freed(key), 1)
                    long_.drained(dve, key)
                    proj.drained(dve, (l, "ag", s))
                    tt_(gates[:, 2, s, :], gates[:, 2, s, :], qkt[:, 0:W]).then_inc(prodC, 1)
                    dve.wait_ge(prodC, ls(l, s))
                elif k == "Y":
                    dve.wait_ge(scan_done, l + 1)
                    for q in range(4):
                        if q >= 2:
                            side.filled(dve, ("Y", l, q - 2))
                        V.tensor_copy(HY[64:128, q % 2].rearrange("p g r s k -> p (g r s) k"),
                                      H[64:128, 0:NCHUNK, 32 * q:32 * q + 32][:, ::-1, :].rearrange("p k x -> p x k")
                                      ).then_inc(hy_bwd, 1)
                elif k == "gelu":
                    s = stg[1]
                    dve.wait_ge(y_in, 16 * 8 * (l + 1))
                    dve.wait_ge(rows_in, 80 * (l + 1))
                    proj.drained(dve, (l, "ssm", s))
                    link(tt_(utok[:, s, :], utok[:, s, :], rows[:, 0, :]))
                    tt_(ytok[:, s, :], ytok[:, s, :], utok[:, s, :], ALU.add).then_inc(gelu_pre, 1)
                elif k == "cback":
                    s = stg[1]
                    key = ("cback", l, s)
                    side.filled(dve, key)
                    first = chunk_at[(l, "meC1", 0)]
                    link(V.bn_stats(st[:, 96:102], side.bank(key)[:, :]))
                    V.bn_aggr(st[:, 104:106], st[:, 96:102]).then_inc(ln_var, 1)
                    low_parts(first + (9 if s else 4))
                    dve.wait_ge(ln_rs, ls(l, s))
                    t = qkt[:, 0:W]
                    V.tensor_scalar(t, side.bank(key)[:, :], st[:, 104:105], st[:, 112:113], ALU.subtract,
                                    ALU.mult).then_inc(side.freed(key), 1)
                    low_parts(first + (10 if s else 5))
                    side.drained(dve, key)
                    link(tt_(t, t, rows[:, 1, :]))
                    tt_(t, t, rows[:, 2, :], ALU.add).then_inc(ln_pre, 1)
                    low_parts(first + (12 if s else 7))
                    dve.wait_ge(ln_pre, ls(l, s))
                    th_ready(dve, (l, "ln", s))
                    proj.drained(dve, (l, "gg", s))
                    tt_(gates[:, 1, s, :], gates[:, 1, s, :], th_view((l, "ln", s))).then_inc(prodA, 1)
                    dve.wait_ge(prodA, ls(l, s))
                elif k == "comb":
                    b, h = stg[1], stg[2]
                    if stg == LAST_COMB:
                        low_parts(ahead(l, "me" + b + str(h)))
                        merged_low(l, 0)
                    low_parts(ahead(l, "br" + b + str(h)))
                    for s in range(NS):
                        km, kb = (l, "me" + b + str(h), s), (l, "br" + b + str(h), s)
                        proj.filled(dve, kb)
                        th_ready(dve, km)
                        acc = mixed[:, s, W * h:W * h + W]
                        dst = acc if b == BRANCHES[0] else qkt[:, 0:W]
                        V.scalar_tensor_tensor(dst, th_view(km), 1.0, proj.bank(kb)[:, :], ALU.add,
                                               ALU.mult).then_inc(proj.freed(kb), 1)
                        if s == 0 and lows[0] < ahead(l, kb[1], CHUNK_ROOMS):
                            low_parts(lows[0] + 1)
                        proj.drained(dve, kb)
                        if b != BRANCHES[0]:
                            m = tt_(acc, acc, dst, ALU.add)
                            if b == BRANCHES[-1]:
                                m.then_inc(mixed_done, 1)
                                dve.wait_ge(mixed_done, 4 * l + 2 * h + s + 1)
                            else:
                                link(m)
                elif k == "chunks":
                    low_parts(chunk_at[(l, stg[1], 0)] + CHUNK_ROOMS)
                elif k == "early":
                    s = stg[1]
                    dve.wait_ge(split_hi, part_at[(l,) + stg] + 1)
                    tt_(hTe[1][:, s, :, :], hT[:, s, :, :], hTe[0][:, s, :, :].bitcast(F32),
                        ALU.subtract).then_inc(early_lo, 1)
                elif k == "split":
                    s = stg[1]
                    dve.wait_ge(split_hi, part_at[(l,) + stg] + 1)
                    tt_(hTs[1][:, s, :, :], hT[:, s, :, :], hTs[0][:, s, :, :].bitcast(F32),
                        ALU.subtract).then_inc(split_lo, 1)
                elif k == "brT":
                    b, s = stg[1], stg[2]
                    key = ("brT", l, b, s)
                    dve.wait_ge(split_hi, part_at[(l,) + stg] + 1)
                    flat = lambda i: brTs[b][i][:, s, :, :].rearrange("p t q -> p (t q)")
                    V.scalar_tensor_tensor(flat(1), side.bank(key)[:, :], 0.5 if b == "B" else 1.0,
                                           flat(0).bitcast(F32), ALU.mult, ALU.subtract).then_inc(side.freed(key), 1)
                elif k == "wout":
                    h = stg[1]
                    if h == 0:
                        low_parts(chunk_at[(l, "wo0", 0)] + WT + 1)
                        merged_low(l, 1)
                    low_parts(ahead(l, "wo" + str(h)))
                    for s in range(NS):
                        kg, kw = (l, "gate" + str(h), s), (l, "wo" + str(h), s)
                        proj.filled(dve, kw)
                        th_ready(dve, kg)
                        tt_(qkt[:, 0:W], proj.bank(kw)[:, :], th_view(kg)).then_inc(proj.freed(kw), 1)
                        proj.drained(dve, kw)
                        tt_(x[:, s, W * h:W * h + W], x[:, s, W * h:W * h + W], qkt[:, 0:W], ALU.add).then_inc(x_done, 1)
                        dve.wait_ge(x_done, 4 * l + 2 * h + s + 1)

        @block.gpsimd
        def _(pool):
            Q = nc.gpsimd
            n_chain = [0]

            def link(ins):
                n_chain[0] += 1
                ins.then_inc(pool_chain, 1)
                pool.wait_ge(pool_chain, n_chain[0])

            def tt_(out, a, b, op=ALU.mult):
                return Q.tensor_tensor(out, a, b, op)

            def rsqrt_mean(dst, src, n, count, tmp, done):
                link(Q.tensor_scalar(tmp, src, 1.0 / n, EPS, ALU.mult, ALU.add))
                tt_(dst, tmp, st[:, 128:128 + count], ALU.pow).then_inc(done, 1)

            Q.memset(Uz[:, :, :], 0.0).then_inc(zeroed, 1)
            Q.memset(cvpad[:, :, :, :], 0.0).then_inc(zeroed, 1)
            Q.memset(kz[0][:, :, :], 0.0).then_inc(zeroed, 1)
            Q.memset(kz[1][:, :, :], 0.0).then_inc(zeroed, 1)
            link(Q.memset(st[:, 128:140], -0.5))
            for l, stg in todo:
                k = stg[0]
                if k == "small":
                    ll = stg[1]
                    pool.wait_ge(small_in, 16 * N_SMALL * (ll + 1))
                    Q.tensor_copy(a32[0:G, 2, :].rearrange("g (d p) -> g d p", d=2),
                                  ldt[0:G, :].unsqueeze(2).to_broadcast([G, 2, SP])).then_inc(ldt_spread, 1)
                elif k == "preP":
                    ll, half = stg[1], stg[2]
                    if half == 0:
                        pool.wait_ge(tab_done, ll + 1)
                        pool.wait_ge(b_in, 64 * (ll + 1))
                        side.filled(pool, ("cT", ll, 1))
                        co = [ss[:, 10 + i, :].unsqueeze(2).to_broadcast([P, G, GC]) for i in range(2)]
                        t1, t2 = (tB[:, 512 * i:512 * i + 512].rearrange("p (g c) -> p g c", g=G) for i in range(2))
                        for r in range(2):
                            link(tt_(t1, co[0], braw[:, r, :, :]))
                            link(tt_(t2, co[1], braw[:, 1 - r, :, :]))
                            link(tt_(bbar[:, r, :, :], t1, t2, ALU.add if r else ALU.subtract))
                    else:
                        side.filled(pool, ("E", ll, 3))
                    g0 = 16 * half
                    lam = [t[:, L + 1:2 * L + 1, g0:g0 + 16].rearrange("p j g -> p g j").unsqueeze(3)
                           .to_broadcast([P, 16, L, GC]) for t in (lamr, lami)]
                    bb = [bbar[:, r, g0:g0 + 16, :].unsqueeze(2).to_broadcast([P, 16, L, GC]) for r in range(2)]
                    t1, t2 = (t[:, :].rearrange("p (g j c) -> p g j c", g=16, j=L) for t in (tA, tB))
                    for r in range(2):
                        link(tt_(t1, lam[0], bb[r]))
                        link(tt_(t2, lam[1], bb[1 - r]))
                        m = tt_(pre[:, r, :, :, :], t1, t2, ALU.add if r else ALU.subtract)
                        if r == 0:
                            link(m)
                        else:
                            m.then_inc(pre_done, 1)
                            pool.wait_ge(pre_done, 2 * ll + half + 1)
                elif k == "xn":
                    l, s = stg[1], stg[2]
                    pool.wait_ge(sq_done, ls(l, s))
                    rsqrt_mean(st[:, 4 + s:5 + s], st[:, s:s + 1], D, 1, st[:, 8 + s:9 + s], rstd_done)
                elif k == "qkn":
                    s = stg[1]
                    pool.wait_ge(qk_sq, ls(l, s))
                    rsqrt_mean(st[:, 48:58], st[:, 16:26], HD, HEADS + KV, st[:, 32:42], qk_rs)
                elif k == "cback":
                    s = stg[1]
                    pool.wait_ge(ln_var, ls(l, s))
                    rsqrt_mean(st[:, 112:113], st[:, 105:106], 1.0, 1, st[:, 114:115], ln_rs)
                elif k == "cp":
                    side.filled(pool, ("S", l, 7))
                    side.drained(pool, ("cT", l, 0))
                    side.drained(pool, ("cT", l, 1))
                    for i0, n in ((0, 2), (2, 2), (4, 1)):
                        t1, t2 = (t[:, 0:512 * n].rearrange("p (i g c) -> p i g c", i=n, g=G) for t in (tA, tB))
                        lam = [t[:, i0:i0 + n, :].unsqueeze(3).to_broadcast([P, n, G, GC]) for t in (lamr, lami)]
                        cc = [cT[:, r:r + 1, :, :].to_broadcast([P, n, G, GC]) for r in range(2)]
                        for r in range(2):
                            link(tt_(t1, cc[r], lam[0]))
                            link(tt_(t2, cc[1 - r], lam[1]))
                            m = tt_(CP[:, r, i0:i0 + n, :, :], t1, t2, ALU.subtract if r else ALU.add)
                            if i0 == 4 and r == 1:
                                m.then_inc(cp_done, 1)
                                pool.wait_ge(cp_done, l + 1)
                            else:
                                link(m)
                elif k == "bz":
                    half = stg[1]
                    g0 = 16 * half
                    if half:
                        side.filled(pool, ("K", l, 3))
                    else:
                        link(Q.memset(bz[:, :, :, :], 0.0))
                    link(Q.tensor_copy(bz[0:64, :, :, 0:GC], bbar[0:64, :, g0:g0 + 16, :]))
                    link(Q.tensor_copy(bz[64:128, :, :, GC:2 * GC], bbar[64:128, :, g0:g0 + 16, :]))
                    Q.tensor_copy(bz[:, :, :, 2 * GC:3 * GC], bbar[:, :, g0:g0 + 16, :]).then_inc(bz_done, 1)


OUTPUTS = (("y_prompt", (1, P, D)), ("y_sample", (1, P, D)), ("new_cache_k", (1, DEPTH, P, KV, HD)),
           ("new_cache_v", (1, DEPTH, P, KV, HD)), ("new_state_ssm_re", (1, DEPTH, 2, G, SP)),
           ("new_state_ssm_im", (1, DEPTH, 2, G, SP)))


def shape_constants():
    import numpy as np

    first = [[0, 1, 2, 3, 4], [3, 2, 1, 0], [L, 1]]
    second = [[0, 4, 3, 2, 1], [0, 1, 2, 3], [L, 1]]
    expo = np.zeros((P, NEXP), np.float32)
    expo[0:SP] = sum(first, [])
    expo[SP:P] = sum(second, [])
    grid_w, pairs = 64, HD // 4
    t = np.arange(P)
    inv = (10000.0 ** (-np.arange(pairs, dtype=np.float32) / pairs)).astype(np.float32)
    ang = np.stack([(t // grid_w)[:, None] * inv, (t % grid_w)[:, None] * inv], 1).astype(np.float32)
    rope = np.zeros((P, 2, 2, 2, pairs), np.float32)
    rope[:, 0, :, 0] = rope[:, 0, :, 1] = np.cos(ang)
    rope[:, 1, :, 0] = -np.sin(ang)
    rope[:, 1, :, 1] = np.sin(ang)
    return {"ident": np.eye(P, dtype=np.float32), "expo": expo, "rope": rope.reshape(P, 2, HD)}


def kernel(**inputs):
    import numpy as np
    import concourse.bacc as bacc
    from concourse.bass_utils import run_bass_kernel_spmd

    nc = bacc.Bacc("TRN2", target_bir_lowering=False, num_devices=1)
    arrays = {}

    def given(prefix, named):
        aps = {}
        for name, a in named.items():
            a = np.ascontiguousarray(a)
            arrays[prefix + name] = a
            aps[name] = nc.dram_tensor(prefix + name, a.shape, mybir.dt.from_np(a.dtype), kind="ExternalInput").ap()
        return aps

    A = given("in_", inputs)
    C = given("const_", shape_constants())
    O = {name: nc.dram_tensor("out_" + name, shape, F32, kind="ExternalOutput").ap() for name, shape in OUTPUTS}
    build(nc, A, C, O)
    r = run_bass_kernel_spmd(nc, [arrays], core_ids=[0])
    return tuple(r.results[0]["out_" + name] for name, _ in OUTPUTS)
```
